# Optimizing a Trainium2 kernel written in Bass

```python
import math
import jax, jax.numpy as jnp
from jax import lax
import numpy as np

D_MODEL = 1024
BATCH = 1
SEQ = 256
DEPTH = 2
DEC_BATCH = 1
DEC_SEQ = 256
PAST_LEN = 128

HEAD_DIM = 64
N_Q_HEADS = 8
N_KV_HEADS = 2
Q_PER_KV = N_Q_HEADS // N_KV_HEADS
ATTN_WIDTH = N_Q_HEADS * HEAD_DIM
KV_WIDTH = N_KV_HEADS * HEAD_DIM
WINDOW = 128
ATTN_BLOCK = 128
KEY_SPAN = ATTN_BLOCK + 2 * WINDOW
ROPE_THETA = 10000.0
SSD_HEADS = 16
SSD_HEAD_DIM = 64
SSD_WIDTH = SSD_HEADS * SSD_HEAD_DIM
SSD_GROUPS = 2
SSD_HEADS_PER_GROUP = SSD_HEADS // SSD_GROUPS
SSD_STATE = 128
SSD_CONV = 5
SSD_CHUNK = 128
XBC_WIDTH = SSD_WIDTH + 2 * SSD_GROUPS * SSD_STATE
MIX_WIDTH = ATTN_WIDTH + SSD_WIDTH
IN_PROJ_WIDTH = ATTN_WIDTH + 2 * KV_WIDTH + SSD_WIDTH + XBC_WIDTH + 2 * SSD_HEADS
D_FF = 2816
FFN_CONV = 3
DEEPNORM_ALPHA = (2 * DEPTH) ** 0.25
DEEPNORM_BETA = (8 * DEPTH) ** -0.25
EPS = 1e-5
MASK_VALUE = -1e30

kernel_name = "hymba_style_bidir_ssd_swa_encoder"

def layer_norm(x, g, b):
    xf = x.astype(jnp.float32)
    mu = jnp.mean(xf, axis=-1, keepdims=True)
    var = jnp.mean(jnp.square(xf - mu), axis=-1, keepdims=True)
    return ((xf - mu) * lax.rsqrt(var + EPS) * g.astype(jnp.float32) + b.astype(jnp.float32)).astype(x.dtype)

def rms_norm(x, g):
    xf = x.astype(jnp.float32)
    ms = jnp.mean(jnp.square(xf), axis=-1, keepdims=True)
    return (xf * lax.rsqrt(ms + EPS) * g.astype(jnp.float32)).astype(x.dtype)

def depthwise_conv(x, w, b):
    pad = (w.shape[0] - 1) // 2
    y = lax.conv_general_dilated(
        x, w[:, None, :].astype(x.dtype), window_strides=(1,), padding=[(pad, pad)],
        dimension_numbers=("NWC", "WIO", "NWC"), feature_group_count=x.shape[-1])
    return y + b.astype(x.dtype)

def rope(x):
    s, d = x.shape[1], x.shape[-1]
    inv_freq = ROPE_THETA ** (-jnp.arange(0, d, 2, dtype=jnp.float32) / d)
    ang = jnp.arange(s, dtype=jnp.float32)[:, None] * inv_freq[None, :]
    cos = jnp.cos(ang)[None, :, None, :]
    sin = jnp.sin(ang)[None, :, None, :]
    xf = x.astype(jnp.float32)
    x1, x2 = xf[..., : d // 2], xf[..., d // 2:]
    return jnp.concatenate([x1 * cos - x2 * sin, x2 * cos + x1 * sin], axis=-1).astype(x.dtype)

def window_attention(q, k, v, sink):
    bsz, s = q.shape[0], q.shape[1]
    nb = s // ATTN_BLOCK
    scale = HEAD_DIM ** -0.5
    kp = jnp.pad(k, ((0, 0), (WINDOW, WINDOW), (0, 0), (0, 0)))
    vp = jnp.pad(v, ((0, 0), (WINDOW, WINDOW), (0, 0), (0, 0)))
    qb = q.reshape(bsz, nb, ATTN_BLOCK, N_KV_HEADS, Q_PER_KV, HEAD_DIM).transpose(1, 0, 2, 3, 4, 5)
    sink_b = sink.astype(jnp.float32).reshape(N_KV_HEADS, Q_PER_KV)[None, :, :, None, None]

    def one_block(args):
        i, q_blk = args
        start = i * ATTN_BLOCK
        k_blk = lax.dynamic_slice_in_dim(kp, start, KEY_SPAN, axis=1)
        v_blk = lax.dynamic_slice_in_dim(vp, start, KEY_SPAN, axis=1)
        sc = jnp.einsum("bqhgd,bkhd->bhgqk", q_blk, k_blk).astype(jnp.float32) * scale
        q_pos = start + jnp.arange(ATTN_BLOCK)
        k_pos = start - WINDOW + jnp.arange(KEY_SPAN)
        mask = (jnp.abs(q_pos[:, None] - k_pos[None, :]) <= WINDOW) & (k_pos[None, :] >= 0) & (k_pos[None, :] < s)
        sc = jnp.where(mask, sc, MASK_VALUE)
        m = jnp.maximum(jnp.max(sc, axis=-1, keepdims=True), sink_b)
        p = jnp.exp(sc - m)
        denom = jnp.sum(p, axis=-1, keepdims=True) + jnp.exp(sink_b - m)
        probs = (p / denom).astype(v_blk.dtype)
        return jnp.einsum("bhgqk,bkhd->bqhgd", probs, v_blk)

    out = lax.map(one_block, (jnp.arange(nb), qb))
    return out.transpose(1, 0, 2, 3, 4, 5).reshape(bsz, s, ATTN_WIDTH)

def ssd_chunked(x, dt, a, bm, cm):
    bsz, s = x.shape[0], x.shape[1]
    nc = s // SSD_CHUNK
    G, E, P, N, Q = SSD_GROUPS, SSD_HEADS_PER_GROUP, SSD_HEAD_DIM, SSD_STATE, SSD_CHUNK
    xd = (x * dt[..., None]).reshape(bsz, nc, Q, G, E, P)
    la = (dt * a).reshape(bsz, nc, Q, G, E).transpose(0, 1, 3, 4, 2)
    a_cs = jnp.cumsum(la, axis=-1)
    bc = bm.reshape(bsz, nc, Q, G, N)
    cc = cm.reshape(bsz, nc, Q, G, N)
    idx = jnp.arange(Q)
    lower = idx[:, None] >= idx[None, :]
    seg = a_cs[..., :, None] - a_cs[..., None, :]
    decay = jnp.where(lower, jnp.exp(jnp.where(lower, seg, 0.0)), 0.0)
    cb = jnp.einsum("bcqgn,bcsgn->bcgqs", cc, bc)
    y_diag = jnp.einsum("bcgeqs,bcsgep->bcqgep", cb[:, :, :, None] * decay, xd)
    decay_to_end = jnp.exp(a_cs[..., -1:] - a_cs)
    states = jnp.einsum("bcsgn,bcges,bcsgep->bcgepn", bc, decay_to_end, xd)
    chunk_decay = jnp.exp(a_cs[..., -1])

    def step(h, inp):
        st, dec = inp
        return dec[..., None, None] * h + st, h

    _, prev = lax.scan(step, jnp.zeros_like(states[:, 0]),
                       (jnp.moveaxis(states, 1, 0), jnp.moveaxis(chunk_decay, 1, 0)))
    y_off = jnp.einsum("bcqgn,cbgepn,bcgeq->bcqgep", cc, prev, jnp.exp(a_cs))
    return (y_diag + y_off).reshape(bsz, s, SSD_HEADS, P)

def bidir_ssd(xs, dt_raw, dt_bias, a_log, bm, cm):
    dt = jax.nn.softplus(dt_raw.astype(jnp.float32) + dt_bias.astype(jnp.float32))
    a = -jnp.exp(a_log.astype(jnp.float32))
    flip = lambda t: jnp.flip(t, axis=1)
    y_f = ssd_chunked(xs, dt[:, :, 0], a[0], bm, cm)
    y_b = flip(ssd_chunked(flip(xs), flip(dt[:, :, 1]), a[1], flip(bm), flip(cm)))
    return y_f + y_b

def hybrid_layer(h, w_in, attn_sink, ssd_conv_w, ssd_conv_b, ssd_a_log, ssd_dt_bias, ssd_d,
                 ssd_norm_g, w_out, ln1_g, ln1_b, w_up, ffn_conv_w, ffn_conv_b, w_down, ln2_g, ln2_b):
    bsz, s = h.shape[0], h.shape[1]
    proj = h @ w_in
    splits = np.cumsum([ATTN_WIDTH, KV_WIDTH, KV_WIDTH, SSD_WIDTH, XBC_WIDTH])
    q, k, v, z, xbc, dt_raw = jnp.split(proj, splits, axis=-1)
    q = rope(q.reshape(bsz, s, N_Q_HEADS, HEAD_DIM))
    k = rope(k.reshape(bsz, s, N_KV_HEADS, HEAD_DIM))
    v = v.reshape(bsz, s, N_KV_HEADS, HEAD_DIM)
    attn_out = window_attention(q, k, v, attn_sink)
    xbc = jax.nn.silu(depthwise_conv(xbc, ssd_conv_w, ssd_conv_b))
    xs, bm, cm = jnp.split(xbc, [SSD_WIDTH, SSD_WIDTH + SSD_GROUPS * SSD_STATE], axis=-1)
    xs = xs.reshape(bsz, s, SSD_HEADS, SSD_HEAD_DIM)
    bm = bm.reshape(bsz, s, SSD_GROUPS, SSD_STATE)
    cm = cm.reshape(bsz, s, SSD_GROUPS, SSD_STATE)
    y = bidir_ssd(xs, dt_raw.reshape(bsz, s, 2, SSD_HEADS), ssd_dt_bias, ssd_a_log, bm, cm)
    y = (y + ssd_d[:, None] * xs).reshape(bsz, s, SSD_WIDTH).astype(h.dtype)
    ssd_out = rms_norm(y * jax.nn.silu(z), ssd_norm_g)
    mix = jnp.concatenate([attn_out, ssd_out], axis=-1) @ w_out
    h = layer_norm(DEEPNORM_ALPHA * h + mix, ln1_g, ln1_b)
    gate, val = jnp.split(h @ w_up, 2, axis=-1)
    gate = depthwise_conv(gate, ffn_conv_w, ffn_conv_b)
    ffn = (jax.nn.silu(gate) * val) @ w_down
    return layer_norm(DEEPNORM_ALPHA * h + ffn, ln2_g, ln2_b)

def setup_inputs(seed: int = 0) -> dict:
    key = jax.random.key(seed)
    ks = jax.random.split(key, 24)
    f32 = jnp.float32
    nrm = lambda k, shape: jax.random.normal(k, shape, dtype=f32)
    dt0 = jnp.exp(jax.random.uniform(ks[9], (DEPTH, 2, SSD_HEADS), dtype=f32,
                                     minval=math.log(1e-3), maxval=math.log(1e-1)))
    return {
        "x_prompt": nrm(ks[0], (BATCH, SEQ, D_MODEL)),
        "x_sample": nrm(ks[1], (DEC_BATCH, DEC_SEQ, D_MODEL)),
        "ln_in_g": 1.0 + 0.02 * nrm(ks[2], (D_MODEL,)),
        "ln_in_b": 0.02 * nrm(ks[3], (D_MODEL,)),
        "w_in": nrm(ks[4], (DEPTH, D_MODEL, IN_PROJ_WIDTH)) * D_MODEL ** -0.5,
        "attn_sink": 0.5 * nrm(ks[5], (DEPTH, N_Q_HEADS)),
        "ssd_conv_w": nrm(ks[6], (DEPTH, SSD_CONV, XBC_WIDTH)) * SSD_CONV ** -0.5,
        "ssd_conv_b": 0.02 * nrm(ks[7], (DEPTH, XBC_WIDTH)),
        "ssd_a_log": jnp.log(jax.random.uniform(ks[8], (DEPTH, 2, SSD_HEADS), dtype=f32, minval=1.0, maxval=16.0)),
        "ssd_dt_bias": dt0 + jnp.log(-jnp.expm1(-dt0)),
        "ssd_d": 1.0 + 0.02 * nrm(ks[10], (DEPTH, SSD_HEADS)),
        "ssd_norm_g": 1.0 + 0.02 * nrm(ks[11], (DEPTH, SSD_WIDTH)),
        "w_out": nrm(ks[12], (DEPTH, MIX_WIDTH, D_MODEL)) * (MIX_WIDTH ** -0.5 * DEEPNORM_BETA),
        "ln1_g": 1.0 + 0.02 * nrm(ks[13], (DEPTH, D_MODEL)),
        "ln1_b": 0.02 * nrm(ks[14], (DEPTH, D_MODEL)),
        "w_up": nrm(ks[15], (DEPTH, D_MODEL, 2 * D_FF)) * D_MODEL ** -0.5,
        "ffn_conv_w": nrm(ks[16], (DEPTH, FFN_CONV, D_FF)) * FFN_CONV ** -0.5,
        "ffn_conv_b": 0.02 * nrm(ks[17], (DEPTH, D_FF)),
        "w_down": nrm(ks[18], (DEPTH, D_FF, D_MODEL)) * (D_FF ** -0.5 * DEEPNORM_BETA),
        "ln2_g": 1.0 + 0.02 * nrm(ks[19], (DEPTH, D_MODEL)),
        "ln2_b": 0.02 * nrm(ks[20], (DEPTH, D_MODEL)),
    }

def reference(x_prompt, x_sample, ln_in_g, ln_in_b, w_in, attn_sink, ssd_conv_w, ssd_conv_b,
              ssd_a_log, ssd_dt_bias, ssd_d, ssd_norm_g, w_out, ln1_g, ln1_b, w_up, ffn_conv_w,
              ffn_conv_b, w_down, ln2_g, ln2_b):
    def trunk(x):
        h = layer_norm(x, ln_in_g, ln_in_b)
        for i in range(DEPTH):
            h = hybrid_layer(h, w_in[i], attn_sink[i], ssd_conv_w[i], ssd_conv_b[i], ssd_a_log[i],
                             ssd_dt_bias[i], ssd_d[i], ssd_norm_g[i], w_out[i], ln1_g[i], ln1_b[i],
                             w_up[i], ffn_conv_w[i], ffn_conv_b[i], w_down[i], ln2_g[i], ln2_b[i])
        return h

    y_prompt = trunk(x_prompt)
    y_sample = trunk(x_sample)
    return (y_prompt, y_sample)


_drawn_inputs = setup_inputs


def setup_inputs(seed=0):
    import zlib

    import numpy as np

    out = dict(_drawn_inputs(seed))
    spreads = {}
    factors = {'attn_sink': 8.0,
     'ssd_conv_b': 4.431,
     'ssd_d': 8.0,
     'ssd_norm_g': 6.741,
     'ffn_conv_b': 8.0}
    for name, (base, spread) in spreads.items():
        noise = np.random.default_rng([zlib.crc32(name.encode()), seed]).standard_normal(out[name].shape)
        drawn = base * np.exp(spread * noise) if base else spread * noise
        out[name] = __import__('jax').numpy.asarray(drawn.astype(out[name].dtype))
    for name, factor in factors.items():
        out[name] = (out[name] * factor).astype(out[name].dtype)
    return out
```

```python
from contextlib import ExitStack

import numpy as np

import concourse.bass as bass
from concourse import mybir

F32 = mybir.dt.float32
F32R = mybir.dt.float32r
ALU = mybir.AluOpType
ACT = mybir.ActivationFunctionType
AX_X = mybir.AxisListType.X

P = 128
DEPTH, D_MODEL, SEQ, NSEQ = 2, 1024, 256, 2
TOK = NSEQ * SEQ
BLK = 128
NBLK = TOK // BLK
HEAD = 64
QPK = 4
SSD_HEADS, SSD_WIDTH, STATE = 16, 1024, 128
HPG = 8
D_FF = 2816
CT = D_MODEL // P
FT = D_FF // P
ALPHA = (2 * DEPTH) ** 0.25
EPS = 1e-5
MASK = -1e30
SCALE = HEAD ** -0.5

U_DT = 0
U_CONV = 1
N_CONV = 12
U_K, U_V, U_Q = 13, 14, 15
U_Z = 19
U_OUT = 27
N_OUT = 12
U_UP = U_OUT + N_OUT
U_DOWN = U_UP + 2 * FT
UNITS = U_DOWN + FT
RING = 3
assert UNITS % RING == 0 and U_UP % RING == 0
TURNS = UNITS // RING

PM = {}
PF = {}


def _columns(table, widths):
    at = 0
    for name, w in widths:
        table[name] = (at, at + w)
        at += w
    return at


PM_W = _columns(PM, [("conv_w", N_CONV * 5), ("conv_b", N_CONV), ("norm_g", CT), ("sink", 8),
                     ("a_log", 32), ("dt_bias", 32), ("d", SSD_HEADS)])
PF_W = _columns(PF, [("conv_w", FT * 3), ("conv_b", FT), ("ln1_g", CT), ("ln1_b", CT),
                     ("ln2_g", CT), ("ln2_b", CT)])
CN = {}
CN_W = _columns(CN, [("ident", P), ("avg", P), ("upper", P), ("lower", P), ("after", P),
                     ("before", P), ("rot", P), ("cos", SEQ), ("sin", SEQ), ("eps", 1),
                     ("ln_g", CT), ("ln_b", CT)])

SEGS = [(t, g, d) for t in range(NBLK) for g in range(2) for d in range(2)]
ATTN = [(t, g) for t in range(NBLK) for g in range(2)]
SEG_SLOTS = {15: [0], 16: [1], 17: [2, 3], 18: [4], 19: [5, 6], 20: [7], 21: [8, 9], 22: [10],
             23: [11, 12], 24: [13], 25: [14, 15], 26: [16]}


def seg_steps(k):
    out = []
    if k >= 1:
        t, g, d = SEGS[k - 1]
        if g == 0 and d == 0:
            if t % 2 == 0:
                out += [("XW", t), ("XW", t + 1), ("ST", (t, 0)), ("ST", (t, 1)),
                        ("ST", (t + 1, 0)), ("ST", (t + 1, 1))]
            out += [("XD", t)]
        if d == 0:
            out += [("YO", (t, g))]
        out += [("SD", k - 1)]
        if d == 1:
            out += [("YA", (t, g))]
    if k < len(SEGS):
        out += [("SB", k), ("SC", k)]
    if k + 1 < len(SEGS):
        out += [("SA", k + 1)]
    return out


def mixer_schedule():
    steps = [("G", 0)]
    for n in range(U_OUT + 3):
        if n + 1 < U_OUT:
            steps.append(("G", n + 1))
        if n < U_OUT:
            steps.append(("E", n))
        if U_CONV <= n - 1 < U_CONV + N_CONV:
            steps.append(("SILU", n - 1 - U_CONV))
        if n == 0:
            steps += [("DTT", 0), ("SP", 0)]
        if n == 2:
            steps.append(("SM", 0))
        if n == 6:
            steps += [("CB", 0), ("CB", 1)]
        j = n - 2 - U_CONV
        if j in (0, 1) or 4 <= j < N_CONV:
            steps.append(("T", j))
        if n - 1 == U_V:
            steps.append(("VT", 0))
        if n - 1 == U_K:
            steps.append(("ROT", 4))
        if U_Q <= n - 1 < U_Q + 4:
            steps.append(("ROT", n - 1 - U_Q))
        if 20 <= n - 2 < 28:
            steps.append(("AV", n - 22))
        if n == 14:
            steps.append(("SA", 0))
        for k in SEG_SLOTS.get(n, []):
            steps += seg_steps(k)
        if 20 <= n - 1 < 28:
            steps.append(("AP", n - 21))
        if n == 23:
            steps += [("YT", (t, 0)) for t in range(NBLK - 1)]
        if n == 26:
            steps += [("YT", (3, 0))]
        if n == 27:
            steps += [("YT", (t, 1)) for t in range(NBLK)]
        if 20 <= n < 28:
            steps.append(("AS", n - 20))
        if n < U_OUT:
            steps.append(("S", n + RING))
    steps += [("RS", c) for c in range(CT)]
    steps += [("RMS", 0)]
    for u in range(U_OUT, U_UP):
        steps.append(("G", u))
        if u - U_OUT >= 1:
            steps.append(("RN", u - U_OUT - 1)) if u - U_OUT - 1 < CT else None
        steps.append(("S", u + RING))
    return steps


SCHED = mixer_schedule()
LINKS = 14 + 1 + 5 + 8 + 5 * 8 + 1


def trunk(nc, x_t, units, pm_d, pf_d, cn_d, y_t):
    ctx = ExitStack()
    with ctx:
        def sb(name, shape, dt=F32):
            return ctx.enter_context(nc.sbuf_tensor(name, shape, dt))

        def sem(name):
            return ctx.enter_context(nc.semaphore(name))

        cn = sb("cn", [P, CN_W])
        pm = sb("pm", [P, PM_W])
        pf = sb("pf", [P, PF_W])
        raw = sb("raw", [P, RING, 1024])
        whi = sb("whi", [P, RING, 1024], F32R)
        wlo = sb("wlo", [P, RING, 1024], F32R)
        hhi = sb("hhi", [P, CT, TOK], F32R)
        hlo = sb("hlo", [P, CT, TOK], F32R)
        dt = sb("dt", [P, NBLK, 32])
        la = sb("la", [P, NBLK, 32])
        dec = sb("dec", [P, NBLK, 2, SSD_HEADS])
        dd = sb("dd", [P, NBLK, 2, SSD_HEADS])
        neg_a = sb("neg_a", [P, 32])
        ast = sb("ast", [P, 6, QPK])
        KB = 1024
        arena_h = sb("arena_h", [P, CT * TOK])
        arena = sb("arena", [P, 102 * KB // 4])
        base_h = nc.sbuf_base - 102 * KB - CT * TOK * 4
        base = nc.sbuf_base - 102 * KB

        def at(name, kb, shape, dtype=F32, start=None):
            return nc.alloc_sbuf_tensor_at(name, shape, dtype, offset=(base if start is None else start) + int(kb * KB))

        h = at("h", 0, [P, CT, TOK], start=base_h)
        zs = at("zs", 0, [P, CT, TOK], start=base_h)
        bc = at("bc", 0, [P, 4, TOK])
        ropet = at("ropet", 0, [P, TOK])
        yo = at("yo", 2, [P, 512])
        b_tm = at("b_tm", 4 + 4, [P, NBLK, 2 * STATE])
        st = at("st", 12, [P, 2, 2, 512])
        qk = at("qk", 20, [P, 5, TOK])
        v_tm = at("v_tm", 30, [P, NBLK, P])
        zt = at("zt", 32, [P, TOK])
        sc = at("sc", 34, [P, QPK, SEQ])
        xsc = at("xsc", 34, [P, 2, TOK])
        p_t = at("p_t", 38, [P, 2, 512])
        cv = at("cv", 38, [P, 2, TOK])
        ahi = at("ahi", 42, [P, N_OUT, TOK], F32R)
        alo = at("alo", 66, [P, N_OUT, TOK], F32R)
        xs_tm = at("xs_tm", 50, [P, NBLK, SSD_WIDTH])
        cb = at("cb", 74, [P, 2, 8, P])
        xd = at("xd", 82, [P, 2, SSD_WIDTH])
        seg_r = at("seg_r", 90, [P, HPG, P])
        sp = at("sp", 90, [P, 8, 128])
        seg_e = at("seg_e", 94, [P, 2, HPG, P])
        sq = at("sq", 94, [P, 2, TOK])
        std = at("std", 98, [P, TOK])
        uhi = at("uhi", 0, [P, FT, TOK], F32R)
        ulo = at("ulo", 44, [P, FT, TOK], F32R)
        gcv = at("gcv", 88, [P, TOK])
        gsg = at("gsg", 90, [P, TOK])
        guf = at("guf", 92, [P, TOK])

        ps = ctx.enter_context(nc.psum_tensor("ps", [P, 8, 512], F32))

        def f(view):
            return view.bitcast(F32)

        def cst(name, lo=0, hi=None):
            a, b = CN[name]
            return cn[:, a + lo:(b if hi is None else a + hi)]

        def pmc(name, lo=0, hi=None):
            a, b = PM[name]
            return pm[:, a + lo:(b if hi is None else a + hi)]

        ident = cst("ident")

        cn_loaded, x_loaded = sem("cn_loaded"), sem("x_loaded")
        pm_loaded, pf_loaded = sem("pm_loaded"), sem("pf_loaded")
        raw_loaded = [sem(f"raw_loaded{k}") for k in range(RING)]
        unit_hi, unit_split, unit_used = sem("unit_hi"), sem("unit_split"), sem("unit_used")
        y_stored = sem("y_stored")
        link = sem("dve_link")
        dt_copied, dt_abs, dt_exp = sem("dt_copied"), sem("dt_abs"), sem("dt_exp")
        dtx_done, la_done, dec_done = sem("dtx_done"), sem("la_done"), sem("dec_done")
        conv_center, conv_taps, silu_done = sem("conv_center"), sem("conv_taps"), sem("silu_done")
        aux_full, t_evac, cb_done = sem("aux_full"), sem("t_evac"), sem("cb_done")
        proj_copied, rope_sin, rope_done = sem("proj_copied"), sem("rope_sin"), sem("rope_done")
        v_done, tanh_done, zs_done = sem("v_done"), sem("tanh_done"), sem("zs_done")
        xw_done, y_full, st_done, xd_done = sem("xw_done"), sem("y_full"), sem("st_done"), sem("xd_done")
        yd_done, r_done, seg_full = sem("yd_done"), sem("r_done"), sem("seg_full")
        exp_done, w_done, seg_used = sem("exp_done"), sem("w_done"), sem("seg_used")
        yo_done, ya_done, gated = sem("yo_done"), sem("ya_done"), sem("gated")
        as_mask, as_copy, as_max = sem("as_mask"), sem("as_copy"), sem("as_max")
        as_exp, as_norm = sem("as_exp"), sem("as_norm")
        pt0_done, pt1_done, ah_done, al_done = sem("pt0_done"), sem("pt1_done"), sem("ah_done"), sem("al_done")
        rms_sq, rms_mm, rms_std = sem("rms_sq"), sem("rms_mm"), sem("rms_std")
        ssd_normed, sh_done, sl_done = sem("ssd_normed"), sem("sh_done"), sem("sl_done")
        h_rebuilt, acc_done, res_done = sem("h_rebuilt"), sem("acc_done"), sem("res_done")
        ln_mean, ln_cent, ln_sq, ln_sqmm = sem("ln_mean"), sem("ln_cent"), sem("ln_sq"), sem("ln_sqmm")
        ln_rstd = sem("ln_rstd")
        ln_std, ln_scaled, ln_hi, ln_h, h_ready = sem("ln_std"), sem("ln_scaled"), sem("ln_hi"), sem("ln_h"), sem("h_ready")
        glu_center, glu_taps, glu_silu = sem("glu_center"), sem("glu_taps"), sem("glu_silu")
        glu_done, glu_hi, glu_ready = sem("glu_done"), sem("glu_hi"), sem("glu_ready")

        aux_use, y_use = {}, {}
        aux_free, y_free = [], []
        aux_counted, y_counted = {}, {}

        def take(use, free, counted, key, releases, counts=True):
            use[key] = len(free)
            free.append(releases)
            if counts:
                counted[key] = len(counted) + 1

        n_t = 0
        for what, i in SCHED:
            aux = lambda key, rel, c=True: take(aux_use, aux_free, aux_counted, key, rel, c)
            yy = lambda key, rel, c=True: take(y_use, y_free, y_counted, key, rel, c)
            if what == "DTT":
                aux(("DTT", 0), [(dtx_done, 1, 1)])
            elif what == "SM":
                aux(("SM", 0), [(dec_done, 1, 1)])
            elif what == "CB":
                aux(("CB", i), [(cb_done, 4, 2 * i + 2)])
            elif what == "T":
                n_t += 1
                aux(("T", i), [(t_evac, 10, n_t)])
            elif what == "VT":
                aux(("VT", 0), [(v_done, 1, 1)])
            elif what == "ROT":
                aux(("ROT", i), [(rope_sin, 5, (i + 1) % 5 + 1)])
            elif what == "AS":
                for m in range(2):
                    aux(("AS", i, m), [(as_mask, 16, 2 * i + m + 1), (as_copy, 16, 2 * i + m + 1)])
            elif what == "AP":
                aux(("AP", i, 0), [(pt0_done, 8, i + 1)])
                aux(("AP", i, 1), [(pt1_done, 8, i + 1)])
            elif what == "AV":
                aux(("AV", i), [(al_done, 8, i + 1)])
            elif what == "RS" and i == 0:
                aux(("RS", 0), [(rms_std, 1, 1)], False)
            elif what == "ST":
                yy(("ST", i), [(st_done, 8, 2 * i[0] + i[1] + 1)])
            elif what == "YO":
                yy(("YO", i), [(yo_done, 8, 2 * i[0] + i[1] + 1)])
            elif what == "SD" and SEGS[i][2] == 0:
                yy(("SD", SEGS[i][:2]), [(ya_done, 8, 2 * SEGS[i][0] + SEGS[i][1] + 1)], False)
            elif what == "YT":
                yy(("YT", i), [(gated, 8, len([1 for k in y_use if k[0] == "YT"]) + 1)])
        AUX_N, Y_N = len(aux_counted), len(y_counted)
        t_index = {i: n + 1 for n, i in enumerate(i for what, i in SCHED if what == "T")}
        gated_index = {i: n + 1 for n, i in enumerate(i for what, i in SCHED if what == "YT")}

        def aux_bank(key):
            return 6 + aux_use[key] % 2

        def y_bank(key):
            return 4 + y_use[key] % 2

        def wait_aux_free(eng, L, key):
            n = aux_use[key] - 2
            if n >= 0:
                for s, per, count in aux_free[n]:
                    eng.wait_ge(s, L * per + count)

        def wait_y_free(eng, L, key):
            n = y_use[key] - 2
            if n >= 0:
                for s, per, count in y_free[n]:
                    eng.wait_ge(s, L * per + count)

        def wait_aux_full(eng, L, key):
            eng.wait_ge(aux_full, L * AUX_N + aux_counted[key])

        def wait_y_full(eng, L, key):
            eng.wait_ge(y_full, L * Y_N + y_counted[key])

        ACC_ORDER = [4, 5, 6, 7, 0, 1, 2, 3]

        block = ctx.enter_context(nc.Block())

        @block.sync
        def _(sp_eng):
            sp_eng.dma_start(h[:], x_t).then_inc(x_loaded, 16)
            for j in range(RING):
                sp_eng.dma_start(raw[:, j, :], units[j]).then_inc(raw_loaded[j], 16)
            with sp_eng.Fori(1, DEPTH * TURNS) as g:
                for j in range(RING):
                    sp_eng.wait_ge(unit_split, g * RING + (j - RING + 1))
                    sp_eng.dma_start(raw[:, j, :], units[g * RING + j]).then_inc(raw_loaded[j], 16)
            for j in range(RING):
                sp_eng.wait_ge(unit_split, (DEPTH * TURNS - 1) * RING + j + 1)
                sp_eng.dma_start(raw[:, j, :], units[j]).then_inc(raw_loaded[j], 16)
            for c in range(CT):
                sp_eng.wait_ge(h_ready, 2 * DEPTH * CT + c + 1)
                sp_eng.dma_start(y_t[:, c, :], h[:, c, :]).then_inc(y_stored, 16)
            sp_eng.wait_ge(y_stored, CT * 16)

        @block.gpsimd
        def _(pool):
            pool.dma_start(cn[:], cn_d).then_inc(cn_loaded, 16)
            with pool.Fori(0, DEPTH) as L:
                pool.wait_ge(h_ready, (L * 2 + 1) * CT)
                pool.dma_start(pm[:], pm_d[L]).then_inc(pm_loaded, 16)
                pool.dma_start(pf[:], pf_d[L]).then_inc(pf_loaded, 16)
                pool.wait_ge(pm_loaded, L * 16 + 16)
                for t in range(NBLK):
                    pool.wait_ge(xd_done, L * 8 + 2 * t + 2)
                    v = xs_tm[:, t, :].rearrange("p (h c) -> p h c", c=HEAD)
                    d_b = pmc("d").unsqueeze(2).broadcast_to((P, SSD_HEADS, HEAD))
                    nc.gpsimd.tensor_tensor(v, v, d_b, ALU.mult).then_inc(yd_done, 1)
                for c in range(CT):
                    pool.wait_ge(sl_done, L * CT + c + 1)
                    nc.gpsimd.tensor_tensor(h[:, c, :], f(hhi[:, c, :]), f(hlo[:, c, :]), ALU.add).then_inc(h_rebuilt, 1)

        @block.scalar
        def _(act):
            A = nc.scalar.activation

            def split_hi(turn, slot, first=False):
                act.wait_ge(raw_loaded[slot], turn * 16 + 16)
                A(whi[:, slot, :], raw[:, slot, :], ACT.Copy).then_inc(unit_hi, 1)

            def split_next(L, n, more=0):
                act.wait_ge(unit_used, L * UNITS + n + 1 + more * RING)
                split_hi(L * TURNS + (n // RING + 1) + more, n % RING)

            def layer_norm(idx, L, gam, bet):
                for c in range(CT):
                    act.wait_ge(ln_cent, idx * CT + c + 1)
                    if c >= 2:
                        act.wait_ge(ln_sqmm, idx * CT + c - 1)
                    A(sq[:, c % 2, :], h[:, c, :], ACT.Square).then_inc(ln_sq, 1)
                act.wait_ge(ln_sqmm, idx * CT + CT)
                A(std[:], ps[:, 5, :], ACT.Sqrt, bias=cst("eps")).then_inc(ln_std, 1)
                for c in range(CT):
                    act.wait_ge(ln_scaled, idx * CT + c + 1)
                    A(hhi[:, c, :], h[:, c, :], ACT.Identity, bias=bet[:, c:c + 1]).then_inc(ln_hi, 1)
                    act.wait_ge(ln_hi, idx * CT + c + 1)
                    A(h[:, c, :], h[:, c, :], ACT.Identity, bias=bet[:, c:c + 1]).then_inc(ln_h, 1)

            act.wait_ge(cn_loaded, 16)
            for j in range(RING):
                split_hi(0, j)
            layer_norm(0, None, cst("ln_g"), cst("ln_b"))

            with act.Fori(0, DEPTH) as L:
                act.wait_ge(pm_loaded, L * 16 + 16)
                for what, i in SCHED:
                    if what == "S":
                        split_next(L, i - RING)
                    elif what == "E" and i == U_DT:
                        act.wait_ge(unit_used, L * UNITS + i + 1)
                        A(zt[0:32, :], ps[0:32, i % 2, :], ACT.Copy).then_inc(dt_copied, 1)
                    elif what == "E" and i < U_K:
                        j = i - U_CONV
                        act.wait_ge(unit_used, L * UNITS + i + 1)
                        if j >= 2:
                            act.wait_ge(silu_done, L * N_CONV + j - 1)
                        A(cv[:, j % 2, :], ps[:, i % 2, :], ACT.Identity, scale=pmc("conv_w", 5 * j + 2, 5 * j + 3),
                          bias=pmc("conv_b", j, j + 1)).then_inc(conv_center, 1)
                    elif what == "E" and i < U_Z:
                        m = i - U_K
                        act.wait_ge(unit_used, L * UNITS + i + 1)
                        dst = zt[:] if i == U_V else qk[:, 4 if i == U_K else i - U_Q, :]
                        A(dst, ps[:, i % 2, :], ACT.Copy).then_inc(proj_copied, 1)
                    elif what == "E":
                        c = i - U_Z
                        act.wait_ge(unit_used, L * UNITS + i + 1)
                        if c >= 1:
                            act.wait_ge(zs_done, L * CT + c)
                        A(zt[:], ps[:, i % 2, :], ACT.Tanh, scale=0.5).then_inc(tanh_done, 1)
                    elif what == "SILU":
                        act.wait_ge(conv_taps, L * 4 * N_CONV + 4 * i + 4)
                        if i >= 6:
                            wait_aux_full(act, L, ("T", i - 2))
                        dst = bc[:, i, :] if i < 4 else xsc[:, i % 2, :]
                        A(dst, cv[:, i % 2, :], ACT.Silu).then_inc(silu_done, 1)
                    elif what == "SP":
                        act.wait_ge(dt_abs, L + 1)
                        A(sp[:, 2, :], sp[:, 1, :], ACT.Exp, scale=-1.0).then_inc(dt_exp, 1)
                        A(neg_a[:], pmc("a_log"), ACT.Exp).then_inc(dt_exp, 1)
                    elif what == "SM":
                        wait_aux_full(act, L, ("SM", 0))
                        A(dec[:].rearrange("p t d h -> p (t d h)"), ps[:, aux_bank(("SM", 0)), 0:128],
                          ACT.Exp).then_inc(dec_done, 1)
                    elif what == "T":
                        wait_aux_full(act, L, ("T", i))
                        dst = b_tm[:, :, i * P:(i + 1) * P] if i < 2 else xs_tm[:, :, (i - 4) * P:(i - 3) * P]
                        A(dst, ps[:, aux_bank(("T", i)), :].rearrange("p (t c) -> p t c", c=P),
                          ACT.Copy).then_inc(t_evac, 1)
                    elif what == "VT":
                        wait_aux_full(act, L, ("VT", 0))
                        A(v_tm[:], ps[:, aux_bank(("VT", 0)), :].rearrange("p (t c) -> p t c", c=P),
                          ACT.Copy).then_inc(v_done, 1)
                    elif what == "ST":
                        t, g = i
                        wait_y_full(act, L, ("ST", i))
                        A(st[:, t % 2, g, :], ps[:, y_bank(("ST", i)), :], ACT.Copy).then_inc(st_done, 1)
                    elif what == "SC":
                        act.wait_ge(seg_full, L * 16 + i + 1)
                        if i >= 2:
                            act.wait_ge(seg_used, L * 16 + i - 1)
                        A(seg_e[:, i % 2, :, :].rearrange("p h q -> p (h q)"),
                          ps[:, 2:4, :].rearrange("p b n -> p (b n)"), ACT.Exp).then_inc(exp_done, 1)
                    elif what == "AS":
                        t, g = ATTN[i]
                        c = t % 2
                        for m in range(2):
                            wait_aux_full(act, L, ("AS", i, m))
                            if m == 0:
                                wait_aux_full(act, L, ("AP", i - 1, 1) if i else ("T", 11))
                            src = ps[:, aux_bank(("AS", i, m)), :].rearrange("p (j k) -> p j k", k=SEQ)
                            A(sc[:, 2 * m:2 * m + 2, c * P:(c + 1) * P], src[:, :, c * P:(c + 1) * P],
                              ACT.Copy).then_inc(as_copy, 1)
                        act.wait_ge(as_max, L * 8 + i + 1)
                        for j in range(QPK):
                            A(sc[:, j, :], sc[:, j, :], ACT.Exp, scale=SCALE, bias=ast[:, 1, j:j + 1],
                              accum_out=ast[:, 3, j:j + 1])
                        A(ast[:, 4, :], ast[:, 2, :], ACT.Exp).then_inc(as_exp, 1)
                    elif what == "AP":
                        wait_aux_full(act, L, ("AP", i, 0))
                        if i >= 1:
                            wait_aux_full(act, L, ("AV", i - 1))
                        A(p_t[:, 0, :], ps[:, aux_bank(("AP", i, 0)), :], ACT.Copy).then_inc(pt0_done, 1)
                    elif what == "AV":
                        t, g = ATTN[i]
                        rows = slice(g * HEAD, (g + 1) * HEAD)
                        wait_aux_full(act, L, ("AV", i))
                        A(ahi[rows, 0:QPK, t * BLK:(t + 1) * BLK],
                          ps[rows, aux_bank(("AV", i)), :].rearrange("p (j q) -> p j q", q=BLK),
                          ACT.Copy).then_inc(ah_done, 1)
                    elif what == "RS":
                        act.wait_ge(gated, L * 8 + 8)
                        if i >= 2:
                            act.wait_ge(rms_mm, L * CT + i - 1)
                        A(sq[:, i % 2, :], zs[:, i, :], ACT.Square).then_inc(rms_sq, 1)
                    elif what == "RMS":
                        act.wait_ge(rms_mm, L * CT + CT)
                        A(std[:], ps[:, aux_bank(("RS", 0)), :], ACT.Sqrt, bias=cst("eps")).then_inc(rms_std, 1)
                    elif what == "RN":
                        act.wait_ge(ssd_normed, L * CT + i + 1)
                        A(ahi[:, QPK + i, :], zs[:, i, :], ACT.Copy).then_inc(sh_done, 1)

                act.wait_ge(pf_loaded, L * 16 + 16)
                a1, b1 = PF["ln1_b"]
                layer_norm(L * 2 + 1, L, None, pf[:, a1:b1])

                def glu(I, p):
                    n = U_UP + 2 * p
                    off = I * 2 * RING
                    act.wait_ge(unit_used, L * UNITS + off + (n + 1))
                    k = (I * RING + p)
                    w0, _ = PF["conv_w"]
                    v0, _ = PF["conv_b"]
                    A(gcv[:], ps[:, 2 * p, :], ACT.Identity, scale=pf[:, bass.ds(k * 3 + (w0 + 1), 1)],
                      bias=pf[:, bass.ds(k + v0, 1)]).then_inc(glu_center, 1)
                    split_next(L, n, I * 2)
                    act.wait_ge(glu_taps, (L * FT + k + 1) * 2)
                    act.wait_ge(glu_done, L * FT + k + RING)
                    A(gsg[:], gcv[:], ACT.Silu).then_inc(glu_silu, 1)
                    split_next(L, n + 1, I * 2)
                    act.wait_ge(glu_done, L * FT + k + RING + 1)
                    A(uhi[:, bass.ds(k, 1), :].rearrange("p a n -> p (a n)"), guf[:], ACT.Copy).then_inc(glu_hi, 1)

                with act.Fori(0, FT // RING) as I:
                    for p in range(RING):
                        glu(I, p)
                glu(FT // RING, 0)
                with act.Fori(0, FT // RING) as I:
                    for j in range(RING):
                        split_next(L, U_DOWN + j, I)
                split_next(L, UNITS - 1)
                a2, b2 = PF["ln2_b"]
                layer_norm(L * 2 + 2, L, None, pf[:, a2:b2])

        @block.tensor
        def _(pe):
            mm = nc.tensor.matmul

            def three(out, slot, cols, xhi, xlo, start, stop):
                mm(out, whi[:, slot, cols], xhi, start=start, stop=False)
                mm(out, whi[:, slot, cols], xlo, start=False, stop=False)
                return mm(out, wlo[:, slot, cols], xhi, start=False, stop=stop)

            def by_columns(slot, bank, norm=None):
                for c in range(CT):
                    if norm is not None:
                        pe.wait_ge(h_ready, norm * CT + c + 1)
                    last = three(ps[:, bank, :], slot, slice(c * P, (c + 1) * P), hhi[:, c, :], hlo[:, c, :],
                                 c == 0, c == CT - 1)
                last.then_inc(unit_used, 1)

            def by_rows(slot, xhi, xlo, start=False, stop=False, before=None):
                order = ACC_ORDER if stop else range(CT)
                for n, c in enumerate(order):
                    if before and c in before:
                        pe.wait_ge(*before[c])
                    last = three(ps[:, c, :], slot, slice(c * P, (c + 1) * P), xhi, xlo, start, stop)
                    if stop and n < CT - 1:
                        last.then_inc(acc_done, 1)
                last.then_inc(unit_used, 1)

            def layer_norm(idx, res_count):
                for c in range(CT):
                    if res_count is not None and c:
                        pe.wait_ge(res_done, res_count + c + 1)
                    ch = ACC_ORDER[c] if res_count is not None else c
                    if res_count is not None and not c:
                        pe.wait_ge(res_done, res_count + 1)
                    last = mm(ps[:, 4, :], cst("avg"), h[:, ch, :], start=(c == 0), stop=(c == CT - 1))
                last.then_inc(ln_mean, 1)
                for c in range(CT):
                    if c == 0 and res_count is not None:
                        pe.wait_ge(res_done, res_count + 2)
                    pe.wait_ge(ln_sq, idx * CT + c + 1)
                    mm(ps[:, 5, :], cst("avg"), sq[:, c % 2, :], start=(c == 0), stop=(c == CT - 1)).then_inc(ln_sqmm, 1)

            pe.wait_ge(cn_loaded, 16)
            pe.wait_ge(x_loaded, 16)
            layer_norm(0, None)
            with pe.Fori(0, DEPTH) as L:
                for what, i in SCHED:
                    if what == "G" and i < U_OUT:
                        if i == 2:
                            pe.wait_ge(dt_copied, L + 1)
                        elif U_CONV <= i - 2 < U_K:
                            pe.wait_ge(conv_taps, L * 4 * N_CONV + 4 * (i - 2 - U_CONV) + 4)
                        elif U_K <= i - 2 < U_Z:
                            pe.wait_ge(proj_copied, L * 6 + i - 2 - U_K + 1)
                        elif i - 2 >= U_Z:
                            pe.wait_ge(zs_done, L * CT + i - 2 - U_Z + 1)
                        pe.wait_ge(unit_split, L * UNITS + i + 1)
                        by_columns(i % RING, i % 2, L * 2 if i == 0 else None)
                    elif what == "G":
                        k = i - U_OUT
                        pe.wait_ge(unit_split, L * UNITS + i + 1)
                        before = {}
                        if k == 0:
                            pe.wait_ge(zs_done, L * CT + CT)
                            pe.wait_ge(exp_done, L * 16 + 16)
                            pe.wait_ge(gated, L * 8 + 8)
                            pe.wait_ge(al_done, L * 8 + 8)
                            before = {aux_bank(("RS", 0)): (rms_std, L + 1)}
                        if k >= QPK:
                            pe.wait_ge(sl_done, L * CT + k - QPK + 1)
                        by_rows(i % RING, ahi[:, k, :], alo[:, k, :], k == 0, k == N_OUT - 1, before)
                    elif what == "DTT":
                        pe.wait_ge(dt_copied, L + 1)
                        for t in range(NBLK):
                            last = mm(ps[:, aux_bank((what, i)), t * 32:(t + 1) * 32],
                                      zt[0:32, t * BLK:(t + 1) * BLK], ident[0:32, 0:32], start=True, stop=True)
                        last.then_inc(aux_full, 1)
                    elif what == "SM":
                        pe.wait_ge(la_done, L + 1)
                        wait_aux_free(pe, L, (what, i))
                        for t in range(NBLK):
                            for d, w in enumerate(("after", "lower") if t % 2 == 0 else ("upper", "before")):
                                at0 = (2 * t + d) * SSD_HEADS
                                last = mm(ps[:, aux_bank((what, i)), at0:at0 + SSD_HEADS], cst(w),
                                          la[:, t, d * SSD_HEADS:(d + 1) * SSD_HEADS], start=True, stop=True)
                        last.then_inc(aux_full, 1)
                    elif what == "T":
                        pe.wait_ge(silu_done, L * N_CONV + i + 1)
                        wait_aux_free(pe, L, (what, i))
                        src = bc[:, i, :] if i < 4 else xsc[:, i % 2, :]
                        for t in range(NBLK):
                            last = nc.tensor.transpose(ps[:, aux_bank((what, i)), t * BLK:(t + 1) * BLK],
                                                       src[:, t * BLK:(t + 1) * BLK], ident)
                        last.then_inc(aux_full, 1)
                    elif what == "CB":
                        pe.wait_ge(silu_done, L * N_CONV + 4)
                        wait_aux_free(pe, L, (what, i))
                        for n in range(4):
                            t, g = 2 * i + n // 2, n % 2
                            last = mm(ps[:, aux_bank((what, i)), n * P:(n + 1) * P], bc[:, g, t * BLK:(t + 1) * BLK],
                                      bc[:, 2 + g, t * BLK:(t + 1) * BLK], start=True, stop=True)
                        last.then_inc(aux_full, 1)
                    elif what == "VT":
                        pe.wait_ge(proj_copied, L * 6 + 2)
                        wait_aux_free(pe, L, (what, i))
                        for t in range(NBLK):
                            last = nc.tensor.transpose(ps[:, aux_bank((what, i)), t * BLK:(t + 1) * BLK],
                                                       zt[:, t * BLK:(t + 1) * BLK], ident)
                        last.then_inc(aux_full, 1)
                    elif what == "ROT":
                        pe.wait_ge(proj_copied, L * 6 + (1 if i == 4 else 3 + i))
                        wait_aux_free(pe, L, (what, i))
                        mm(ps[:, aux_bank((what, i)), :], cst("rot"), qk[:, i, :], start=True,
                           stop=True).then_inc(aux_full, 1)
                    elif what == "ST":
                        t, g = i
                        pe.wait_ge(xw_done, L * NBLK + t + 1)
                        wait_y_free(pe, L, (what, i))
                        mm(ps[:, y_bank((what, i)), :], b_tm[:, t, g * STATE:(g + 1) * STATE],
                           xd[:, t % 2, g * 512:(g + 1) * 512], start=True, stop=True).then_inc(y_full, 1)
                    elif what == "YO":
                        t, g = i
                        pe.wait_ge(st_done, L * 8 + 4 * (t // 2) + 4)
                        wait_y_free(pe, L, (what, i))
                        mm(ps[:, y_bank((what, i)), :], bc[:, 2 + g, t * BLK:(t + 1) * BLK],
                           st[:, 1 - t % 2, g, :], start=True, stop=True).then_inc(y_full, 1)
                    elif what == "SB":
                        t, g, d = SEGS[i]
                        pe.wait_ge(r_done, L * 16 + i + 1)
                        if i >= 1:
                            pe.wait_ge(exp_done, L * 16 + i)
                        for n in range(2):
                            last = mm(ps[:, 2 + n, :], cst("after" if d == 0 else "before"),
                                      seg_r[:, 4 * n:4 * n + 4, :].rearrange("p h q -> p (h q)"), start=True, stop=True)
                        last.then_inc(seg_full, 1)
                    elif what == "SD":
                        t, g, d = SEGS[i]
                        pe.wait_ge(xd_done, L * 8 + 2 * t + 2)
                        pe.wait_ge(w_done, L * 16 + i + 1)
                        if d == 0:
                            wait_y_free(pe, L, ("SD", (t, g)))
                        bank = y_bank(("SD", (t, g)))
                        for n in range(HPG):
                            hd = g * HPG + n
                            last = mm(ps[:, bank, n * HEAD:(n + 1) * HEAD], seg_e[:, i % 2, n, :],
                                      xd[:, d, hd * HEAD:(hd + 1) * HEAD], start=(d == 0 and n == 0), stop=(d == 1),
                                      skip_group_check=True)
                        last.then_inc(seg_used, 1)
                    elif what == "YT":
                        t, g = i
                        pe.wait_ge(ya_done, L * 8 + 2 * t + g + 1)
                        wait_y_free(pe, L, (what, i))
                        for n in range(4):
                            c = 4 * g + n
                            last = nc.tensor.transpose(ps[:, y_bank((what, i)), n * BLK:(n + 1) * BLK],
                                                       xs_tm[:, t, c * P:(c + 1) * P], ident)
                        last.then_inc(y_full, 1)
                    elif what == "AS":
                        t, g = ATTN[i]
                        rows = slice(g * HEAD, (g + 1) * HEAD)
                        pe.wait_ge(rope_done, L * 5 + 5)
                        for m in range(2):
                            wait_aux_free(pe, L, (what, i, m))
                            for n in range(2):
                                last = mm(ps[:, aux_bank((what, i, m)), n * SEQ:(n + 1) * SEQ],
                                          qk[rows, 2 * m + n, t * BLK:(t + 1) * BLK],
                                          qk[rows, 4, (t // 2) * SEQ:(t // 2 + 1) * SEQ], start=True, stop=True)
                            last.then_inc(aux_full, 1)
                    elif what == "AP":
                        pe.wait_ge(as_norm, L * 8 + i + 1)
                        for kt in range(2):
                            wait_aux_free(pe, L, (what, i, kt))
                            for j in range(QPK):
                                last = nc.tensor.transpose(ps[:, aux_bank((what, i, kt)), j * BLK:(j + 1) * BLK],
                                                           sc[:, j, kt * P:(kt + 1) * P], ident)
                            last.then_inc(aux_full, 1)
                    elif what == "AV":
                        t, g = ATTN[i]
                        pe.wait_ge(v_done, L + 1)
                        pe.wait_ge(pt0_done, L * 8 + i + 1)
                        pe.wait_ge(pt1_done, L * 8 + i + 1)
                        wait_aux_free(pe, L, (what, i))
                        for kt in range(2):
                            last = mm(ps[g * HEAD:(g + 1) * HEAD, aux_bank((what, i)), :],
                                      v_tm[:, (t // 2) * 2 + kt, g * HEAD:(g + 1) * HEAD], p_t[:, kt, :],
                                      start=(kt == 0), stop=(kt == 1))
                        last.then_inc(aux_full, 1)
                    elif what == "RS":
                        pe.wait_ge(rms_sq, L * CT + i + 1)
                        if i == 0:
                            wait_aux_free(pe, L, (what, i))
                        mm(ps[:, aux_bank(("RS", 0)), :], cst("avg"), sq[:, i % 2, :], start=(i == 0),
                           stop=(i == CT - 1)).then_inc(rms_mm, 1)

                layer_norm(L * 2 + 1, L * 2 * CT)

                def glu(I, p):
                    k = I * RING + p
                    pe.wait_ge(h_ready, (L * 2 + 2) * CT)
                    pe.wait_ge(glu_done, L * FT + k + 1)
                    for half in range(2):
                        n = U_UP + 2 * p + half
                        pe.wait_ge(unit_split, L * UNITS + I * 2 * RING + (n + 1))
                        by_columns(n % RING, 2 * p + half)

                with pe.Fori(0, FT // RING) as I:
                    for p in range(RING):
                        glu(I, p)
                glu(FT // RING, 0)

                def down(k, n, start=False, stop=False):
                    pe.wait_ge(unit_split, L * UNITS + k + (U_DOWN + 1))
                    pe.wait_ge(glu_ready, L * FT + k + 1)
                    if start:
                        pe.wait_ge(glu_done, L * FT + FT + RING)
                    if isinstance(k, int):
                        xhi, xlo = uhi[:, k, :], ulo[:, k, :]
                    else:
                        xhi = uhi[:, bass.ds(k, 1), :].rearrange("p a n -> p (a n)")
                        xlo = ulo[:, bass.ds(k, 1), :].rearrange("p a n -> p (a n)")
                    by_rows((U_DOWN + n) % RING, xhi, xlo, start, stop)

                down(0, 0, start=True)
                with pe.Fori(0, (FT - 4) // RING) as I:
                    for j in range(RING):
                        down(I * RING + (1 + j), 1 + j)
                for k in range(FT - 3, FT):
                    down(k, k, stop=(k == FT - 1))
                layer_norm(L * 2 + 2, L * 2 * CT + CT)

        @block.vector
        def _(dve):
            V = nc.vector

            def split_lo(slot, count):
                dve.wait_ge(unit_hi, count)
                V.tensor_tensor(wlo[:, slot, :], raw[:, slot, :], f(whi[:, slot, :]), ALU.subtract).then_inc(unit_split, 1)

            def split_next(L, n, more=0):
                split_lo(n % RING, L * UNITS + (n + RING + 1) + more * RING)

            def residual(L, first, acc, rebuilt):
                for n, c in enumerate(ACC_ORDER):
                    if n < CT - 1:
                        dve.wait_ge(acc_done, acc + n + 1)
                    else:
                        dve.wait_ge(unit_used, first)
                    if rebuilt is not None:
                        dve.wait_ge(h_rebuilt, rebuilt + c + 1)
                    V.scalar_tensor_tensor(out=h[:, c, :], in0=h[:, c, :], scalar=ALPHA, in1=ps[:, c, :],
                                           op0=ALU.mult, op1=ALU.add).then_inc(res_done, 1)

            def layer_norm(idx, res_count, gam):
                dve.wait_ge(ln_mean, idx + 1)
                for c in range(CT):
                    V.tensor_tensor(h[:, c, :], h[:, c, :], ps[:, 4, :], ALU.subtract).then_inc(ln_cent, 1)
                dve.wait_ge(ln_std, idx + 1)
                V.reciprocal(std[:], std[:]).then_inc(ln_rstd, 1)
                dve.wait_ge(ln_rstd, idx + 1)
                for c in range(CT):
                    V.scalar_tensor_tensor(out=h[:, c, :], in0=h[:, c, :], scalar=gam[:, c:c + 1], in1=std[:],
                                           op0=ALU.mult, op1=ALU.mult).then_inc(ln_scaled, 1)
                    if c >= 1:
                        low(idx, c - 1)
                low(idx, CT - 1)

            def low(idx, c):
                dve.wait_ge(ln_h, idx * CT + c + 1)
                V.tensor_tensor(hlo[:, c, :], h[:, c, :], f(hhi[:, c, :]), ALU.subtract).then_inc(h_ready, 1)

            dve.sem_inc(glu_done, RING)
            dve.wait_ge(cn_loaded, 16)
            for j in range(RING):
                split_lo(j, j + 1)
            dve.wait_ge(x_loaded, 16)
            layer_norm(0, None, cst("ln_g"))

            with dve.Fori(0, DEPTH) as L:
                count = [0]

                def chain(ins):
                    count[0] += 1
                    ins.then_inc(link, 1)
                    dve.wait_ge(link, L * LINKS + count[0])

                dve.wait_ge(pm_loaded, L * 16 + 16)
                for what, i in SCHED:
                    if what == "S":
                        split_next(L, i - RING)
                    elif what == "E" and U_CONV <= i < U_K:
                        j = i - U_CONV
                        dve.wait_ge(conv_center, L * N_CONV + j + 1)
                        dst = cv[:, j % 2, :].rearrange("p (b s) -> p b s", b=NSEQ)
                        src = ps[:, i % 2, :].rearrange("p (b s) -> p b s", b=NSEQ)
                        for n, tap in enumerate((0, 1, 3, 4)):
                            s = tap - 2
                            lo, hi = max(0, -s), SEQ - max(0, s)
                            if n:
                                dve.wait_ge(conv_taps, L * 4 * N_CONV + 4 * j + n)
                            V.scalar_tensor_tensor(out=dst[:, :, lo:hi], in0=src[:, :, lo + s:hi + s],
                                                   scalar=pmc("conv_w", 5 * j + tap, 5 * j + tap + 1),
                                                   in1=dst[:, :, lo:hi], op0=ALU.mult, op1=ALU.add).then_inc(conv_taps, 1)
                    elif what == "E" and i >= U_Z:
                        c = i - U_Z
                        dve.wait_ge(tanh_done, L * CT + c + 1)
                        V.scalar_tensor_tensor(out=zs[:, c, :], in0=zt[:], scalar=1.0, in1=ps[:, i % 2, :],
                                               op0=ALU.add, op1=ALU.mult).then_inc(zs_done, 1)
                    elif what == "SP":
                        X, AB, E_, DEN, U1, U2, PL, MX = (sp[:, n, :] for n in range(8))
                        wait_aux_full(dve, L, ("DTT", 0))
                        bias = pmc("dt_bias").unsqueeze(1).broadcast_to((P, NBLK, 32))
                        V.tensor_tensor(X.rearrange("p (t c) -> p t c", c=32),
                                        ps[:, aux_bank(("DTT", 0)), 0:128].rearrange("p (t c) -> p t c", c=32),
                                        bias, ALU.add).then_inc(dtx_done, 1)
                        dve.wait_ge(dtx_done, L + 1)
                        V.scalar_tensor_tensor(out=AB, in0=X, scalar=-1.0, in1=X, op0=ALU.mult, op1=ALU.max).then_inc(dt_abs, 1)
                        dve.wait_ge(dt_exp, L * 2 + 2)
                        chain(V.tensor_scalar(DEN, E_, 2.0, None, ALU.add))
                        chain(V.reciprocal(DEN, DEN))
                        chain(V.tensor_tensor(U1, E_, DEN, ALU.mult))
                        chain(V.tensor_tensor(U2, U1, U1, ALU.mult))
                        chain(V.tensor_scalar(PL, U2, 1.0 / 15, None, ALU.mult))
                        for n in range(6, 0, -1):
                            chain(V.scalar_tensor_tensor(out=PL, in0=PL, scalar=1.0 / (2 * n + 1), in1=U2,
                                                         op0=ALU.add, op1=ALU.mult))
                        chain(V.scalar_tensor_tensor(out=PL, in0=PL, scalar=1.0, in1=U1, op0=ALU.add, op1=ALU.mult))
                        chain(V.tensor_scalar(MX, X, 0.0, None, ALU.max))
                        chain(V.scalar_tensor_tensor(out=dt[:].rearrange("p t c -> p (t c)"), in0=PL, scalar=2.0,
                                                     in1=MX, op0=ALU.mult, op1=ALU.add))
                        V.scalar_tensor_tensor(out=la[:], in0=dt[:], scalar=-1.0,
                                               in1=neg_a[:].unsqueeze(1).broadcast_to((P, NBLK, 32)),
                                               op0=ALU.mult, op1=ALU.mult).then_inc(la_done, 1)
                    elif what == "SM":
                        dve.wait_ge(dec_done, L + 1)
                        chain(V.tensor_tensor(dd[:].rearrange("p t d h -> p (t d h)"), dt[:].rearrange("p t c -> p (t c)"),
                                              dec[:].rearrange("p t d h -> p (t d h)"), ALU.mult))
                    elif what == "CB":
                        wait_aux_full(dve, L, (what, i))
                        src = ps[:, aux_bank((what, i)), :].rearrange("p (n q) -> p n q", q=P)
                        for d, m in enumerate(("upper", "lower")):
                            V.tensor_tensor(cb[:, d, 4 * i:4 * i + 4, :], src,
                                            cst(m).unsqueeze(1).broadcast_to((P, 4, P)), ALU.mult).then_inc(cb_done, 1)
                    elif what == "ROT":
                        wait_aux_full(dve, L, (what, i))
                        n = (i + 1) % 5
                        tt = ropet[:].rearrange("p (b s) -> p b s", b=NSEQ)
                        x = qk[:, i, :].rearrange("p (b s) -> p b s", b=NSEQ)
                        r = ps[:, aux_bank((what, i)), :].rearrange("p (b s) -> p b s", b=NSEQ)
                        if n:
                            dve.wait_ge(rope_done, L * 5 + n)
                        V.tensor_tensor(tt, r, cst("sin").unsqueeze(1).broadcast_to((P, NSEQ, SEQ)), ALU.mult).then_inc(rope_sin, 1)
                        chain(V.tensor_tensor(x, x, cst("cos").unsqueeze(1).broadcast_to((P, NSEQ, SEQ)), ALU.mult))
                        dve.wait_ge(rope_sin, L * 5 + n + 1)
                        V.tensor_tensor(qk[:, i, :], qk[:, i, :], ropet[:], ALU.add).then_inc(rope_done, 1)
                    elif what == "XW":
                        if i == 0:
                            dve.wait_ge(t_evac, L * 10 + 10)
                        if i == 2:
                            dve.wait_ge(seg_used, L * 16 + 8)
                        V.tensor_tensor(xd[:, i % 2, :].rearrange("p (h c) -> p h c", c=HEAD),
                                        xs_tm[:, i, :].rearrange("p (h c) -> p h c", c=HEAD),
                                        dd[:, i, i % 2, :].unsqueeze(2).broadcast_to((P, SSD_HEADS, HEAD)),
                                        ALU.mult).then_inc(xw_done, 1)
                    elif what == "XD":
                        if i % 2 == 0:
                            wait_y_full(dve, L, ("ST", (i + 1, 1)))
                            dve.wait_ge(xw_done, L * NBLK + i + 2)
                        else:
                            dve.wait_ge(seg_used, L * 16 + 4 * i)
                        for d in range(2):
                            V.tensor_tensor(xd[:, d, :].rearrange("p (h c) -> p h c", c=HEAD),
                                            xs_tm[:, i, :].rearrange("p (h c) -> p h c", c=HEAD),
                                            dt[:, i, d * SSD_HEADS:(d + 1) * SSD_HEADS].unsqueeze(2).broadcast_to((P, SSD_HEADS, HEAD)),
                                            ALU.mult).then_inc(xd_done, 1)
                    elif what == "SA":
                        t, g, d = SEGS[i]
                        if i >= 1:
                            dve.wait_ge(seg_full, L * 16 + i)
                        a0 = d * SSD_HEADS + g * HPG
                        V.tensor_tensor(seg_r[:], cst("upper" if d == 0 else "lower").unsqueeze(1).broadcast_to((P, HPG, P)),
                                        la[:, t, a0:a0 + HPG].unsqueeze(2).broadcast_to((P, HPG, P)),
                                        ALU.mult).then_inc(r_done, 1)
                    elif what == "SC":
                        t, g, d = SEGS[i]
                        dve.wait_ge(exp_done, L * 16 + i + 1)
                        if i == 0:
                            dve.wait_ge(cb_done, L * 4 + 4)
                        V.tensor_tensor(seg_e[:, i % 2, :, :], seg_e[:, i % 2, :, :],
                                        cb[:, d, 2 * t + g, :].unsqueeze(1).broadcast_to((P, HPG, P)),
                                        ALU.mult).then_inc(w_done, 1)
                    elif what == "YO":
                        t, g = i
                        wait_y_full(dve, L, (what, i))
                        V.tensor_tensor(yo[:].rearrange("p (h c) -> p h c", c=HEAD),
                                        ps[:, y_bank((what, i)), :].rearrange("p (h c) -> p h c", c=HEAD),
                                        dec[:, t, 1 - t % 2, g * HPG:(g + 1) * HPG].unsqueeze(2).broadcast_to((P, HPG, HEAD)),
                                        ALU.mult).then_inc(yo_done, 1)
                        dve.wait_ge(yo_done, L * 8 + 2 * t + g + 1)
                        dve.wait_ge(yd_done, L * NBLK + t + 1)
                        y = xs_tm[:, t, g * 512:(g + 1) * 512]
                        chain(V.tensor_tensor(y, y, yo[:], ALU.add))
                    elif what == "YA":
                        t, g = i
                        dve.wait_ge(seg_used, L * 16 + 4 * t + 2 * g + 2)
                        y = xs_tm[:, t, g * 512:(g + 1) * 512]
                        V.tensor_tensor(y, y, ps[:, y_bank(("SD", i)), :], ALU.add).then_inc(ya_done, 1)
                    elif what == "YT":
                        t, g = i
                        wait_y_full(dve, L, (what, i))
                        dve.wait_ge(zs_done, L * CT + 4 * g + 4)
                        z = zs[:, 4 * g:4 * g + 4, t * BLK:(t + 1) * BLK]
                        V.scalar_tensor_tensor(out=z, in0=ps[:, y_bank((what, i)), :].rearrange("p (n q) -> p n q", q=BLK),
                                               scalar=0.5, in1=z, op0=ALU.mult, op1=ALU.mult).then_inc(gated, 1)
                    elif what == "AS":
                        t, g = ATTN[i]
                        o = 1 - t % 2
                        mask = cst("before" if t % 2 == 0 else "after").unsqueeze(1).broadcast_to((P, 2, P))
                        for m in range(2):
                            wait_aux_full(dve, L, (what, i, m))
                            if m == 0:
                                wait_aux_full(dve, L, ("AP", i - 1, 1) if i else ("T", 11))
                            dve.wait_ge(as_copy, L * 16 + 2 * i + m + 1)
                            src = ps[:, aux_bank((what, i, m)), :].rearrange("p (j k) -> p j k", k=SEQ)
                            V.scalar_tensor_tensor(out=sc[:, 2 * m:2 * m + 2, o * P:(o + 1) * P], in0=mask,
                                                   scalar=MASK / SCALE, in1=src[:, :, o * P:(o + 1) * P],
                                                   op0=ALU.mult, op1=ALU.add).then_inc(as_mask, 1)
                        dve.wait_ge(as_mask, L * 16 + 2 * i + 2)
                        sink = pmc("sink", g * QPK, (g + 1) * QPK)
                        chain(V.tensor_reduce(ast[:, 0, :], sc[:], AX_X, ALU.max))
                        chain(V.scalar_tensor_tensor(out=ast[:, 0, :], in0=ast[:, 0, :], scalar=SCALE, in1=sink,
                                                     op0=ALU.mult, op1=ALU.max))
                        chain(V.tensor_scalar(ast[:, 1, :], ast[:, 0, :], -1.0, None, ALU.mult))
                        V.tensor_tensor(ast[:, 2, :], sink, ast[:, 0, :], ALU.subtract).then_inc(as_max, 1)
                        dve.wait_ge(as_exp, L * 8 + i + 1)
                        chain(V.tensor_tensor(ast[:, 5, :], ast[:, 3, :], ast[:, 4, :], ALU.add))
                        chain(V.reciprocal(ast[:, 5, :], ast[:, 5, :]))
                        for j in range(QPK):
                            last = V.tensor_scalar(sc[:, j, :], sc[:, j, :], ast[:, 5, j:j + 1], None, ALU.mult)
                        last.then_inc(as_norm, 1)
                    elif what == "AP":
                        wait_aux_full(dve, L, (what, i, 1))
                        if i >= 1:
                            wait_aux_full(dve, L, ("AV", i - 1))
                        V.tensor_copy(p_t[:, 1, :], ps[:, aux_bank((what, i, 1)), :]).then_inc(pt1_done, 1)
                    elif what == "AV":
                        t, g = ATTN[i]
                        rows = slice(g * HEAD, (g + 1) * HEAD)
                        dve.wait_ge(ah_done, L * 8 + i + 1)
                        V.tensor_tensor(alo[rows, 0:QPK, t * BLK:(t + 1) * BLK],
                                        ps[rows, aux_bank((what, i)), :].rearrange("p (j q) -> p j q", q=BLK),
                                        f(ahi[rows, 0:QPK, t * BLK:(t + 1) * BLK]), ALU.subtract).then_inc(al_done, 1)
                    elif what == "RMS":
                        dve.wait_ge(rms_std, L + 1)
                        chain(V.reciprocal(std[:], std[:]))
                        V.scalar_tensor_tensor(out=zs[:, 0, :], in0=zs[:, 0, :], scalar=pmc("norm_g", 0, 1), in1=std[:],
                                               op0=ALU.mult, op1=ALU.mult).then_inc(ssd_normed, 1)
                    elif what == "RN":
                        if i + 1 < CT:
                            V.scalar_tensor_tensor(out=zs[:, i + 1, :], in0=zs[:, i + 1, :],
                                                   scalar=pmc("norm_g", i + 1, i + 2), in1=std[:],
                                                   op0=ALU.mult, op1=ALU.mult).then_inc(ssd_normed, 1)
                        dve.wait_ge(sh_done, L * CT + i + 1)
                        V.tensor_tensor(alo[:, QPK + i, :], zs[:, i, :], f(ahi[:, QPK + i, :]), ALU.subtract).then_inc(sl_done, 1)

                assert count[0] == LINKS, count[0]
                residual(L, L * UNITS + U_UP, L * 14, L * CT)
                dve.wait_ge(pf_loaded, L * 16 + 16)
                a1, b1 = PF["ln1_g"]
                layer_norm(L * 2 + 1, None, pf[:, a1:b1])

                def glu(I, p):
                    n = U_UP + 2 * p
                    k = I * RING + p
                    w0, _ = PF["conv_w"]
                    dst = gcv[:].rearrange("p (b s) -> p b s", b=NSEQ)
                    src = ps[:, 2 * p, :].rearrange("p (b s) -> p b s", b=NSEQ)
                    dve.wait_ge(glu_center, L * FT + k + 1)
                    V.scalar_tensor_tensor(out=dst[:, :, 1:SEQ], in0=src[:, :, 0:SEQ - 1], scalar=pf[:, bass.ds(k * 3 + w0, 1)],
                                           in1=dst[:, :, 1:SEQ], op0=ALU.mult, op1=ALU.add).then_inc(glu_taps, 1)
                    dve.wait_ge(glu_taps, (L * FT + k) * 2 + 1)
                    V.scalar_tensor_tensor(out=dst[:, :, 0:SEQ - 1], in0=src[:, :, 1:SEQ], scalar=pf[:, bass.ds(k * 3 + (w0 + 2), 1)],
                                           in1=dst[:, :, 0:SEQ - 1], op0=ALU.mult, op1=ALU.add).then_inc(glu_taps, 1)
                    split_next(L, n, I * 2)
                    dve.wait_ge(unit_used, L * UNITS + I * 2 * RING + (n + 2))
                    dve.wait_ge(glu_silu, L * FT + k + 1)
                    V.tensor_tensor(guf[:], gsg[:], ps[:, 2 * p + 1, :], ALU.mult).then_inc(glu_done, 1)
                    split_next(L, n + 1, I * 2)
                    dve.wait_ge(glu_hi, L * FT + k + 1)
                    V.tensor_tensor(ulo[:, bass.ds(k, 1), :].rearrange("p a n -> p (a n)"), guf[:],
                                    f(uhi[:, bass.ds(k, 1), :]).rearrange("p a n -> p (a n)"),
                                    ALU.subtract).then_inc(glu_ready, 1)

                with dve.Fori(0, FT // RING) as I:
                    for p in range(RING):
                        glu(I, p)
                glu(FT // RING, 0)
                with dve.Fori(0, FT // RING) as I:
                    for j in range(RING):
                        split_next(L, U_DOWN + j, I)
                split_next(L, UNITS - 1)
                residual(L, L * UNITS + UNITS, L * 14 + 7, None)
                a2, b2 = PF["ln2_g"]
                layer_norm(L * 2 + 2, None, pf[:, a2:b2])


def constants():
    k = np.arange(P)[:, None]
    q = np.arange(P)[None, :]
    rot = np.zeros((P, P), np.float32)
    for m in range(P):
        if m % HEAD < HEAD // 2:
            rot[m + HEAD // 2, m] = -1.0
        else:
            rot[m - HEAD // 2, m] = 1.0
    freq = np.float32(10000.0) ** (-np.arange(0, HEAD, 2, dtype=np.float32) / np.float32(HEAD))
    ang = np.arange(SEQ, dtype=np.float32)[None, :] * freq[np.arange(P) % (HEAD // 2)][:, None]
    return {
        "ident": np.eye(P), "avg": np.full((P, P), 1.0 / D_MODEL), "upper": q >= k, "lower": q <= k,
        "after": k > q, "before": k < q, "rot": rot, "cos": np.cos(ang), "sin": np.sin(ang),
        "eps": np.full((P, 1), EPS),
    }


def lay_out(x_prompt, x_sample, ln_in_g, ln_in_b, w_in, attn_sink, ssd_conv_w, ssd_conv_b, ssd_a_log,
            ssd_dt_bias, ssd_d, ssd_norm_g, w_out, ln1_g, ln1_b, w_up, ffn_conv_w, ffn_conv_b, w_down,
            ln2_g, ln2_b):
    def by_columns(w):
        n = w.shape[1] // P
        return w.reshape(CT, P, n, P).transpose(2, 1, 0, 3).reshape(n, P, D_MODEL)

    def channels(v):
        return v.reshape(-1, P).T

    def everywhere(v):
        return np.broadcast_to(v.reshape(1, -1), (P, v.size))

    x = np.concatenate([x_prompt.reshape(SEQ, D_MODEL), x_sample.reshape(SEQ, D_MODEL)])
    x_t = x.T.reshape(CT, P, TOK).transpose(1, 0, 2)
    aw, kw = 512, 128
    z0 = aw + 2 * kw
    xbc0 = z0 + SSD_WIDTH
    dt0 = xbc0 + SSD_WIDTH + 4 * STATE
    units, pms, pfs = [], [], []
    for i in range(DEPTH):
        w = w_in[i]
        dtw = np.zeros((D_MODEL, P), w.dtype)
        dtw[:, :32] = w[:, dt0:dt0 + 32]
        xbc = w[:, xbc0:dt0]
        q = w[:, :aw].reshape(D_MODEL, 2, QPK, HEAD).transpose(0, 2, 1, 3).reshape(D_MODEL, aw)
        units.append(by_columns(np.concatenate(
            [dtw, xbc[:, SSD_WIDTH:], xbc[:, :SSD_WIDTH], w[:, aw:z0], q, w[:, z0:xbc0]], axis=1)))
        wo = w_out[i]
        wa = wo[:aw].reshape(2, QPK, HEAD, D_MODEL).transpose(1, 0, 2, 3).reshape(QPK, P, D_MODEL)
        units += [wa, wo[aw:].reshape(CT, P, D_MODEL)]
        up = by_columns(w_up[i])
        units.append(np.stack([up[:FT], up[FT:]], axis=1).reshape(2 * FT, P, D_MODEL))
        units.append(w_down[i].reshape(FT, P, D_MODEL))
        cw = np.concatenate([ssd_conv_w[i][:, SSD_WIDTH:], ssd_conv_w[i][:, :SSD_WIDTH]], axis=1)
        cbias = np.concatenate([ssd_conv_b[i][SSD_WIDTH:], ssd_conv_b[i][:SSD_WIDTH]])
        pms.append(np.concatenate([
            cw.reshape(5, N_CONV, P).transpose(2, 1, 0).reshape(P, 5 * N_CONV), channels(cbias),
            channels(ssd_norm_g[i]), everywhere(attn_sink[i]), everywhere(ssd_a_log[i]),
            everywhere(ssd_dt_bias[i]), everywhere(ssd_d[i])], axis=1))
        pfs.append(np.concatenate([
            ffn_conv_w[i].reshape(3, FT, P).transpose(2, 1, 0).reshape(P, 3 * FT), channels(ffn_conv_b[i]),
            channels(ln1_g[i]), channels(ln1_b[i]), channels(ln2_g[i]), channels(ln2_b[i])], axis=1))
    cn = np.zeros((P, CN_W), x.dtype)
    for name, v in constants().items():
        cn[:, CN[name][0]:CN[name][1]] = v
    cn[:, CN["ln_g"][0]:CN["ln_g"][1]] = channels(ln_in_g)
    cn[:, CN["ln_b"][0]:CN["ln_b"][1]] = channels(ln_in_b)
    return {"x_t": x_t, "units": np.concatenate(units), "pm": np.stack(pms), "pf": np.stack(pfs), "cn": cn}


def kernel(**inputs):
    import concourse.bacc as _bacc
    from concourse.bass_utils import run_bass_kernel_spmd as _run

    nc = _bacc.Bacc("TRN2", target_bir_lowering=False, num_devices=1)
    arrays, args = {}, []
    for name, a in lay_out(**{k: np.asarray(v) for k, v in inputs.items()}).items():
        a = np.ascontiguousarray(a)
        arrays[f"in_{name}"] = a
        args.append(nc.dram_tensor(f"in_{name}", a.shape, mybir.dt.from_np(a.dtype), kind="ExternalInput").ap())
    y_t = nc.dram_tensor("out_y", (P, CT, TOK), F32, kind="ExternalOutput").ap()
    trunk(nc, *args, y_t)
    r = _run(nc, [arrays], core_ids=[0])
    y = np.asarray(r.results[0]["out_y"]).transpose(2, 1, 0).reshape(NSEQ, 1, SEQ, D_MODEL)
    return y[0], y[1]
```

```python
from contextlib import ExitStack

import numpy as np

import concourse.bass as bass
from concourse import mybir

F32 = mybir.dt.float32
F32R = mybir.dt.float32r
ALU = mybir.AluOpType
ACT = mybir.ActivationFunctionType
AX_X = mybir.AxisListType.X

P = 128
DEPTH, D_MODEL, SEQ, NSEQ = 2, 1024, 256, 2
TOK = NSEQ * SEQ
BLK = 128
NBLK = TOK // BLK
HEAD = 64
QPK = 4
SSD_HEADS, SSD_WIDTH, STATE = 16, 1024, 128
HPG = 8
D_FF = 2816
CT = D_MODEL // P
FT = D_FF // P
ALPHA = (2 * DEPTH) ** 0.25
EPS = 1e-5
MASK = -1e30
SCALE = HEAD ** -0.5

U_DT = 0
U_K, U_V, U_Q = 1, 2, 3
U_CONV = 7
N_CONV = 12
U_Z = U_CONV + N_CONV
U_OUT = 27
N_OUT = 12
U_UP = U_OUT + N_OUT
U_DOWN = U_UP + 2 * FT
UNITS = U_DOWN + FT
RING = 3
assert UNITS % RING == 0 and U_UP % RING == 0
TURNS = UNITS // RING

PM = {}
PF = {}


def _columns(table, widths):
    at = 0
    for name, w in widths:
        table[name] = (at, at + w)
        at += w
    return at


PM_W = _columns(PM, [("conv_w", N_CONV * 5), ("conv_b", N_CONV), ("norm_g", CT), ("sink", 8),
                     ("a_log", 32), ("dt_bias", 32), ("d", SSD_HEADS)])
PF_W = _columns(PF, [("conv_w", FT * 3), ("conv_b", FT), ("ln1_g", CT), ("ln1_b", CT),
                     ("ln2_g", CT), ("ln2_b", CT)])
CN = {}
CN_W = _columns(CN, [("ident", P), ("avg", P), ("upper", P), ("lower", P), ("after", P),
                     ("before", P), ("rot", P), ("cos", SEQ), ("sin", SEQ), ("eps", 1),
                     ("ln_g", CT), ("ln_b", CT)])

SEGS = [(t, g, d) for g in range(2) for t in range(NBLK) for d in range(2)]
ATTN = [(t, g) for t in range(NBLK) for g in range(2)]
A0 = 8
SEG_SLOTS = {17: [0], 18: [1, 2], 19: [3], 20: [4, 5], 21: [6, 7], 22: [8, 9], 23: [10], 24: [11, 12],
             25: [13], 26: [14, 15]}
SEG_LAG = 2


def seg_steps(k):
    out = []
    if k < len(SEGS):
        out += [("SB", k), ("SE", k)]
        if k + 1 < len(SEGS):
            out += [("SA", k + 1)]
        out += [("SC", k)]
    n = k - SEG_LAG
    if n >= 0:
        m, d = divmod(n, 2)
        out += [("SD", n)]
        out += [("YO", m)] if d == 0 else [("YA", m)]
    return out


def mixer_schedule():
    steps = []
    for n in range(U_OUT):
        i = n - A0
        steps += [("G", n), ("E", n)]
        if 0 <= i < 8:
            steps += [("AS", i), ("AM", i)]
        if n == 1:
            steps += [("DTT", 0), ("SP", 0)]
        if n == 3:
            steps += [("SM", 0)]
        if n - 1 == U_V:
            steps += [("VT", 0)]
        if n - 1 == U_K:
            steps += [("ROT", 4)]
        if U_Q <= n - 1 < U_Q + 4:
            steps += [("ROT", n - 1 - U_Q)]
        j = n - 1 - U_CONV
        if j in (0, 1) or 4 <= j < N_CONV:
            steps += [("T", j)]
        if j == 4:
            steps += [("CB", 0)]
        if j == 5:
            steps += [("CB", 1)]
        steps += [("S", n + RING)]
        if 0 <= i < 8:
            steps += [("AX", i)]
        steps += [("F", n)]
        if 0 <= i < 8:
            steps += [("AD", i), ("AN", i)]
        if 0 <= i - 1 < 8:
            steps += [("AP", i - 1)]
        if 0 <= i - 2 < 8:
            steps += [("AV", i - 2)]
        if n in (16, 21):
            m = 0 if n == 16 else 4
            steps += [("XD", m), ("XW", m), ("XW", m + 1), ("DS", m), ("XD", m + 1), ("DS", m + 1),
                      ("XW", m + 2), ("XW", m + 3)]
        if n in (19, 24):
            m = 2 if n == 19 else 6
            steps += [("XD", m), ("DS", m), ("XD", m + 1), ("DS", m + 1)]
        if n in (17, 22):
            m = 0 if n == 17 else 4
            steps += [("ST", m), ("ST", m + 1)]
        if n in (18, 23):
            m = 2 if n == 18 else 6
            steps += [("ST", m), ("ST", m + 1)]
        if n == 16:
            steps += [("SA", 0)]
        for k in SEG_SLOTS.get(n, []):
            steps += seg_steps(k)
        if n == 24:
            steps += [("YT", 0), ("YT", 1)]
        if n == 25:
            steps += [("YT", 2), ("YT", 3)]
        if n == 26:
            steps += [("RS", c) for c in range(4)]
        steps += [("SILU", n - U_CONV)] if U_CONV <= n < U_Z else []
    steps += [("YT", 4), ("YT", 5)]
    steps += seg_steps(16) + seg_steps(17)
    steps += [("YT", 6), ("GA", U_OUT), ("YT", 7)]
    steps += [("RS", c) for c in range(4, CT)]
    steps += [("RMS", 0)]
    for u in range(U_OUT, U_UP):
        steps.append(("G", u))
        if u - U_OUT >= 1:
            steps.append(("RN", u - U_OUT - 1)) if u - U_OUT - 1 < CT else None
        if u + 1 < U_UP:
            steps.append(("S", u + RING))
    return steps


SCHED = mixer_schedule()
LINKS = 14 + 5 + 8 + 4 * 8 + 1


def trunk(nc, x_t, units, pm_d, pf_d, cn_d, y_t):
    ctx = ExitStack()
    with ctx:
        def sb(name, shape, dt=F32):
            return ctx.enter_context(nc.sbuf_tensor(name, shape, dt))

        def sem(name):
            return ctx.enter_context(nc.semaphore(name))

        cn = sb("cn", [P, CN_W])
        pm = sb("pm", [P, PM_W])
        pf = sb("pf", [P, PF_W])
        raw = sb("raw", [P, RING, 1024])
        whi = sb("whi", [P, RING, 1024], F32R)
        wlo = sb("wlo", [P, RING, 1024], F32R)
        hhi = sb("hhi", [P, CT, TOK], F32R)
        hlo = sb("hlo", [P, CT, TOK], F32R)
        dt = sb("dt", [P, NBLK, 32])
        la = sb("la", [P, NBLK, 32])
        dec = sb("dec", [P, NBLK, 2, SSD_HEADS])
        dd = sb("dd", [P, NBLK, 2, SSD_HEADS])
        neg_a = sb("neg_a", [P, 32])
        ast = sb("ast", [P, 2, 6, QPK])
        big_i = sb("big_i", [P, P], F32R)
        cut = sb("cut", [P, 2, P], F32R)
        KB = 1024
        arena_h = sb("arena_h", [P, CT * TOK])
        arena = sb("arena", [P, 102 * KB // 4])
        base_h = nc.sbuf_base - 102 * KB - CT * TOK * 4
        base = nc.sbuf_base - 102 * KB

        def at(name, kb, shape, dtype=F32, start=None):
            return nc.alloc_sbuf_tensor_at(name, shape, dtype, offset=(base if start is None else start) + int(kb * KB))

        h = at("h", 0, [P, CT, TOK], start=base_h)
        zs = at("zs", 0, [P, CT, TOK], start=base_h)
        bc = at("bc", 0, [P, 4, TOK])
        ropet = at("ropet", 0, [P, TOK])
        yo = at("yo", 2, [P, 512])
        b_tm = at("b_tm", 8, [P, NBLK, 2 * STATE])
        st = at("st", 12, [P, NBLK, 512])
        qk = at("qk", 20, [P, 5, TOK])
        xw = at("xw", 20, [P, NBLK, 512])
        sqr = at("sqr", 28, [P, 2, TOK])
        v_tm = at("v_tm", 30, [P, NBLK, P])
        zt = at("zt", 32, [P, TOK])
        sc = [at("sc0", 34, [P, QPK, SEQ]), at("sc1", 0, [P, QPK, SEQ], start=base_h)]
        p_t = [at("p_t0", 38, [P, 2, 512]), at("p_t1", 4, [P, 2, 512], start=base_h)]
        cv = at("cv", 8, [P, 2, TOK], start=base_h)
        xsc = at("xsc", 12, [P, 2, TOK], start=base_h)
        ahi = at("ahi", 42, [P, N_OUT, TOK], F32R)
        alo = at("alo", 66, [P, N_OUT, TOK], F32R)
        xs_tm = at("xs_tm", 50, [P, NBLK, SSD_WIDTH])
        cb = at("cb", 74, [P, 2, 8, P])
        xd = at("xd", 82, [P, 2, 2, 512])
        seg_r = [at("seg_r0", 90, [P, HPG, P]), at("seg_r1", 38, [P, HPG, P])]
        sp = at("sp", 90, [P, 8, 128])
        seg_e = [at("seg_e0", 94, [P, HPG, P]), at("seg_e1", 98, [P, HPG, P]), at("seg_e2", 34, [P, HPG, P])]
        sq = at("sq", 94, [P, 2, TOK])
        std = at("std", 98, [P, TOK])
        uhi = at("uhi", 0, [P, FT, TOK], F32R)
        ulo = at("ulo", 44, [P, FT, TOK], F32R)
        gcv = at("gcv", 88, [P, TOK])
        gsg = at("gsg", 90, [P, TOK])
        guf = at("guf", 92, [P, TOK])

        ps = ctx.enter_context(nc.psum_tensor("ps", [P, 8, 512], F32))

        def f(view):
            return view.bitcast(F32)

        def cst(name, lo=0, hi=None):
            a, b = CN[name]
            return cn[:, a + lo:(b if hi is None else a + hi)]

        def pmc(name, lo=0, hi=None):
            a, b = PM[name]
            return pm[:, a + lo:(b if hi is None else a + hi)]

        ident = cst("ident")

        cn_loaded, x_loaded = sem("cn_loaded"), sem("x_loaded")
        pm_loaded, pf_loaded = sem("pm_loaded"), sem("pf_loaded")
        raw_loaded = [sem(f"raw_loaded{k}") for k in range(RING)]
        unit_hi, unit_split, unit_used = sem("unit_hi"), sem("unit_split"), sem("unit_used")
        y_stored = sem("y_stored")
        link = sem("dve_link")
        dt_copied, dt_abs, dt_exp = sem("dt_copied"), sem("dt_abs"), sem("dt_exp")
        dtx_done, la_done, dec_done = sem("dtx_done"), sem("la_done"), sem("dec_done")
        dd_done = sem("dd_done")
        conv_center, conv_taps = sem("conv_center"), sem("conv_taps")
        conv_tanh, silu_done = sem("conv_tanh"), sem("silu_done")
        aux_full, t_evac, cb_done = sem("aux_full"), sem("t_evac"), sem("cb_done")
        proj_copied, rope_sin, rope_done = sem("proj_copied"), sem("rope_sin"), sem("rope_done")
        v_done, tanh_done, zs_done = sem("v_done"), sem("tanh_done"), sem("zs_done")
        xw_done, y_full, st_done, xd_done = sem("xw_done"), sem("y_full"), sem("st_done"), sem("xd_done")
        yd_done, r_done, seg_full = sem("yd_done"), sem("r_done"), sem("seg_full")
        exp_done, w_done, seg_used = sem("exp_done"), sem("w_done"), sem("seg_used")
        yo_done, ya_done, gated = sem("yo_done"), sem("ya_done"), sem("gated")
        as_const, as_full, as_max = sem("as_const"), sem("as_full"), sem("as_max")
        as_exp, as_den, as_norm = sem("as_exp"), sem("as_den"), sem("as_norm")
        pt0_done, pt1_done, ah_done, al_done = sem("pt0_done"), sem("pt1_done"), sem("ah_done"), sem("al_done")
        rms_sq, rms_mm, rms_std = sem("rms_sq"), sem("rms_mm"), sem("rms_std")
        ssd_normed, sh_done, sl_done = sem("ssd_normed"), sem("sh_done"), sem("sl_done")
        h_rebuilt, acc_done, res_done = sem("h_rebuilt"), sem("acc_done"), sem("res_done")
        ln_mean, ln_cent, ln_sq, ln_sqmm = sem("ln_mean"), sem("ln_cent"), sem("ln_sq"), sem("ln_sqmm")
        ln_rstd = sem("ln_rstd")
        ln_std, ln_scaled, ln_hi, h_ready = sem("ln_std"), sem("ln_scaled"), sem("ln_hi"), sem("h_ready")
        h_back, y_ready = sem("h_back"), sem("y_ready")
        glu_center, glu_taps, glu_silu = sem("glu_center"), sem("glu_taps"), sem("glu_silu")
        glu_done, glu_hi, glu_ready = sem("glu_done"), sem("glu_hi"), sem("glu_ready")

        aux_use, y_use = {}, {}
        aux_free, y_free = [], []
        aux_counted, y_counted = {}, {}

        def take(use, free, counted, key, releases, counts=True):
            use[key] = len(free)
            free.append(releases)
            if counts:
                counted[key] = len(counted) + 1

        n_t = 0
        for what, i in SCHED:
            aux = lambda key, rel, c=True: take(aux_use, aux_free, aux_counted, key, rel, c)
            yy = lambda key, rel, c=True: take(y_use, y_free, y_counted, key, rel, c)
            if what == "DTT":
                aux(("DTT", 0), [(dtx_done, 1, 1)])
            elif what == "SM":
                aux(("SM", 0), [(dec_done, 1, 1)])
            elif what == "CB":
                aux(("CB", i), [(cb_done, 4, 2 * i + 2)])
            elif what == "T":
                n_t += 1
                aux(("T", i), [(t_evac, 10, n_t)])
            elif what == "VT":
                aux(("VT", 0), [(v_done, 1, 1)])
            elif what == "ROT":
                aux(("ROT", i), [(rope_sin, 5, (i + 1) % 5 + 1)])
            elif what == "AP":
                yy(("AP", i, 0), [(pt0_done, 8, i + 1)])
                yy(("AP", i, 1), [(pt1_done, 8, i + 1)])
            elif what == "AV":
                aux(("AV", i), [(al_done, 8, i + 1)])
            elif what == "RS" and i == 0:
                aux(("RS", 0), [(rms_std, 1, 1)], False)
            elif what == "ST":
                aux(("ST", i), [(st_done, 8, i + 1)])
            elif what == "YO":
                yy(("YO", i), [(yo_done, 8, i + 1)])
            elif what == "SD" and SEGS[i][2] == 0:
                yy(("SD", i // 2), [(ya_done, 8, i // 2 + 1)], False)
            elif what == "YT":
                (aux if i < 4 else yy)(("YT", i), [(gated, 8, i + 1)])
        AUX_N, Y_N = len(aux_counted), len(y_counted)
        def aux_bank(key):
            return 6 + aux_use[key] % 2

        def y_bank(key):
            return 4 + y_use[key] % 2

        def wait_aux_free(eng, L, key):
            n = aux_use[key] - 2
            if n >= 0:
                for s, per, count in aux_free[n]:
                    eng.wait_ge(s, L * per + count)

        def wait_y_free(eng, L, key):
            n = y_use[key] - 2
            if n >= 0:
                for s, per, count in y_free[n]:
                    eng.wait_ge(s, L * per + count)

        def wait_aux_full(eng, L, key):
            eng.wait_ge(aux_full, L * AUX_N + aux_counted[key])

        def wait_y_full(eng, L, key):
            eng.wait_ge(y_full, L * Y_N + y_counted[key])

        ACC_ORDER = [4, 5, 6, 7, 0, 1, 2, 3]
        LAG = 3

        block = ctx.enter_context(nc.Block())

        @block.sync
        def _(sp_eng):
            sp_eng.dma_start(h[:], x_t).then_inc(x_loaded, 16)
            for j in range(RING):
                sp_eng.dma_start(raw[:, j, :], units[j]).then_inc(raw_loaded[j], 16)
            with sp_eng.Fori(1, DEPTH * TURNS) as g:
                for j in range(RING):
                    sp_eng.wait_ge(unit_split, g * RING + (j - RING + 1))
                    sp_eng.dma_start(raw[:, j, :], units[g * RING + j]).then_inc(raw_loaded[j], 16)
            for j in range(RING):
                sp_eng.wait_ge(unit_split, (DEPTH * TURNS - 1) * RING + j + 1)
                sp_eng.dma_start(raw[:, j, :], units[j]).then_inc(raw_loaded[j], 16)
            for c in range(CT):
                sp_eng.wait_ge(y_ready, c + 1)
                sp_eng.dma_start(y_t[:, c, :], h[:, c, :]).then_inc(y_stored, 16)
            sp_eng.wait_ge(y_stored, CT * 16)

        @block.gpsimd
        def _(pool):
            pool.dma_start(cn[:], cn_d).then_inc(cn_loaded, 16)
            with pool.Fori(0, DEPTH) as L:
                pool.wait_ge(h_ready, (L * 2 + 1) * CT)
                pool.dma_start(pm[:], pm_d[L]).then_inc(pm_loaded, 16)
                pool.dma_start(pf[:], pf_d[L]).then_inc(pf_loaded, 16)
                pool.wait_ge(pm_loaded, L * 16 + 16)
                for what, i in SCHED:
                    if what == "AN":
                        pool.wait_ge(as_den, L * 8 + i + 1)
                        nc.gpsimd.tensor_tensor(sc[i % 2][:], sc[i % 2][:],
                                                ast[:, i % 2, 5, :].unsqueeze(2).broadcast_to((P, QPK, SEQ)),
                                                ALU.mult).then_inc(as_norm, 1)
                    elif what in ("XD", "XW", "DS"):
                        g, t = divmod(i, NBLK)
                        x = xs_tm[:, t, g * 512:(g + 1) * 512].rearrange("p (h c) -> p h c", c=HEAD)
                        scaled = (P, HPG, HEAD)
                        if i in (0, NBLK) and what == "XD":
                            pool.wait_ge(t_evac, L * 10 + 6 + 4 * g)
                            pool.wait_ge(dd_done, L + 1)
                        if what == "XD":
                            if i >= 2:
                                pool.wait_ge(seg_used, L * 16 + 2 * i - 2)
                            for d in range(2):
                                a0 = d * SSD_HEADS + g * HPG
                                nc.gpsimd.tensor_tensor(xd[:, i % 2, d, :].rearrange("p (h c) -> p h c", c=HEAD), x,
                                                        dt[:, t, a0:a0 + HPG].unsqueeze(2).broadcast_to(scaled),
                                                        ALU.mult).then_inc(xd_done, 1)
                        elif what == "XW":
                            if i == 0:
                                pool.wait_ge(as_full, L * 8 + 8)
                            if g == 1:
                                wait_aux_full(pool, L, ("ST", i - NBLK))
                            nc.gpsimd.tensor_tensor(xw[:, t, :].rearrange("p (h c) -> p h c", c=HEAD), x,
                                                    dd[:, t, t % 2, g * HPG:(g + 1) * HPG].unsqueeze(2).broadcast_to(scaled),
                                                    ALU.mult).then_inc(xw_done, 1)
                        else:
                            pool.wait_ge(xd_done, L * 16 + 2 * i + 2)
                            pool.wait_ge(xw_done, L * 8 + i + 1)
                            nc.gpsimd.tensor_tensor(x, x, pmc("d", g * HPG, (g + 1) * HPG).unsqueeze(2).broadcast_to(scaled),
                                                    ALU.mult).then_inc(yd_done, 1)
                for c in range(CT):
                    pool.wait_ge(sl_done, L * CT + c + 1)
                    nc.gpsimd.tensor_tensor(h[:, c, :], f(hhi[:, c, :]), f(hlo[:, c, :]), ALU.add).then_inc(h_rebuilt, 1)
                for c in range(CT):
                    pool.wait_ge(h_ready, (L * 2 + 1) * CT + c + 1)
                    nc.gpsimd.tensor_tensor(h[:, c, :], f(hhi[:, c, :]), f(hlo[:, c, :]), ALU.add).then_inc(h_back, 1)

        @block.scalar
        def _(act):
            A = nc.scalar.activation

            def split_hi(turn, slot, first=False):
                act.wait_ge(raw_loaded[slot], turn * 16 + 16)
                A(whi[:, slot, :], raw[:, slot, :], ACT.Copy).then_inc(unit_hi, 1)

            def split_next(L, n, more=0):
                act.wait_ge(unit_used, L * UNITS + n + 1 + more * RING)
                split_hi(L * TURNS + (n // RING + 1) + more, n % RING)

            def layer_norm(idx, L, gam, bet):
                for c in range(CT):
                    act.wait_ge(ln_cent, idx * CT + c + 1)
                    if c >= 2:
                        act.wait_ge(ln_sqmm, idx * CT + c - 1)
                    A(sq[:, c % 2, :], h[:, c, :], ACT.Square).then_inc(ln_sq, 1)
                act.wait_ge(ln_sqmm, idx * CT + CT)
                A(std[:], ps[:, 5, :], ACT.Sqrt, bias=cst("eps")).then_inc(ln_std, 1)
                for c in range(CT):
                    act.wait_ge(ln_scaled, idx * CT + c + 1)
                    A(hhi[:, c, :], h[:, c, :], ACT.Identity, bias=bet[:, c:c + 1]).then_inc(ln_hi, 1)

            act.wait_ge(cn_loaded, 16)
            A(big_i[:], ident, ACT.Copy, scale=MASK / SCALE).then_inc(as_const, 1)
            A(cut[:, 0, :], cst("before"), ACT.Copy).then_inc(as_const, 1)
            A(cut[:, 1, :], cst("after"), ACT.Copy).then_inc(as_const, 1)
            for j in range(RING):
                split_hi(0, j)
            layer_norm(0, None, cst("ln_g"), cst("ln_b"))

            with act.Fori(0, DEPTH) as L:
                act.wait_ge(pm_loaded, L * 16 + 16)
                for what, i in SCHED:
                    if what == "S":
                        split_next(L, i - RING)
                    elif what == "E" and i == U_DT:
                        act.wait_ge(unit_used, L * UNITS + i + 1)
                        A(zt[0:32, :], ps[0:32, i % 2, :], ACT.Copy).then_inc(dt_copied, 1)
                    elif what == "E" and U_CONV <= i < U_Z:
                        j = i - U_CONV
                        act.wait_ge(unit_used, L * UNITS + i + 1)
                        if j >= 2:
                            act.wait_ge(silu_done, L * N_CONV + j - 1)
                        A(cv[:, j % 2, :], ps[:, i % 2, :], ACT.Identity, scale=pmc("conv_w", 5 * j + 2, 5 * j + 3),
                          bias=pmc("conv_b", j, j + 1)).then_inc(conv_center, 1)
                    elif what == "E" and i < U_Z:
                        m = i - U_K
                        act.wait_ge(unit_used, L * UNITS + i + 1)
                        dst = zt[:] if i == U_V else qk[:, 4 if i == U_K else i - U_Q, :]
                        A(dst, ps[:, i % 2, :], ACT.Copy).then_inc(proj_copied, 1)
                    elif what == "E":
                        c = i - U_Z
                        act.wait_ge(unit_used, L * UNITS + i + 1)
                        if c >= 1:
                            act.wait_ge(zs_done, L * CT + c)
                        A(zt[:], ps[:, i % 2, :], ACT.Tanh, scale=0.5).then_inc(tanh_done, 1)
                    elif what == "SILU":
                        act.wait_ge(conv_taps, L * 4 * N_CONV + 4 * i + 4)
                        if i == 0:
                            act.wait_ge(rope_done, L * 5 + 5)
                        if i >= 6:
                            wait_aux_full(act, L, ("T", i - 2))
                        dst = bc[:, i, :] if i < 4 else xsc[:, i % 2, :]
                        A(dst, cv[:, i % 2, :], ACT.Tanh, scale=0.5).then_inc(conv_tanh, 1)
                    elif what == "SP":
                        act.wait_ge(dt_abs, L + 1)
                        A(sp[:, 2, :], sp[:, 1, :], ACT.Exp, scale=-1.0).then_inc(dt_exp, 1)
                        A(neg_a[:], pmc("a_log"), ACT.Exp).then_inc(dt_exp, 1)
                    elif what == "SM":
                        wait_aux_full(act, L, ("SM", 0))
                        A(dec[:].rearrange("p t d h -> p (t d h)"), ps[:, aux_bank(("SM", 0)), 0:128],
                          ACT.Exp).then_inc(dec_done, 1)
                    elif what == "T":
                        wait_aux_full(act, L, ("T", i))
                        dst = b_tm[:, :, i * P:(i + 1) * P] if i < 2 else xs_tm[:, :, (i - 4) * P:(i - 3) * P]
                        A(dst, ps[:, aux_bank(("T", i)), :].rearrange("p (t c) -> p t c", c=P),
                          ACT.Copy, scale=0.5).then_inc(t_evac, 1)
                    elif what == "VT":
                        wait_aux_full(act, L, ("VT", 0))
                        A(v_tm[:], ps[:, aux_bank(("VT", 0)), :].rearrange("p (t c) -> p t c", c=P),
                          ACT.Copy).then_inc(v_done, 1)
                    elif what == "ST":
                        t = i % NBLK
                        wait_aux_full(act, L, ("ST", i))
                        if i >= NBLK:
                            wait_y_full(act, L, ("YO", (i - NBLK) ^ 1))
                        A(st[:, t, :], ps[:, aux_bank(("ST", i)), :], ACT.Copy).then_inc(st_done, 1)
                    elif what == "SE":
                        act.wait_ge(seg_full, L * 16 + i + 1)
                        if i >= 3:
                            act.wait_ge(seg_used, L * 16 + i - 2)
                        A(seg_e[i % 3][:].rearrange("p h q -> p (h q)"),
                          ps[:, 2:4, :].rearrange("p b n -> p (b n)"), ACT.Exp).then_inc(exp_done, 1)
                    elif what == "AX":
                        act.wait_ge(as_max, L * 8 + i + 1)
                        if i >= 2:
                            wait_y_full(act, L, ("AP", i - 2, 1))
                        for j in range(QPK):
                            A(sc[i % 2][:, j, :], ps[:, 2 + j // 2, (j % 2) * SEQ:(j % 2 + 1) * SEQ], ACT.Exp, scale=SCALE,
                              bias=ast[:, i % 2, 1, j:j + 1], accum_out=ast[:, i % 2, 3, j:j + 1])
                        A(ast[:, i % 2, 4, :], ast[:, i % 2, 2, :], ACT.Exp).then_inc(as_exp, 1)
                    elif what == "AP":
                        wait_y_full(act, L, ("AP", i, 0))
                        if i >= 2:
                            wait_aux_full(act, L, ("AV", i - 2))
                        A(p_t[i % 2][:, 0, :], ps[:, y_bank(("AP", i, 0)), :], ACT.Copy).then_inc(pt0_done, 1)
                    elif what == "AV":
                        t, g = ATTN[i]
                        rows = slice(g * HEAD, (g + 1) * HEAD)
                        wait_aux_full(act, L, ("AV", i))
                        A(ahi[rows, 0:QPK, t * BLK:(t + 1) * BLK],
                          ps[rows, aux_bank(("AV", i)), :].rearrange("p (j q) -> p j q", q=BLK),
                          ACT.Copy).then_inc(ah_done, 1)
                    elif what == "RS":
                        act.wait_ge(gated, L * 8 + (4 if i < 4 else 8))
                        if i >= 2:
                            act.wait_ge(rms_mm, L * CT + i - 1)
                        A(sqr[:, i % 2, :], zs[:, i, :], ACT.Square).then_inc(rms_sq, 1)
                    elif what == "RMS":
                        act.wait_ge(rms_mm, L * CT + CT)
                        A(std[:], ps[:, aux_bank(("RS", 0)), :], ACT.Sqrt, bias=cst("eps")).then_inc(rms_std, 1)
                    elif what == "RN":
                        act.wait_ge(ssd_normed, L * CT + i + 1)
                        A(ahi[:, QPK + i, :], zs[:, i, :], ACT.Copy).then_inc(sh_done, 1)

                split_next(L, U_UP - 1)
                act.wait_ge(pf_loaded, L * 16 + 16)
                a1, b1 = PF["ln1_b"]
                layer_norm(L * 2 + 1, L, None, pf[:, a1:b1])

                def glu(I, p):
                    n, bank = U_UP + 2 * p, 2 * (p % RING)
                    off = I * 2 * RING
                    act.wait_ge(unit_used, L * UNITS + off + (n + 1))
                    k = (I * RING + p)
                    w0, _ = PF["conv_w"]
                    v0, _ = PF["conv_b"]
                    A(gcv[:], ps[:, bank, :], ACT.Identity, scale=pf[:, bass.ds(k * 3 + (w0 + 1), 1)],
                      bias=pf[:, bass.ds(k + v0, 1)]).then_inc(glu_center, 1)
                    split_next(L, n, I * 2)
                    act.wait_ge(glu_taps, (L * FT + k + 1) * 2)
                    act.wait_ge(glu_done, L * FT + k + RING)
                    A(gsg[:], gcv[:], ACT.Silu).then_inc(glu_silu, 1)
                    split_next(L, n + 1, I * 2)
                    act.wait_ge(glu_done, L * FT + k + RING + 1)
                    A(uhi[:, bass.ds(k, 1), :].rearrange("p a n -> p (a n)"), guf[:], ACT.Copy).then_inc(glu_hi, 1)

                glu(0, 0)
                with act.Fori(0, FT // RING) as I:
                    for p in range(RING):
                        glu(I, p + 1)
                with act.Fori(0, FT // RING) as I:
                    for j in range(RING):
                        split_next(L, U_DOWN + j, I)
                split_next(L, UNITS - 1)
                a2, b2 = PF["ln2_b"]
                layer_norm(L * 2 + 2, L, None, pf[:, a2:b2])

        @block.tensor
        def _(pe):
            mm = nc.tensor.matmul

            def three(out, slot, cols, xhi, xlo, start, stop):
                mm(out, whi[:, slot, cols], xhi, start=start, stop=False)
                mm(out, whi[:, slot, cols], xlo, start=False, stop=False)
                return mm(out, wlo[:, slot, cols], xhi, start=False, stop=stop)

            def by_columns(slot, bank):
                for c in range(CT):
                    last = three(ps[:, bank, :], slot, slice(c * P, (c + 1) * P), hhi[:, c, :], hlo[:, c, :],
                                 c == 0, c == CT - 1)
                last.then_inc(unit_used, 1)

            def first_units(norm):
                for c in range(CT):
                    pe.wait_ge(h_ready, norm * CT + c + 1)
                    for k in range(2):
                        last = three(ps[:, k, :], k, slice(c * P, (c + 1) * P), hhi[:, c, :], hlo[:, c, :],
                                     c == 0, c == CT - 1)
                        if c == CT - 1:
                            last.then_inc(unit_used, 1)

            def by_rows(slot, xhi, xlo, start=False, residuals=None, before=None, banks=range(CT)):
                stop = residuals is not None
                for n, c in enumerate(ACC_ORDER if stop else banks):
                    if before and c in before:
                        pe.wait_ge(*before[c])
                    last = three(ps[:, c, :], slot, slice(c * P, (c + 1) * P), xhi, xlo, start, stop)
                    if stop and n < CT - 1:
                        last.then_inc(acc_done, 1)
                    elif n == CT - 1 or (start and c == CT - 1):
                        last.then_inc(unit_used, 1)
                    if stop and n >= LAG:
                        mean(n - LAG, residuals)
                if stop:
                    for n in range(CT - LAG, CT):
                        mean(n, residuals)

            def mean(n, res_count):
                if res_count is not None:
                    pe.wait_ge(res_done, res_count + n + 1)
                last = mm(ps[:, 4, :], cst("avg"), h[:, ACC_ORDER[n], :], start=(n == 0), stop=(n == CT - 1))
                if n == CT - 1:
                    last.then_inc(ln_mean, 1)

            def squares(idx):
                for c in range(CT):
                    pe.wait_ge(ln_sq, idx * CT + c + 1)
                    mm(ps[:, 5, :], cst("avg"), sq[:, c % 2, :], start=(c == 0), stop=(c == CT - 1)).then_inc(ln_sqmm, 1)

            pe.wait_ge(cn_loaded, 16)
            pe.wait_ge(x_loaded, 16)
            for n in range(CT):
                mean(n, None)
            squares(0)
            with pe.Fori(0, DEPTH) as L:
                for what, i in SCHED:
                    if what == "G" and i == 0:
                        pe.wait_ge(unit_split, L * UNITS + 2)
                        first_units(L * 2)
                    elif what == "G" and i == 1:
                        pass
                    elif what == "G" and i < U_OUT:
                        if i == 2:
                            pe.wait_ge(dt_copied, L + 1)
                        elif U_CONV <= i - 2 < U_Z:
                            pe.wait_ge(conv_taps, L * 4 * N_CONV + 4 * (i - 2 - U_CONV) + 4)
                        elif U_K <= i - 2 < U_CONV:
                            pe.wait_ge(proj_copied, L * 6 + i - 2 - U_K + 1)
                        elif i - 2 >= U_Z:
                            pe.wait_ge(zs_done, L * CT + i - 2 - U_Z + 1)
                        pe.wait_ge(unit_split, L * UNITS + i + 1)
                        by_columns(i % RING, i % 2)
                    elif what == "G":
                        k = i - U_OUT
                        pe.wait_ge(unit_split, L * UNITS + i + 1)
                        before = None
                        if k == 0:
                            pe.wait_ge(gated, L * 8 + 8)
                            pe.wait_ge(st_done, L * 8 + 8)
                            before = {aux_bank(("RS", 0)): (rms_std, L + 1)}
                        if k >= QPK:
                            pe.wait_ge(sl_done, L * CT + k - QPK + 1)
                        by_rows(i % RING, ahi[:, k, :], alo[:, k, :], k == 0, L * 2 * CT if k == N_OUT - 1 else None, before,
                                range(4, CT) if k == 0 else range(CT))
                    elif what == "GA":
                        pe.wait_ge(unit_split, L * UNITS + i + 1)
                        pe.wait_ge(zs_done, L * CT + CT)
                        pe.wait_ge(exp_done, L * 16 + 16)
                        pe.wait_ge(al_done, L * 8 + 8)
                        by_rows(i % RING, ahi[:, 0, :], alo[:, 0, :], True, banks=range(4))
                    elif what == "DTT":
                        pe.wait_ge(dt_copied, L + 1)
                        for t in range(NBLK):
                            last = mm(ps[:, aux_bank((what, i)), t * 32:(t + 1) * 32],
                                      zt[0:32, t * BLK:(t + 1) * BLK], ident[0:32, 0:32], start=True, stop=True)
                        last.then_inc(aux_full, 1)
                    elif what == "SM":
                        pe.wait_ge(la_done, L + 1)
                        wait_aux_free(pe, L, (what, i))
                        for t in range(NBLK):
                            for d, w in enumerate(("after", "lower") if t % 2 == 0 else ("upper", "before")):
                                at0 = (2 * t + d) * SSD_HEADS
                                last = mm(ps[:, aux_bank((what, i)), at0:at0 + SSD_HEADS], cst(w),
                                          la[:, t, d * SSD_HEADS:(d + 1) * SSD_HEADS], start=True, stop=True)
                        last.then_inc(aux_full, 1)
                    elif what == "T":
                        pe.wait_ge(silu_done, L * N_CONV + i + 1)
                        wait_aux_free(pe, L, (what, i))
                        src = bc[:, i, :] if i < 4 else xsc[:, i % 2, :]
                        for t in range(NBLK):
                            last = nc.tensor.transpose(ps[:, aux_bank((what, i)), t * BLK:(t + 1) * BLK],
                                                       src[:, t * BLK:(t + 1) * BLK], ident)
                        last.then_inc(aux_full, 1)
                    elif what == "CB":
                        pe.wait_ge(silu_done, L * N_CONV + 4)
                        wait_aux_free(pe, L, (what, i))
                        for n in range(4):
                            t, g = 2 * i + n // 2, n % 2
                            last = mm(ps[:, aux_bank((what, i)), n * P:(n + 1) * P], bc[:, g, t * BLK:(t + 1) * BLK],
                                      bc[:, 2 + g, t * BLK:(t + 1) * BLK], start=True, stop=True)
                        last.then_inc(aux_full, 1)
                    elif what == "VT":
                        pe.wait_ge(proj_copied, L * 6 + 2)
                        wait_aux_free(pe, L, (what, i))
                        for t in range(NBLK):
                            last = nc.tensor.transpose(ps[:, aux_bank((what, i)), t * BLK:(t + 1) * BLK],
                                                       zt[:, t * BLK:(t + 1) * BLK], ident)
                        last.then_inc(aux_full, 1)
                    elif what == "ROT":
                        pe.wait_ge(proj_copied, L * 6 + (1 if i == 4 else 3 + i))
                        wait_aux_free(pe, L, (what, i))
                        mm(ps[:, aux_bank((what, i)), :], cst("rot"), qk[:, i, :], start=True,
                           stop=True).then_inc(aux_full, 1)
                    elif what == "ST":
                        g, t = divmod(i, NBLK)
                        pe.wait_ge(xw_done, L * 8 + i + 1)
                        wait_aux_free(pe, L, (what, i))
                        mm(ps[:, aux_bank((what, i)), :], b_tm[:, t, g * STATE:(g + 1) * STATE],
                           xw[:, t, :], start=True, stop=True).then_inc(aux_full, 1)
                    elif what == "YO":
                        g, t = divmod(i, NBLK)
                        pe.wait_ge(st_done, L * 8 + (i ^ 1) + 1)
                        wait_y_free(pe, L, (what, i))
                        mm(ps[:, y_bank((what, i)), :], bc[:, 2 + g, t * BLK:(t + 1) * BLK],
                           st[:, t ^ 1, :], start=True, stop=True).then_inc(y_full, 1)
                    elif what == "SB":
                        t, g, d = SEGS[i]
                        pe.wait_ge(r_done, L * 16 + i + 1)
                        if i >= 1:
                            pe.wait_ge(exp_done, L * 16 + i)
                        else:
                            pe.wait_ge(as_exp, L * 8 + 8)
                        for n in range(2):
                            last = mm(ps[:, 2 + n, :], cst("after" if d == 0 else "before"),
                                      seg_r[i % 2][:, 4 * n:4 * n + 4, :].rearrange("p h q -> p (h q)"), start=True, stop=True)
                        last.then_inc(seg_full, 1)
                    elif what == "SD":
                        t, g, d = SEGS[i]
                        m = i // 2
                        pe.wait_ge(xd_done, L * 16 + 2 * m + 2)
                        pe.wait_ge(w_done, L * 16 + i + 1)
                        if d == 0:
                            wait_y_free(pe, L, ("SD", m))
                        bank = y_bank(("SD", m))
                        for n in range(HPG):
                            last = mm(ps[:, bank, n * HEAD:(n + 1) * HEAD], seg_e[i % 3][:, n, :],
                                      xd[:, m % 2, d, n * HEAD:(n + 1) * HEAD], start=(d == 0 and n == 0), stop=(d == 1),
                                      skip_group_check=True)
                        last.then_inc(seg_used, 1)
                    elif what == "YT":
                        g, t = divmod(i, NBLK)
                        pe.wait_ge(ya_done, L * 8 + i + 1)
                        if i < NBLK:
                            wait_aux_free(pe, L, (what, i))
                        else:
                            wait_y_free(pe, L, (what, i))
                        bank = (aux_bank if i < NBLK else y_bank)((what, i))
                        for n in range(4):
                            c = 4 * g + n
                            last = nc.tensor.transpose(ps[:, bank, n * BLK:(n + 1) * BLK],
                                                       xs_tm[:, t, c * P:(c + 1) * P], ident)
                        last.then_inc(aux_full if i < NBLK else y_full, 1)
                    elif what == "AS":
                        t, g = ATTN[i]
                        rows = slice(g * HEAD, (g + 1) * HEAD)
                        if i == 0:
                            pe.wait_ge(rope_done, L * 5 + 5)
                            pe.wait_ge(as_const, 3)
                        else:
                            pe.wait_ge(as_exp, L * 8 + i)
                        o = 1 - t % 2
                        for m in range(2):
                            mm(ps[:, 2 + m, :].rearrange("p (j k) -> p j k", k=SEQ)[:, :, o * P:(o + 1) * P], big_i[:],
                               cut[:, t % 2, :].unsqueeze(1).broadcast_to((P, 2, P)), start=True, stop=False,
                               skip_group_check=True)
                            for n in range(2):
                                last = mm(ps[:, 2 + m, n * SEQ:(n + 1) * SEQ],
                                          qk[rows, 2 * m + n, t * BLK:(t + 1) * BLK],
                                          qk[rows, 4, (t // 2) * SEQ:(t // 2 + 1) * SEQ], start=False, stop=True,
                                          skip_group_check=True)
                        last.then_inc(as_full, 1)
                    elif what == "AP":
                        pe.wait_ge(as_norm, L * 8 + i + 1)
                        for kt in range(2):
                            wait_y_free(pe, L, (what, i, kt))
                            for j in range(QPK):
                                last = nc.tensor.transpose(ps[:, y_bank((what, i, kt)), j * BLK:(j + 1) * BLK],
                                                           sc[i % 2][:, j, kt * P:(kt + 1) * P], ident)
                            last.then_inc(y_full, 1)
                    elif what == "AV":
                        t, g = ATTN[i]
                        pe.wait_ge(v_done, L + 1)
                        pe.wait_ge(pt0_done, L * 8 + i + 1)
                        pe.wait_ge(pt1_done, L * 8 + i + 1)
                        wait_aux_free(pe, L, (what, i))
                        for kt in range(2):
                            last = mm(ps[g * HEAD:(g + 1) * HEAD, aux_bank((what, i)), :],
                                      v_tm[:, (t // 2) * 2 + kt, g * HEAD:(g + 1) * HEAD], p_t[i % 2][:, kt, :],
                                      start=(kt == 0), stop=(kt == 1))
                        last.then_inc(aux_full, 1)
                    elif what == "RS":
                        pe.wait_ge(rms_sq, L * CT + i + 1)
                        if i == 0:
                            wait_aux_free(pe, L, (what, i))
                        mm(ps[:, aux_bank(("RS", 0)), :], cst("avg"), sqr[:, i % 2, :], start=(i == 0),
                           stop=(i == CT - 1)).then_inc(rms_mm, 1)

                squares(L * 2 + 1)

                pe.wait_ge(unit_split, L * UNITS + U_UP + 2)
                first_units(L * 2 + 1)

                def glu(I, p):
                    k = I * RING + p
                    pe.wait_ge(glu_done, L * FT + k + 1)
                    for half in range(2):
                        n = U_UP + 2 * p + half
                        pe.wait_ge(unit_split, L * UNITS + I * 2 * RING + (n + 1))
                        by_columns(n % RING, 2 * (p % RING) + half)

                with pe.Fori(0, FT // RING) as I:
                    for p in range(RING):
                        glu(I, p + 1)

                def down(k, n, start=False, residuals=None):
                    pe.wait_ge(unit_split, L * UNITS + k + (U_DOWN + 1))
                    pe.wait_ge(glu_ready, L * FT + k + 1)
                    if start:
                        pe.wait_ge(glu_done, L * FT + FT + RING)
                    if isinstance(k, int):
                        xhi, xlo = uhi[:, k, :], ulo[:, k, :]
                    else:
                        xhi = uhi[:, bass.ds(k, 1), :].rearrange("p a n -> p (a n)")
                        xlo = ulo[:, bass.ds(k, 1), :].rearrange("p a n -> p (a n)")
                    by_rows((U_DOWN + n) % RING, xhi, xlo, start, residuals)

                down(0, 0, start=True)
                with pe.Fori(0, (FT - 4) // RING) as I:
                    for j in range(RING):
                        down(I * RING + (1 + j), 1 + j)
                for k in range(FT - 3, FT):
                    down(k, k, residuals=L * 2 * CT + CT if k == FT - 1 else None)
                squares(L * 2 + 2)

        @block.vector
        def _(dve):
            V = nc.vector

            def split_lo(slot, count):
                dve.wait_ge(unit_hi, count)
                V.tensor_tensor(wlo[:, slot, :], raw[:, slot, :], f(whi[:, slot, :]), ALU.subtract).then_inc(unit_split, 1)

            def split_next(L, n, more=0):
                split_lo(n % RING, L * UNITS + (n + RING + 1) + more * RING)

            def residual(L, first, acc, rebuilt):
                for n, c in enumerate(ACC_ORDER):
                    if n < CT - 1:
                        dve.wait_ge(acc_done, acc + n + 1)
                    else:
                        dve.wait_ge(unit_used, first)
                    dve.wait_ge(rebuilt, L * CT + c + 1)
                    V.scalar_tensor_tensor(out=h[:, c, :], in0=h[:, c, :], scalar=ALPHA, in1=ps[:, c, :],
                                           op0=ALU.mult, op1=ALU.add).then_inc(res_done, 1)

            def low(idx, c, bet):
                dve.wait_ge(ln_hi, idx * CT + c + 1)
                V.scalar_tensor_tensor(out=hlo[:, c, :], in0=h[:, c, :], scalar=bet[:, c:c + 1],
                                       in1=f(hhi[:, c, :]), op0=ALU.add, op1=ALU.subtract).then_inc(h_ready, 1)

            def layer_norm(idx, gam, bet):
                dve.wait_ge(ln_mean, idx + 1)
                for c in range(CT):
                    V.tensor_tensor(h[:, c, :], h[:, c, :], ps[:, 4, :], ALU.subtract).then_inc(ln_cent, 1)
                dve.wait_ge(ln_std, idx + 1)
                V.reciprocal(std[:], std[:]).then_inc(ln_rstd, 1)
                dve.wait_ge(ln_rstd, idx + 1)
                for c in range(CT):
                    V.scalar_tensor_tensor(out=h[:, c, :], in0=h[:, c, :], scalar=gam[:, c:c + 1], in1=std[:],
                                           op0=ALU.mult, op1=ALU.mult).then_inc(ln_scaled, 1)
                    if c >= 1:
                        low(idx, c - 1, bet)
                low(idx, CT - 1, bet)

            dve.sem_inc(glu_done, RING)
            dve.wait_ge(cn_loaded, 16)
            for j in range(RING):
                split_lo(j, j + 1)
            dve.wait_ge(x_loaded, 16)
            layer_norm(0, cst("ln_g"), cst("ln_b"))

            with dve.Fori(0, DEPTH) as L:
                count = [0]

                def chain(ins):
                    count[0] += 1
                    ins.then_inc(link, 1)
                    dve.wait_ge(link, L * LINKS + count[0])

                dve.wait_ge(pm_loaded, L * 16 + 16)
                for what, i in SCHED:
                    if what == "S":
                        split_next(L, i - RING)
                    elif what == "F" and U_CONV <= i < U_Z:
                        j = i - U_CONV
                        dve.wait_ge(conv_center, L * N_CONV + j + 1)
                        dst = cv[:, j % 2, :].rearrange("p (b s) -> p b s", b=NSEQ)
                        src = ps[:, i % 2, :].rearrange("p (b s) -> p b s", b=NSEQ)
                        for n, tap in enumerate((0, 1, 3, 4)):
                            s = tap - 2
                            lo, hi = max(0, -s), SEQ - max(0, s)
                            if n:
                                dve.wait_ge(conv_taps, L * 4 * N_CONV + 4 * j + n)
                            V.scalar_tensor_tensor(out=dst[:, :, lo:hi], in0=src[:, :, lo + s:hi + s],
                                                   scalar=pmc("conv_w", 5 * j + tap, 5 * j + tap + 1),
                                                   in1=dst[:, :, lo:hi], op0=ALU.mult, op1=ALU.add).then_inc(conv_taps, 1)
                    elif what == "SILU":
                        dve.wait_ge(conv_tanh, L * N_CONV + i + 1)
                        x = bc[:, i, :] if i < 4 else xsc[:, i % 2, :]
                        V.scalar_tensor_tensor(out=x, in0=x, scalar=1.0, in1=cv[:, i % 2, :],
                                               op0=ALU.add, op1=ALU.mult).then_inc(silu_done, 1)
                    elif what == "F" and i >= U_Z:
                        c = i - U_Z
                        if c == 0:
                            wait_aux_full(dve, L, ("AV", 7))
                        if c == 4:
                            wait_aux_full(dve, L, ("T", N_CONV - 1))
                        dve.wait_ge(tanh_done, L * CT + c + 1)
                        V.scalar_tensor_tensor(out=zs[:, c, :], in0=zt[:], scalar=1.0, in1=ps[:, i % 2, :],
                                               op0=ALU.add, op1=ALU.mult).then_inc(zs_done, 1)
                    elif what == "SP":
                        X, AB, E_, DEN, U1, U2, PL, MX = (sp[:, n, :] for n in range(8))
                        wait_aux_full(dve, L, ("DTT", 0))
                        bias = pmc("dt_bias").unsqueeze(1).broadcast_to((P, NBLK, 32))
                        V.tensor_tensor(X.rearrange("p (t c) -> p t c", c=32),
                                        ps[:, aux_bank(("DTT", 0)), 0:128].rearrange("p (t c) -> p t c", c=32),
                                        bias, ALU.add).then_inc(dtx_done, 1)
                        dve.wait_ge(dtx_done, L + 1)
                        V.scalar_tensor_tensor(out=AB, in0=X, scalar=-1.0, in1=X, op0=ALU.mult, op1=ALU.max).then_inc(dt_abs, 1)
                        dve.wait_ge(dt_exp, L * 2 + 2)
                        chain(V.tensor_scalar(DEN, E_, 2.0, None, ALU.add))
                        chain(V.reciprocal(DEN, DEN))
                        chain(V.tensor_tensor(U1, E_, DEN, ALU.mult))
                        chain(V.tensor_tensor(U2, U1, U1, ALU.mult))
                        chain(V.tensor_scalar(PL, U2, 1.0 / 15, None, ALU.mult))
                        for n in range(6, 0, -1):
                            chain(V.scalar_tensor_tensor(out=PL, in0=PL, scalar=1.0 / (2 * n + 1), in1=U2,
                                                         op0=ALU.add, op1=ALU.mult))
                        chain(V.scalar_tensor_tensor(out=PL, in0=PL, scalar=1.0, in1=U1, op0=ALU.add, op1=ALU.mult))
                        chain(V.tensor_scalar(MX, X, 0.0, None, ALU.max))
                        chain(V.scalar_tensor_tensor(out=dt[:].rearrange("p t c -> p (t c)"), in0=PL, scalar=2.0,
                                                     in1=MX, op0=ALU.mult, op1=ALU.add))
                        V.scalar_tensor_tensor(out=la[:], in0=dt[:], scalar=-1.0,
                                               in1=neg_a[:].unsqueeze(1).broadcast_to((P, NBLK, 32)),
                                               op0=ALU.mult, op1=ALU.mult).then_inc(la_done, 1)
                    elif what == "SM":
                        dve.wait_ge(dec_done, L + 1)
                        V.tensor_tensor(dd[:].rearrange("p t d h -> p (t d h)"), dt[:].rearrange("p t c -> p (t c)"),
                                        dec[:].rearrange("p t d h -> p (t d h)"), ALU.mult).then_inc(dd_done, 1)
                    elif what == "CB":
                        wait_aux_full(dve, L, (what, i))
                        src = ps[:, aux_bank((what, i)), :].rearrange("p (n q) -> p n q", q=P)
                        for d, m in enumerate(("upper", "lower")):
                            V.scalar_tensor_tensor(out=cb[:, d, 4 * i:4 * i + 4, :], in0=src, scalar=0.25,
                                                   in1=cst(m).unsqueeze(1).broadcast_to((P, 4, P)),
                                                   op0=ALU.mult, op1=ALU.mult).then_inc(cb_done, 1)
                    elif what == "ROT":
                        wait_aux_full(dve, L, (what, i))
                        n = (i + 1) % 5
                        tt = ropet[:].rearrange("p (b s) -> p b s", b=NSEQ)
                        x = qk[:, i, :].rearrange("p (b s) -> p b s", b=NSEQ)
                        r = ps[:, aux_bank((what, i)), :].rearrange("p (b s) -> p b s", b=NSEQ)
                        if n:
                            dve.wait_ge(rope_done, L * 5 + n)
                        V.tensor_tensor(tt, r, cst("sin").unsqueeze(1).broadcast_to((P, NSEQ, SEQ)), ALU.mult).then_inc(rope_sin, 1)
                        chain(V.tensor_tensor(x, x, cst("cos").unsqueeze(1).broadcast_to((P, NSEQ, SEQ)), ALU.mult))
                        dve.wait_ge(rope_sin, L * 5 + n + 1)
                        V.tensor_tensor(qk[:, i, :], qk[:, i, :], ropet[:], ALU.add).then_inc(rope_done, 1)
                    elif what == "SA":
                        t, g, d = SEGS[i]
                        if i == 1:
                            wait_aux_full(dve, L, ("AV", 7))
                        if i >= 2:
                            dve.wait_ge(seg_full, L * 16 + i - 1)
                        a0 = d * SSD_HEADS + g * HPG
                        V.tensor_tensor(seg_r[i % 2][:], cst("upper" if d == 0 else "lower").unsqueeze(1).broadcast_to((P, HPG, P)),
                                        la[:, t, a0:a0 + HPG].unsqueeze(2).broadcast_to((P, HPG, P)),
                                        ALU.mult).then_inc(r_done, 1)
                    elif what == "SC":
                        t, g, d = SEGS[i]
                        dve.wait_ge(exp_done, L * 16 + i + 1)
                        if i == 0:
                            dve.wait_ge(cb_done, L * 4 + 4)
                        V.tensor_tensor(seg_e[i % 3][:], seg_e[i % 3][:],
                                        cb[:, d, 2 * t + g, :].unsqueeze(1).broadcast_to((P, HPG, P)),
                                        ALU.mult).then_inc(w_done, 1)
                    elif what == "YO":
                        g, t = divmod(i, NBLK)
                        wait_y_full(dve, L, (what, i))
                        V.scalar_tensor_tensor(out=yo[:].rearrange("p (h c) -> p h c", c=HEAD),
                                               in0=ps[:, y_bank((what, i)), :].rearrange("p (h c) -> p h c", c=HEAD), scalar=0.5,
                                               in1=dec[:, t, 1 - t % 2, g * HPG:(g + 1) * HPG].unsqueeze(2).broadcast_to((P, HPG, HEAD)),
                                               op0=ALU.mult, op1=ALU.mult).then_inc(yo_done, 1)
                        dve.wait_ge(yo_done, L * 8 + i + 1)
                        dve.wait_ge(yd_done, L * 8 + i + 1)
                        y = xs_tm[:, t, g * 512:(g + 1) * 512]
                        chain(V.tensor_tensor(y, y, yo[:], ALU.add))
                    elif what == "YA":
                        g, t = divmod(i, NBLK)
                        dve.wait_ge(seg_used, L * 16 + 2 * i + 2)
                        y = xs_tm[:, t, g * 512:(g + 1) * 512]
                        V.tensor_tensor(y, y, ps[:, y_bank(("SD", i)), :], ALU.add).then_inc(ya_done, 1)
                    elif what == "YT":
                        g, t = divmod(i, NBLK)
                        (wait_aux_full if i < NBLK else wait_y_full)(dve, L, (what, i))
                        dve.wait_ge(zs_done, L * CT + 4 * g + 4)
                        bank = (aux_bank if i < NBLK else y_bank)((what, i))
                        z = zs[:, 4 * g:4 * g + 4, t * BLK:(t + 1) * BLK]
                        V.scalar_tensor_tensor(out=z, in0=ps[:, bank, :].rearrange("p (n q) -> p n q", q=BLK),
                                               scalar=0.5, in1=z, op0=ALU.mult, op1=ALU.mult).then_inc(gated, 1)
                    elif what == "AM":
                        t, g = ATTN[i]
                        dve.wait_ge(as_full, L * 8 + i + 1)
                        sink = pmc("sink", g * QPK, (g + 1) * QPK)
                        top, minus, sink_in = (ast[:, i % 2, n, :] for n in range(3))
                        chain(V.tensor_reduce(top, ps[:, 2:4, :].rearrange("p b (j k) -> p (b j) k", k=SEQ), AX_X, ALU.max))
                        chain(V.scalar_tensor_tensor(out=top, in0=top, scalar=SCALE, in1=sink, op0=ALU.mult, op1=ALU.max))
                        chain(V.tensor_scalar(minus, top, -1.0, None, ALU.mult))
                        V.tensor_tensor(sink_in, sink, top, ALU.subtract).then_inc(as_max, 1)
                    elif what == "AD":
                        dve.wait_ge(as_exp, L * 8 + i + 1)
                        if i >= 2:
                            dve.wait_ge(as_norm, L * 8 + i - 1)
                        den = ast[:, i % 2, 5, :]
                        chain(V.tensor_tensor(den, ast[:, i % 2, 3, :], ast[:, i % 2, 4, :], ALU.add))
                        V.reciprocal(den, den).then_inc(as_den, 1)
                    elif what == "AP":
                        wait_y_full(dve, L, (what, i, 1))
                        if i >= 2:
                            wait_aux_full(dve, L, ("AV", i - 2))
                        V.tensor_copy(p_t[i % 2][:, 1, :], ps[:, y_bank((what, i, 1)), :]).then_inc(pt1_done, 1)
                    elif what == "AV":
                        t, g = ATTN[i]
                        rows = slice(g * HEAD, (g + 1) * HEAD)
                        dve.wait_ge(ah_done, L * 8 + i + 1)
                        V.tensor_tensor(alo[rows, 0:QPK, t * BLK:(t + 1) * BLK],
                                        ps[rows, aux_bank((what, i)), :].rearrange("p (j q) -> p j q", q=BLK),
                                        f(ahi[rows, 0:QPK, t * BLK:(t + 1) * BLK]), ALU.subtract).then_inc(al_done, 1)
                    elif what == "RMS":
                        dve.wait_ge(rms_std, L + 1)
                        chain(V.reciprocal(std[:], std[:]))
                        V.scalar_tensor_tensor(out=zs[:, 0, :], in0=zs[:, 0, :], scalar=pmc("norm_g", 0, 1), in1=std[:],
                                               op0=ALU.mult, op1=ALU.mult).then_inc(ssd_normed, 1)
                    elif what == "RN":
                        if i + 1 < CT:
                            V.scalar_tensor_tensor(out=zs[:, i + 1, :], in0=zs[:, i + 1, :],
                                                   scalar=pmc("norm_g", i + 1, i + 2), in1=std[:],
                                                   op0=ALU.mult, op1=ALU.mult).then_inc(ssd_normed, 1)
                        dve.wait_ge(sh_done, L * CT + i + 1)
                        V.tensor_tensor(alo[:, QPK + i, :], zs[:, i, :], f(ahi[:, QPK + i, :]), ALU.subtract).then_inc(sl_done, 1)

                assert count[0] == LINKS, count[0]
                residual(L, L * UNITS + U_UP, L * 14, h_rebuilt)
                split_next(L, U_UP - 1)
                dve.wait_ge(pf_loaded, L * 16 + 16)
                (g0, g1), (b0, b1) = PF["ln1_g"], PF["ln1_b"]
                layer_norm(L * 2 + 1, pf[:, g0:g1], pf[:, b0:b1])

                def glu(I, p):
                    n, bank = U_UP + 2 * p, 2 * (p % RING)
                    k = I * RING + p
                    w0, _ = PF["conv_w"]
                    dst = gcv[:].rearrange("p (b s) -> p b s", b=NSEQ)
                    src = ps[:, bank, :].rearrange("p (b s) -> p b s", b=NSEQ)
                    dve.wait_ge(glu_center, L * FT + k + 1)
                    V.scalar_tensor_tensor(out=dst[:, :, 1:SEQ], in0=src[:, :, 0:SEQ - 1], scalar=pf[:, bass.ds(k * 3 + w0, 1)],
                                           in1=dst[:, :, 1:SEQ], op0=ALU.mult, op1=ALU.add).then_inc(glu_taps, 1)
                    dve.wait_ge(glu_taps, (L * FT + k) * 2 + 1)
                    V.scalar_tensor_tensor(out=dst[:, :, 0:SEQ - 1], in0=src[:, :, 1:SEQ], scalar=pf[:, bass.ds(k * 3 + (w0 + 2), 1)],
                                           in1=dst[:, :, 0:SEQ - 1], op0=ALU.mult, op1=ALU.add).then_inc(glu_taps, 1)
                    split_next(L, n, I * 2)
                    dve.wait_ge(unit_used, L * UNITS + I * 2 * RING + (n + 2))
                    dve.wait_ge(glu_silu, L * FT + k + 1)
                    V.tensor_tensor(guf[:], gsg[:], ps[:, bank + 1, :], ALU.mult).then_inc(glu_done, 1)
                    split_next(L, n + 1, I * 2)
                    dve.wait_ge(glu_hi, L * FT + k + 1)
                    V.tensor_tensor(ulo[:, bass.ds(k, 1), :].rearrange("p a n -> p (a n)"), guf[:],
                                    f(uhi[:, bass.ds(k, 1), :]).rearrange("p a n -> p (a n)"),
                                    ALU.subtract).then_inc(glu_ready, 1)

                glu(0, 0)
                with dve.Fori(0, FT // RING) as I:
                    for p in range(RING):
                        glu(I, p + 1)
                with dve.Fori(0, FT // RING) as I:
                    for j in range(RING):
                        split_next(L, U_DOWN + j, I)
                residual(L, L * UNITS + UNITS, L * 14 + 7, h_back)
                split_next(L, UNITS - 1)
                (g0, g1), (b0, b1) = PF["ln2_g"], PF["ln2_b"]
                layer_norm(L * 2 + 2, pf[:, g0:g1], pf[:, b0:b1])
            for c in range(CT):
                dve.wait_ge(h_ready, 2 * DEPTH * CT + c + 1)
                V.tensor_tensor(h[:, c, :], f(hhi[:, c, :]), f(hlo[:, c, :]), ALU.add).then_inc(y_ready, 1)


def constants():
    k = np.arange(P)[:, None]
    q = np.arange(P)[None, :]
    rot = np.zeros((P, P), np.float32)
    for m in range(P):
        if m % HEAD < HEAD // 2:
            rot[m + HEAD // 2, m] = -1.0
        else:
            rot[m - HEAD // 2, m] = 1.0
    freq = np.float32(10000.0) ** (-np.arange(0, HEAD, 2, dtype=np.float32) / np.float32(HEAD))
    ang = np.arange(SEQ, dtype=np.float32)[None, :] * freq[np.arange(P) % (HEAD // 2)][:, None]
    return {
        "ident": np.eye(P), "avg": np.full((P, P), 1.0 / D_MODEL), "upper": q >= k, "lower": q <= k,
        "after": k > q, "before": k < q, "rot": rot, "cos": np.cos(ang), "sin": np.sin(ang),
        "eps": np.full((P, 1), EPS),
    }


def lay_out(x_prompt, x_sample, ln_in_g, ln_in_b, w_in, attn_sink, ssd_conv_w, ssd_conv_b, ssd_a_log,
            ssd_dt_bias, ssd_d, ssd_norm_g, w_out, ln1_g, ln1_b, w_up, ffn_conv_w, ffn_conv_b, w_down,
            ln2_g, ln2_b):
    def by_columns(w):
        n = w.shape[1] // P
        return w.reshape(CT, P, n, P).transpose(2, 1, 0, 3).reshape(n, P, D_MODEL)

    def channels(v):
        return v.reshape(-1, P).T

    def everywhere(v):
        return np.broadcast_to(v.reshape(1, -1), (P, v.size))

    x = np.concatenate([x_prompt.reshape(SEQ, D_MODEL), x_sample.reshape(SEQ, D_MODEL)])
    x_t = x.T.reshape(CT, P, TOK).transpose(1, 0, 2)
    aw, kw = 512, 128
    z0 = aw + 2 * kw
    xbc0 = z0 + SSD_WIDTH
    dt0 = xbc0 + SSD_WIDTH + 4 * STATE
    units, pms, pfs = [], [], []
    for i in range(DEPTH):
        w = w_in[i]
        dtw = np.zeros((D_MODEL, P), w.dtype)
        dtw[:, :32] = w[:, dt0:dt0 + 32]
        xbc = w[:, xbc0:dt0]
        q = w[:, :aw].reshape(D_MODEL, 2, QPK, HEAD).transpose(0, 2, 1, 3).reshape(D_MODEL, aw)
        units.append(by_columns(np.concatenate(
            [dtw, w[:, aw:z0], q, xbc[:, SSD_WIDTH:], xbc[:, :SSD_WIDTH], w[:, z0:xbc0]], axis=1)))
        wo = w_out[i]
        wa = wo[:aw].reshape(2, QPK, HEAD, D_MODEL).transpose(1, 0, 2, 3).reshape(QPK, P, D_MODEL)
        units += [wa, wo[aw:].reshape(CT, P, D_MODEL)]
        up = by_columns(w_up[i])
        units.append(np.stack([up[:FT], up[FT:]], axis=1).reshape(2 * FT, P, D_MODEL))
        units.append(w_down[i].reshape(FT, P, D_MODEL))
        cw = np.concatenate([ssd_conv_w[i][:, SSD_WIDTH:], ssd_conv_w[i][:, :SSD_WIDTH]], axis=1)
        cbias = np.concatenate([ssd_conv_b[i][SSD_WIDTH:], ssd_conv_b[i][:SSD_WIDTH]])
        pms.append(np.concatenate([
            cw.reshape(5, N_CONV, P).transpose(2, 1, 0).reshape(P, 5 * N_CONV), channels(cbias),
            channels(ssd_norm_g[i]), everywhere(attn_sink[i]), everywhere(ssd_a_log[i]),
            everywhere(ssd_dt_bias[i]), everywhere(ssd_d[i])], axis=1))
        pfs.append(np.concatenate([
            ffn_conv_w[i].reshape(3, FT, P).transpose(2, 1, 0).reshape(P, 3 * FT), channels(ffn_conv_b[i]),
            channels(ln1_g[i]), channels(ln1_b[i]), channels(ln2_g[i]), channels(ln2_b[i])], axis=1))
    cn = np.zeros((P, CN_W), x.dtype)
    for name, v in constants().items():
        cn[:, CN[name][0]:CN[name][1]] = v
    cn[:, CN["ln_g"][0]:CN["ln_g"][1]] = channels(ln_in_g)
    cn[:, CN["ln_b"][0]:CN["ln_b"][1]] = channels(ln_in_b)
    return {"x_t": x_t, "units": np.concatenate(units), "pm": np.stack(pms), "pf": np.stack(pfs), "cn": cn}


def kernel(**inputs):
    import concourse.bacc as _bacc
    from concourse.bass_utils import run_bass_kernel_spmd as _run

    nc = _bacc.Bacc("TRN2", target_bir_lowering=False, num_devices=1)
    arrays, args = {}, []
    for name, a in lay_out(**{k: np.asarray(v) for k, v in inputs.items()}).items():
        a = np.ascontiguousarray(a)
        arrays[f"in_{name}"] = a
        args.append(nc.dram_tensor(f"in_{name}", a.shape, mybir.dt.from_np(a.dtype), kind="ExternalInput").ap())
    y_t = nc.dram_tensor("out_y", (P, CT, TOK), F32, kind="ExternalOutput").ap()
    trunk(nc, *args, y_t)
    r = _run(nc, [arrays], core_ids=[0])
    y = np.asarray(r.results[0]["out_y"]).transpose(2, 1, 0).reshape(NSEQ, 1, SEQ, D_MODEL)
    return y[0], y[1]
```

```python
from contextlib import ExitStack

import numpy as np

import concourse.bass as bass
from concourse import mybir

F32 = mybir.dt.float32
F32R = mybir.dt.float32r
ALU = mybir.AluOpType
ACT = mybir.ActivationFunctionType
AX_X = mybir.AxisListType.X

P = 128
DEPTH, D_MODEL, SEQ, NSEQ = 2, 1024, 256, 2
TOK = NSEQ * SEQ
BLK = 128
NBLK = TOK // BLK
HEAD = 64
QPK = 4
SSD_HEADS, SSD_WIDTH, STATE = 16, 1024, 128
HPG = 8
D_FF = 2816
CT = D_MODEL // P
FT = D_FF // P
ALPHA = (2 * DEPTH) ** 0.25
EPS = 1e-5
MASK = -1e30
SCALE = HEAD ** -0.5

U_DT = 0
U_K, U_V, U_Q = 1, 2, 3
U_CONV = 7
N_CONV = 12
U_Z = U_CONV + N_CONV
U_OUT = 27
N_OUT = 12
U_UP = U_OUT + N_OUT
U_DOWN = U_UP + 2 * FT
UNITS = U_DOWN + FT
RING = 3
assert UNITS % RING == 0 and U_UP % RING == 0
TURNS = UNITS // RING

PM = {}
PF = {}


def _columns(table, widths):
    at = 0
    for name, w in widths:
        table[name] = (at, at + w)
        at += w
    return at


PM_W = _columns(PM, [("conv_w", N_CONV * 5), ("conv_b", N_CONV), ("norm_g", CT), ("sink", 8),
                     ("a_log", 32), ("dt_bias", 32), ("d", SSD_HEADS)])
PF_W = _columns(PF, [("conv_w", FT * 3), ("conv_b", FT), ("ln1_g", CT), ("ln1_b", CT),
                     ("ln2_g", CT), ("ln2_b", CT)])
CN = {}
CN_W = _columns(CN, [("ident", P), ("upper", P), ("lower", P), ("after", P),
                     ("before", P), ("rot", P), ("cos", SEQ), ("sin", SEQ), ("eps", 1),
                     ("ln_g", CT), ("ln_b", CT)])

SEGS = [(t, g, d) for g in range(2) for t in range(NBLK) for d in range(2)]
ATTN = [(t, g) for t in range(NBLK) for g in range(2)]
A0 = 8
SEG_SLOTS = {17: [0], 18: [1, 2], 19: [3], 20: [4, 5], 21: [6, 7], 22: [8, 9], 23: [10], 24: [11, 12],
             25: [13], 26: [14, 15]}
SEG_LAG = 2
STATES = {17: 1, 18: 0, 19: 3, 20: 2, 22: 5, 23: 4, 24: 7, 25: 6}


def seg_steps(k, ahead=True):
    out = []
    if k < len(SEGS):
        out += [("SB", k), ("SE", k)]
        if ahead and k + 1 < len(SEGS):
            out += [("SA", k + 1)]
    n = k - SEG_LAG
    weights = [("SC", k)] if k < len(SEGS) else []
    if n >= 0:
        m, d = divmod(n, 2)
        out += [("SD", n)]
        out += weights + [("YO", m)] if d == 0 else [("YA", m)] + weights
    else:
        out += weights
    if k % 2 and 2 <= (k + 1) // 2 < 8:
        out += [("XD", (k + 1) // 2), ("DS", (k + 1) // 2)]
    return out


def mixer_schedule():
    steps = []
    for n in range(U_OUT):
        i = n - A0
        segs = SEG_SLOTS.get(n, [])
        steps += [("G", n), ("E", n)]
        if len(segs) == 2:
            steps += [("SA", segs[0] + 1)]
        if 0 <= i < 8:
            steps += [("AS", i), ("AM", i)]
        if 0 <= i - 2 < 8:
            steps += [("AV", i - 2)]
        if n == 1:
            steps += [("DTT", 0), ("SP", 0)]
        if n == 3:
            steps += [("SM", 0)]
        if n - 1 == U_V:
            steps += [("VT", 0)]
        if n - 1 == U_K:
            steps += [("ROT", 4)]
        if U_Q <= n - 1 < U_Q + 4:
            steps += [("ROT", n - 1 - U_Q)]
        steps += [("S", n + RING)]
        if 0 <= i < 8:
            steps += [("AX", i)]
        steps += [("F", n)]
        if 0 <= i < 8:
            steps += [("AD", i), ("AN", i)]
        if U_CONV <= n < U_Z:
            steps += [("F2", n)]
        if 0 <= i - 1 < 8:
            steps += [("AP", i - 1)]
        j = n - 1 - U_CONV
        if j in (2, 3):
            steps += [("T", j - 2)]
        if 4 <= j < N_CONV:
            steps += [("T", j)]
        if j in (4, 6):
            steps += [("CB", j // 2 - 2)]
        if U_CONV <= n < 17:
            steps += [("SILU", n - U_CONV)]
        if n == 16:
            steps += [("SA", 0), ("XD", 0), ("XW", 1), ("XW", 0), ("DS", 0), ("XD", 1), ("DS", 1)]
        if n in (20, 21):
            m = 4 if n == 20 else 6
            steps += [("XW", m + 1), ("XW", m)]
        if n == 17:
            steps += [("SA", 1)]
        if n == 18:
            steps += [("XW", 3), ("XW", 2)]
        if n == 26:
            steps += [("YT", 4), ("YT", 5)]
        for k in segs:
            steps += seg_steps(k, k > 0 and (len(segs) == 1 or k == segs[1]))
            if k == segs[0] and n in STATES:
                steps += [("ST", STATES[n])]
            if k == segs[0] and 17 <= n < U_Z:
                steps += [("SILU", n - U_CONV)]
        if n == 24:
            steps += [("YT", 0), ("YT", 1)]
        if n == 25:
            steps += [("YT", 2), ("YT", 3)]
        if n == 26:
            steps += [("SQ", c) for c in range(4)]
    steps += [("GA", (U_OUT, (0, 1)))]
    steps += seg_steps(16)
    steps += [("GA", (U_OUT, (2, 3)))]
    steps += seg_steps(17)
    steps += [("GA", (U_OUT + 1, (0, 1))), ("YT", 6), ("YT", 7), ("GA", (U_OUT + 1, (2, 3)))]
    steps += [("SQ", c) for c in range(4, CT)] + [("RS", n) for n in (0, 2, 3, 1)]
    steps += [("RMS", 0)]
    for u in range(U_OUT, U_UP):
        steps.append(("G", u))
        if u - U_OUT >= 1:
            steps.append(("RN", u - U_OUT - 1)) if u - U_OUT - 1 < CT else None
        if u + 2 < U_UP:
            steps.append(("S", u + RING))
    return steps


SCHED = mixer_schedule()
LINKS = 14 + 5 + 8 + 4 * 8 + 1


def trunk(nc, x_t, units, pm_d, pf_d, cn_d, y_t):
    ctx = ExitStack()
    with ctx:
        def sb(name, shape, dt=F32):
            return ctx.enter_context(nc.sbuf_tensor(name, shape, dt))

        def sem(name):
            return ctx.enter_context(nc.semaphore(name))

        cn = sb("cn", [P, CN_W])
        avg = sb("avg", [P, P])
        avg_row = sb("avg_row", [P, NBLK, NBLK])
        pm = sb("pm", [P, PM_W])
        pf = sb("pf", [P, PF_W])
        raw = sb("raw", [P, RING, 1024])
        whi = sb("whi", [P, RING, 1024], F32R)
        wlo = sb("wlo", [P, RING, 1024], F32R)
        hhi = sb("hhi", [P, CT, TOK], F32R)
        hlo = sb("hlo", [P, CT, TOK], F32R)
        dt = sb("dt", [P, NBLK, 32])
        la = sb("la", [P, NBLK, 32])
        la_hi = sb("la_hi", [P, NBLK, 32], F32R)
        la_lo = sb("la_lo", [P, NBLK, 32], F32R)
        dec = sb("dec", [P, NBLK, 2, SSD_HEADS])
        dd = sb("dd", [P, NBLK, 2, SSD_HEADS])
        neg_a = sb("neg_a", [P, 32])
        ast = sb("ast", [P, 2, 6, QPK])
        big_i = sb("big_i", [P, P], F32R)
        cut = sb("cut", [P, 2, P], F32R)
        KB = 1024
        ARENA_KB = 110
        arena_h = sb("arena_h", [P, CT * TOK])
        arena = sb("arena", [P, ARENA_KB * KB // 4])
        base_h = nc.sbuf_base - ARENA_KB * KB - CT * TOK * 4
        base = nc.sbuf_base - ARENA_KB * KB

        def at(name, kb, shape, dtype=F32, start=None):
            return nc.alloc_sbuf_tensor_at(name, shape, dtype, offset=(base if start is None else start) + int(kb * KB))

        h = at("h", 0, [P, CT, TOK], start=base_h)
        zs = at("zs", 0, [P, CT, TOK], start=base_h)
        bc = at("bc", 0, [P, 4, TOK])
        ropet = at("ropet", 0, [P, TOK])
        yo = at("yo", 2, [P, 512])
        b_tm = at("b_tm", 8, [P, NBLK, 2 * STATE])
        st = at("st", 12, [P, NBLK, 512])
        qk = at("qk", 20, [P, 5, TOK])
        xw = at("xw", 20, [P, NBLK, 512])
        sqr = [at(f"sqr{n}", kb, [P, TOK]) for n, kb in enumerate((20, 22, 24, 26))]
        rms_sum = [at("rms_sum0", 28, [P, TOK]), at("rms_sum1", 30, [P, TOK])]
        v_tm = at("v_tm", 30, [P, NBLK, P])
        zt = at("zt", 32, [P, TOK])
        sc = [at("sc0", 34, [P, QPK, SEQ]), at("sc1", 0, [P, QPK, SEQ], start=base_h)]
        p_t = [at("p_t0", 38, [P, 2, 512]), at("p_t1", 4, [P, 2, 512], start=base_h)]
        cv = at("cv", 8, [P, 2, TOK], start=base_h)
        xsc = at("xsc", 12, [P, 2, TOK], start=base_h)
        ahi = at("ahi", 42, [P, N_OUT, TOK], F32R)
        alo = at("alo", 66, [P, N_OUT, TOK], F32R)
        xs_tm = at("xs_tm", 50, [P, NBLK, SSD_WIDTH])
        cb = at("cb", 74, [P, 2, 8, P])
        xd = at("xd", 82, [P, 2, 2, 512])
        seg_hi = [at("seg_hi0", 90, [P, HPG, P], F32R), at("seg_hi1", 38, [P, HPG, P], F32R)]
        seg_lo = [at("seg_lo0", 102, [P, HPG, P], F32R), at("seg_lo1", 106, [P, HPG, P], F32R)]
        sp = at("sp", 90, [P, 8, 128])
        seg_e = [at("seg_e0", 94, [P, HPG, P]), at("seg_e1", 98, [P, HPG, P]), at("seg_e2", 34, [P, HPG, P])]
        sq = at("sq", 0, [P, CT, TOK])
        pair = at("pair", 16, [P, 4, TOK])
        std = at("std", 98, [P, TOK])
        rstd = at("rstd", 100, [NBLK, BLK])
        uhi = at("uhi", 0, [P, FT, TOK], F32R)
        ulo = at("ulo", 44, [P, FT, TOK], F32R)
        gcv = at("gcv", 88, [P, TOK])
        gsg = at("gsg", 90, [P, TOK])
        guf = at("guf", 92, [P, TOK])

        ps = ctx.enter_context(nc.psum_tensor("ps", [P, 8, 512], F32))

        def f(view):
            return view.bitcast(F32)

        def cst(name, lo=0, hi=None):
            a, b = CN[name]
            return cn[:, a + lo:(b if hi is None else a + hi)]

        def pmc(name, lo=0, hi=None):
            a, b = PM[name]
            return pm[:, a + lo:(b if hi is None else a + hi)]

        ident = cst("ident")

        cn_loaded, avg_set = sem("cn_loaded"), sem("avg_set")
        x_loaded = [sem(f"x_loaded{k}") for k in range(CT // 2)]
        pm_loaded, pf_loaded = sem("pm_loaded"), sem("pf_loaded")
        raw_loaded = [sem(f"raw_loaded{k}") for k in range(RING)]
        unit_hi, unit_split, unit_used = sem("unit_hi"), sem("unit_split"), sem("unit_used")
        y_stored = sem("y_stored")
        link = sem("dve_link")
        dt_copied, dt_abs, dt_exp = sem("dt_copied"), sem("dt_abs"), sem("dt_exp")
        dtx_done, la_done, dec_done = sem("dtx_done"), sem("la_done"), sem("dec_done")
        dd_done, la_high, la_split, r_low = sem("dd_done"), sem("la_high"), sem("la_split"), sem("r_low")
        conv_center, conv_taps = sem("conv_center"), sem("conv_taps")
        conv_tanh, silu_done = sem("conv_tanh"), sem("silu_done")
        aux_full, t_evac, cb_done = sem("aux_full"), sem("t_evac"), sem("cb_done")
        proj_copied, rope_sin, rope_done = sem("proj_copied"), sem("rope_sin"), sem("rope_done")
        v_done, tanh_done, zs_done = sem("v_done"), sem("tanh_done"), sem("zs_done")
        xw_done, y_full, st_done, xd_done = sem("xw_done"), sem("y_full"), sem("st_done"), sem("xd_done")
        yd_done, r_done, seg_full = sem("yd_done"), sem("r_done"), sem("seg_full")
        exp_done, w_done, seg_used = sem("exp_done"), sem("w_done"), sem("seg_used")
        yo_done, ya_done, gated = sem("yo_done"), sem("ya_done"), sem("gated")
        as_const, as_full, as_max = sem("as_const"), sem("as_full"), sem("as_max")
        as_exp, as_den, as_norm = sem("as_exp"), sem("as_den"), sem("as_norm")
        pt_done, ah_done, al_done = sem("pt_done"), sem("ah_done"), sem("al_done")
        rms_sq, rms_pair, rms_mm, rms_std = sem("rms_sq"), sem("rms_pair"), sem("rms_mm"), sem("rms_std")
        ssd_normed, sh_done, sl_done = sem("ssd_normed"), sem("sh_done"), sem("sl_done")
        h_rebuilt, acc_done, res_done = sem("h_rebuilt"), sem("acc_done"), sem("res_done")
        ln_mean, ln_cent, ln_sq, ln_sqmm = sem("ln_mean"), sem("ln_cent"), sem("ln_sq"), sem("ln_sqmm")
        ln_rstd, ln_spread = sem("ln_rstd"), sem("ln_spread")
        pair_sum, pair_sq = sem("pair_sum"), sem("pair_sq")
        ln_std, ln_scaled, ln_hi, ln_bias = sem("ln_std"), sem("ln_scaled"), sem("ln_hi"), sem("ln_bias")
        h_ready = [sem("h_ready_even"), sem("h_ready_odd")]
        h_back, y_ready = sem("h_back"), sem("y_ready")
        glu_center, glu_taps, glu_silu = sem("glu_center"), sem("glu_taps"), sem("glu_silu")
        glu_done, glu_hi, glu_ready = sem("glu_done"), sem("glu_hi"), sem("glu_ready")

        aux_use, y_use = {}, {}
        aux_free, y_free = [], []
        aux_counted, y_counted = {}, {}

        def take(use, free, counted, key, releases, counts=True):
            use[key] = len(free)
            free.append(releases)
            if counts:
                counted[key] = len(counted) + 1

        n_t = 0
        for what, i in SCHED:
            aux = lambda key, rel, c=True: take(aux_use, aux_free, aux_counted, key, rel, c)
            yy = lambda key, rel, c=True: take(y_use, y_free, y_counted, key, rel, c)
            if what == "DTT":
                aux(("DTT", 0), [(dtx_done, 1, 1)])
            elif what == "SM":
                aux(("SM", 0), [(dec_done, 1, 1)])
            elif what == "CB":
                aux(("CB", i), [(cb_done, 4, 2 * i + 2)])
            elif what == "T":
                n_t += 1
                aux(("T", i), [(t_evac, 10, n_t)])
            elif what == "VT":
                aux(("VT", 0), [(v_done, 1, 1)])
            elif what == "ROT":
                aux(("ROT", i), [(rope_sin, 5, (i + 1) % 5 + 1)])
            elif what == "AP":
                yy(("AP", i, 0), [(pt_done, 8, i + 1)])
                yy(("AP", i, 1), [(pt_done, 8, i + 1)])
            elif what == "AV":
                aux(("AV", i), [(al_done, 8, i + 1)])
            elif what == "RS" and i == 0:
                aux(("RS", 0), [(rms_std, 1, 1)], False)
            elif what == "ST":
                aux(("ST", i), [(st_done, 8, (i ^ 1) + 1)])
            elif what == "YO":
                yy(("YO", i), [(yo_done, 8, i + 1)])
            elif what == "SD" and SEGS[i][2] == 0:
                yy(("SD", i // 2), [(ya_done, 8, i // 2 + 1)], False)
            elif what == "YT":
                aux(("YT", i), [(gated, 8, i + 1)])
        AUX_N, Y_N = len(aux_counted), len(y_counted)
        def aux_bank(key):
            return 6 + aux_use[key] % 2

        def y_bank(key):
            return 4 + y_use[key] % 2

        def wait_aux_free(eng, L, key):
            n = aux_use[key] - 2
            if n >= 0:
                for s, per, count in aux_free[n]:
                    eng.wait_ge(s, L * per + count)

        def wait_y_free(eng, L, key):
            n = y_use[key] - 2
            if n >= 0:
                for s, per, count in y_free[n]:
                    eng.wait_ge(s, L * per + count)

        def wait_aux_full(eng, L, key):
            eng.wait_ge(aux_full, L * AUX_N + aux_counted[key])

        def wait_y_full(eng, L, key):
            eng.wait_ge(y_full, L * Y_N + y_counted[key])

        ACC_ORDER = [4, 5, 6, 7, 0, 1, 2, 3]
        MEANS = [0, 1, 3, 2, 4]
        MEANS_AFTER = {4: 0, 6: 1}
        WARM = (2, 2)
        SQUARES = [("tile", 0), ("tile", 1), ("tile", 2), ("tile", 3), ("tile", 6), ("pair", 0), ("tile", 7)]

        def wait_tile(eng, idx, c):
            eng.wait_ge(h_ready[c % 2], idx * (CT // 2) + c // 2 + 1)

        block = ctx.enter_context(nc.Block())

        @block.sync
        def _(sp_eng):
            for k in range(CT // 2):
                c = ACC_ORDER[2 * k]
                sp_eng.dma_start(h[:, c:c + 2, :], x_t[:, c:c + 2, :]).then_inc(x_loaded[c // 2], 16)
            sp_eng.dma_start(cn[:], cn_d).then_inc(cn_loaded, 16)
            sp_eng.wait_ge(x_loaded[ACC_ORDER[4] // 2], 16)
            for j in range(RING):
                sp_eng.dma_start(raw[:, j, :], units[j]).then_inc(raw_loaded[j], 16)
            with sp_eng.Fori(1, DEPTH * TURNS) as g:
                for j in range(RING):
                    sp_eng.wait_ge(unit_split, g * RING + (j - RING + 1))
                    sp_eng.dma_start(raw[:, j, :], units[g * RING + j]).then_inc(raw_loaded[j], 16)
            for j in range(RING):
                sp_eng.wait_ge(unit_split, (DEPTH * TURNS - 1) * RING + j + 1)
                sp_eng.dma_start(raw[:, j, :], units[j]).then_inc(raw_loaded[j], 16)
            for c in (1, 3, 5, 7, 0, 2, 4, 6):
                if c % 2:
                    sp_eng.wait_ge(ln_bias, 2 * DEPTH * (CT // 2) + c // 2 + 1)
                else:
                    sp_eng.wait_ge(y_ready, c // 2 + 1)
                sp_eng.dma_start(y_t[:, c, :], h[:, c, :]).then_inc(y_stored, 16)
            sp_eng.wait_ge(y_stored, CT * 16)

        @block.gpsimd
        def _(pool):
            def lows(idx):
                for c in range(1, CT, 2):
                    pool.wait_ge(ln_bias, idx * (CT // 2) + c // 2 + 1)
                    nc.gpsimd.tensor_tensor(hlo[:, c, :], h[:, c, :], f(hhi[:, c, :]), ALU.subtract).then_inc(h_ready[1], 1)

            def pair_sums(idx, res_count):
                for q in range(3):
                    if res_count is None:
                        pool.wait_ge(x_loaded[ACC_ORDER[2 * q] // 2], 16)
                    else:
                        pool.wait_ge(res_done, res_count + 2 * q + 2)
                    nc.gpsimd.tensor_tensor(pair[:, q, :], h[:, ACC_ORDER[2 * q], :], h[:, ACC_ORDER[2 * q + 1], :],
                                            ALU.add).then_inc(pair_sum, 1)
                pool.wait_ge(ln_sq, idx * CT + 6)
                nc.gpsimd.tensor_tensor(pair[:, 3, :], sq[:, 4, :], sq[:, 5, :], ALU.add).then_inc(pair_sq, 1)

            nc.gpsimd.memset(avg[:], 1.0 / D_MODEL).then_inc(avg_set, 1)
            nc.gpsimd.memset(avg_row[:], 0.0).then_inc(avg_set, 1)
            pool.wait_ge(avg_set, 2)
            for b in range(NBLK):
                nc.gpsimd.memset(avg_row[:, b, b:b + 1], 1.0 / D_MODEL).then_inc(avg_set, 1)
            pair_sums(0, None)
            for j in range(2):
                pool.wait_ge(unit_hi, j + 1)
                nc.gpsimd.tensor_tensor(wlo[:, j, :], raw[:, j, :], f(whi[:, j, :]), ALU.subtract).then_inc(unit_split, 1)
            lows(0)
            with pool.Fori(0, DEPTH) as L:
                wait_tile(pool, L * 2, CT - 2)
                wait_tile(pool, L * 2, CT - 1)
                pool.dma_start(pm[:], pm_d[L]).then_inc(pm_loaded, 16)
                pool.dma_start(pf[:], pf_d[L]).then_inc(pf_loaded, 16)
                pool.wait_ge(pm_loaded, L * 16 + 16)
                for what, i in SCHED:
                    if what == "AN":
                        pool.wait_ge(as_den, L * 8 + i + 1)
                        nc.gpsimd.tensor_tensor(sc[i % 2][:], sc[i % 2][:],
                                                ast[:, i % 2, 5, :].unsqueeze(2).broadcast_to((P, QPK, SEQ)),
                                                ALU.mult).then_inc(as_norm, 1)
                    elif what == "SQ" and i in (1, 3, 5):
                        pool.wait_ge(rms_sq, L * CT + i + 1)
                        out = rms_sum[0 if i == 1 else 1]
                        nc.gpsimd.tensor_tensor(out[:], sqr[(i - 1) % 4][:], sqr[i % 4][:], ALU.add).then_inc(rms_pair, 1)
                        if i == 3:
                            pool.wait_ge(rms_pair, L * 4 + 2)
                            nc.gpsimd.tensor_tensor(rms_sum[0][:], rms_sum[0][:], rms_sum[1][:], ALU.add).then_inc(rms_pair, 1)
                    elif what == "SA":
                        t, g, d = SEGS[i]
                        if i == 0:
                            pool.wait_ge(la_split, L + 1)
                        if i >= 2:
                            pool.wait_ge(seg_full, L * 16 + i - 1)
                        a0 = d * SSD_HEADS + g * HPG
                        nc.gpsimd.tensor_tensor(seg_lo[i % 2][:],
                                                cst("upper" if d == 0 else "lower").unsqueeze(1).broadcast_to((P, HPG, P)),
                                                f(la_lo[:, t, a0:a0 + HPG]).unsqueeze(2).broadcast_to((P, HPG, P)),
                                                ALU.mult).then_inc(r_low, 1)
                    elif what in ("XD", "XW", "DS"):
                        g, t = divmod(i, NBLK)
                        x = xs_tm[:, t, g * 512:(g + 1) * 512].rearrange("p (h c) -> p h c", c=HEAD)
                        scaled = (P, HPG, HEAD)
                        if (what, i) in (("XD", 0), ("XW", NBLK + 1)):
                            pool.wait_ge(t_evac, L * 10 + 6 + 4 * g)
                            pool.wait_ge(dd_done, L + 1)
                        if what == "XD":
                            if i >= 2:
                                pool.wait_ge(seg_used, L * 16 + 2 * i - 2)
                            for d in range(2):
                                a0 = d * SSD_HEADS + g * HPG
                                nc.gpsimd.tensor_tensor(xd[:, i % 2, d, :].rearrange("p (h c) -> p h c", c=HEAD), x,
                                                        dt[:, t, a0:a0 + HPG].unsqueeze(2).broadcast_to(scaled),
                                                        ALU.mult).then_inc(xd_done, 1)
                        elif what == "XW":
                            if i == 1:
                                pool.wait_ge(as_full, L * 8 + 8)
                            if g == 1:
                                wait_aux_full(pool, L, ("ST", i - NBLK))
                            nc.gpsimd.tensor_tensor(xw[:, t, :].rearrange("p (h c) -> p h c", c=HEAD), x,
                                                    dd[:, t, t % 2, g * HPG:(g + 1) * HPG].unsqueeze(2).broadcast_to(scaled),
                                                    ALU.mult).then_inc(xw_done, 1)
                        else:
                            pool.wait_ge(xd_done, L * 16 + 2 * i + 2)
                            pool.wait_ge(xw_done, L * 8 + (i ^ 1) + 1)
                            nc.gpsimd.tensor_tensor(x, x, pmc("d", g * HPG, (g + 1) * HPG).unsqueeze(2).broadcast_to(scaled),
                                                    ALU.mult).then_inc(yd_done, 1)
                for c in range(CT):
                    pool.wait_ge(sl_done, L * CT + c + 1)
                    nc.gpsimd.tensor_tensor(h[:, c, :], f(hhi[:, c, :]), f(hlo[:, c, :]), ALU.add).then_inc(h_rebuilt, 1)
                pair_sums(L * 2 + 1, L * 2 * CT)
                lows(L * 2 + 1)
                for c in range(CT):
                    wait_tile(pool, L * 2 + 1, c)
                    nc.gpsimd.tensor_tensor(h[:, c, :], f(hhi[:, c, :]), f(hlo[:, c, :]), ALU.add).then_inc(h_back, 1)
                pair_sums(L * 2 + 2, L * 2 * CT + CT)
                lows(L * 2 + 2)

        @block.scalar
        def _(act):
            A = nc.scalar.activation

            def split_hi(turn, slot, first=False):
                act.wait_ge(raw_loaded[slot], turn * 16 + 16)
                A(whi[:, slot, :], raw[:, slot, :], ACT.Copy).then_inc(unit_hi, 1)

            def split_next(L, n, more=0):
                act.wait_ge(unit_used, L * UNITS + n + 1 + more * RING)
                split_hi(L * TURNS + (n // RING + 1) + more, n % RING)

            def layer_norm(idx, bet, between=None):
                for c in range(CT):
                    act.wait_ge(ln_cent, idx * CT + c + 1)
                    A(sq[:, c, :], h[:, c, :], ACT.Square).then_inc(ln_sq, 1)
                if between:
                    between()
                act.wait_ge(ln_sqmm, idx + 1)
                A(rstd[:], ps[0:NBLK, 5, 0:BLK], ACT.Sqrt, bias=cst("eps")[0:NBLK, :]).then_inc(ln_std, 1)
                for c in range(CT):
                    act.wait_ge(ln_scaled, idx * CT + c + 1)
                    A(hhi[:, c, :], h[:, c, :], ACT.Identity, bias=bet[:, c:c + 1]).then_inc(ln_hi, 1)
                    if c % 2:
                        A(h[:, c, :], h[:, c, :], ACT.Identity, bias=bet[:, c:c + 1]).then_inc(ln_bias, 1)

            def first_splits():
                for j in range(2):
                    split_hi(0, j)
                act.wait_ge(cn_loaded, 16)

            layer_norm(0, cst("ln_b"), first_splits)
            split_hi(0, 2)
            A(big_i[:], ident, ACT.Copy, scale=MASK / SCALE).then_inc(as_const, 1)
            A(cut[:, 0, :], cst("before"), ACT.Copy).then_inc(as_const, 1)
            A(cut[:, 1, :], cst("after"), ACT.Copy).then_inc(as_const, 1)

            with act.Fori(0, DEPTH) as L:
                act.wait_ge(pm_loaded, L * 16 + 16)
                for what, i in SCHED:
                    if what == "S":
                        split_next(L, i - RING)
                    elif what == "E" and i == U_DT:
                        act.wait_ge(unit_used, L * UNITS + i + 1)
                        A(zt[0:32, :], ps[0:32, i % 2, :], ACT.Copy).then_inc(dt_copied, 1)
                    elif what == "E" and U_CONV <= i < U_Z:
                        j = i - U_CONV
                        act.wait_ge(unit_used, L * UNITS + i + 1)
                        if j >= 2:
                            act.wait_ge(silu_done, L * N_CONV + j - 1)
                        A(cv[:, j % 2, :], ps[:, i % 2, :], ACT.Identity, scale=pmc("conv_w", 5 * j + 2, 5 * j + 3),
                          bias=pmc("conv_b", j, j + 1)).then_inc(conv_center, 1)
                    elif what == "E" and i < U_Z:
                        m = i - U_K
                        act.wait_ge(unit_used, L * UNITS + i + 1)
                        dst = zt[:] if i == U_V else qk[:, 4 if i == U_K else i - U_Q, :]
                        A(dst, ps[:, i % 2, :], ACT.Copy).then_inc(proj_copied, 1)
                    elif what == "E":
                        c = i - U_Z
                        act.wait_ge(unit_used, L * UNITS + i + 1)
                        if c >= 1:
                            act.wait_ge(zs_done, L * CT + c)
                        A(zt[:], ps[:, i % 2, :], ACT.Tanh, scale=0.5).then_inc(tanh_done, 1)
                    elif what == "SILU":
                        act.wait_ge(conv_taps, L * 4 * N_CONV + 4 * i + 4)
                        if i == 0:
                            act.wait_ge(rope_done, L * 5 + 5)
                        if i >= 6:
                            wait_aux_full(act, L, ("T", i - 2))
                        dst = bc[:, i, :] if i < 4 else xsc[:, i % 2, :]
                        A(dst, cv[:, i % 2, :], ACT.Tanh, scale=0.5).then_inc(conv_tanh, 1)
                    elif what == "SP":
                        act.wait_ge(dt_abs, L + 1)
                        A(sp[:, 2, :], sp[:, 1, :], ACT.Exp, scale=-1.0).then_inc(dt_exp, 1)
                        A(neg_a[:], pmc("a_log"), ACT.Exp).then_inc(dt_exp, 1)
                    elif what == "SM":
                        act.wait_ge(la_done, L + 1)
                        A(la_hi[:], la[:], ACT.Copy).then_inc(la_high, 1)
                        wait_aux_full(act, L, ("SM", 0))
                        A(dec[:].rearrange("p t d h -> p (t d h)"), ps[:, aux_bank(("SM", 0)), 0:128],
                          ACT.Exp).then_inc(dec_done, 1)
                    elif what == "T":
                        wait_aux_full(act, L, ("T", i))
                        dst = b_tm[:, :, i * P:(i + 1) * P] if i < 2 else xs_tm[:, :, (i - 4) * P:(i - 3) * P]
                        A(dst, ps[:, aux_bank(("T", i)), :].rearrange("p (t c) -> p t c", c=P),
                          ACT.Copy, scale=0.5).then_inc(t_evac, 1)
                    elif what == "VT":
                        wait_aux_full(act, L, ("VT", 0))
                        A(v_tm[:], ps[:, aux_bank(("VT", 0)), :].rearrange("p (t c) -> p t c", c=P),
                          ACT.Copy).then_inc(v_done, 1)
                    elif what == "ST":
                        t = i % NBLK
                        wait_aux_full(act, L, ("ST", i))
                        if i >= NBLK:
                            wait_y_full(act, L, ("YO", (i - NBLK) ^ 1))
                        A(st[:, t, :], ps[:, aux_bank(("ST", i)), :], ACT.Copy).then_inc(st_done, 1)
                    elif what == "SE":
                        act.wait_ge(seg_full, L * 16 + i + 1)
                        if i >= 3:
                            act.wait_ge(seg_used, L * 16 + i - 2)
                        A(seg_e[i % 3][:].rearrange("p h q -> p (h q)"),
                          ps[:, 2:4, :].rearrange("p b n -> p (b n)"), ACT.Exp).then_inc(exp_done, 1)
                    elif what == "AX":
                        act.wait_ge(as_max, L * 8 + i + 1)
                        if i >= 2:
                            wait_y_full(act, L, ("AP", i - 2, 1))
                        for j in range(QPK):
                            A(sc[i % 2][:, j, :], ps[:, 2 + j // 2, (j % 2) * SEQ:(j % 2 + 1) * SEQ], ACT.Exp, scale=SCALE,
                              bias=ast[:, i % 2, 1, j:j + 1], accum_out=ast[:, i % 2, 3, j:j + 1])
                        A(ast[:, i % 2, 4, :], ast[:, i % 2, 2, :], ACT.Exp).then_inc(as_exp, 1)
                    elif what == "AP":
                        wait_y_full(act, L, ("AP", i, 1))
                        if i >= 2:
                            wait_aux_full(act, L, ("AV", i - 2))
                        assert y_bank(("AP", i, 0)) == 4
                        A(p_t[i % 2][:], ps[:, 4:6, :], ACT.Copy).then_inc(pt_done, 1)
                    elif what == "AV":
                        t, g = ATTN[i]
                        rows = slice(g * HEAD, (g + 1) * HEAD)
                        wait_aux_full(act, L, ("AV", i))
                        A(ahi[rows, 0:QPK, t * BLK:(t + 1) * BLK],
                          ps[rows, aux_bank(("AV", i)), :].rearrange("p (j q) -> p j q", q=BLK),
                          ACT.Copy).then_inc(ah_done, 1)
                    elif what == "SQ":
                        act.wait_ge(gated, L * 8 + (4 if i < 4 else 8))
                        if i >= 4:
                            act.wait_ge(rms_pair, L * 4 + 3)
                        A(sqr[i % 4][:], zs[:, i, :], ACT.Square).then_inc(rms_sq, 1)
                    elif what == "RMS":
                        act.wait_ge(rms_mm, L + 1)
                        A(std[:], ps[:, aux_bank(("RS", 0)), :], ACT.Sqrt, bias=cst("eps")).then_inc(rms_std, 1)
                    elif what == "RN":
                        act.wait_ge(ssd_normed, L * CT + i + 1)
                        A(ahi[:, QPK + i, :], zs[:, i, :], ACT.Copy).then_inc(sh_done, 1)

                split_next(L, U_UP - 2)
                split_next(L, U_UP - 1)
                act.wait_ge(pf_loaded, L * 16 + 16)
                a1, b1 = PF["ln1_b"]
                layer_norm(L * 2 + 1, pf[:, a1:b1])

                def glu(I, p):
                    n, bank = U_UP + 2 * p, 2 * (p % RING)
                    off = I * 2 * RING
                    act.wait_ge(unit_used, L * UNITS + off + (n + 1))
                    k = (I * RING + p)
                    w0, _ = PF["conv_w"]
                    v0, _ = PF["conv_b"]
                    A(gcv[:], ps[:, bank, :], ACT.Identity, scale=pf[:, bass.ds(k * 3 + (w0 + 1), 1)],
                      bias=pf[:, bass.ds(k + v0, 1)]).then_inc(glu_center, 1)
                    split_next(L, n, I * 2)
                    act.wait_ge(glu_taps, (L * FT + k + 1) * 2)
                    act.wait_ge(glu_done, L * FT + k + RING)
                    A(gsg[:], gcv[:], ACT.Silu).then_inc(glu_silu, 1)
                    split_next(L, n + 1, I * 2)
                    act.wait_ge(glu_done, L * FT + k + RING + 1)
                    A(uhi[:, bass.ds(k, 1), :].rearrange("p a n -> p (a n)"), guf[:], ACT.Copy).then_inc(glu_hi, 1)

                glu(0, 0)
                with act.Fori(0, FT // RING) as I:
                    for p in range(RING):
                        glu(I, p + 1)
                with act.Fori(0, FT // RING) as I:
                    for j in range(RING):
                        split_next(L, U_DOWN + j, I)
                split_next(L, UNITS - 1)
                a2, b2 = PF["ln2_b"]
                layer_norm(L * 2 + 2, pf[:, a2:b2])

        @block.tensor
        def _(pe):
            mm = nc.tensor.matmul

            def three(out, slot, cols, xhi, xlo, start, stop):
                mm(out, whi[:, slot, cols], xhi, start=start, stop=False)
                mm(out, whi[:, slot, cols], xlo, start=False, stop=False)
                return mm(out, wlo[:, slot, cols], xhi, start=False, stop=stop)

            def by_columns(slot, bank):
                for c in range(CT):
                    last = three(ps[:, bank, :], slot, slice(c * P, (c + 1) * P), hhi[:, c, :], hlo[:, c, :],
                                 c == 0, c == CT - 1)
                last.then_inc(unit_used, 1)

            def first_units(norm):
                for c in range(CT):
                    wait_tile(pe, norm, c)
                    for k in range(2):
                        last = three(ps[:, k, :], k, slice(c * P, (c + 1) * P), hhi[:, c, :], hlo[:, c, :],
                                     c == 0, c == CT - 1)
                        if c == CT - 1:
                            last.then_inc(unit_used, 1)

            def by_rows(slot, xhi, xlo, start=False, residuals=None, before=None, banks=range(CT), norm=None, ends=True):
                stop = residuals is not None
                order = ACC_ORDER if stop else banks
                for n, c in enumerate(order):
                    if before and c in before:
                        pe.wait_ge(*before[c])
                    last = three(ps[:, c, :], slot, slice(c * P, (c + 1) * P), xhi, xlo, start, stop)
                    if stop and n < CT - 1:
                        last.then_inc(acc_done, 1)
                    elif n == len(order) - 1 and ends:
                        last.then_inc(unit_used, 1)
                    if stop and n in MEANS_AFTER:
                        mean(norm, MEANS_AFTER[n], residuals)
                if stop:
                    for q in MEANS[len(MEANS_AFTER):]:
                        mean(norm, q, residuals)

            def mean(idx, q, res_count):
                if q < 3:
                    pe.wait_ge(pair_sum, idx * 3 + q + 1)
                    x = pair[:, q, :]
                else:
                    c = ACC_ORDER[CT - 5 + q]
                    if res_count is not None:
                        pe.wait_ge(res_done, res_count + CT - 4 + q)
                    else:
                        pe.wait_ge(x_loaded[c // 2], 16)
                    x = h[:, c, :]
                if q == MEANS[0]:
                    if res_count is not None:
                        pe.wait_ge(res_done, res_count + 2)
                last = mm(ps[:, 4, :], avg[:], x, start=(q == MEANS[0]), stop=(q == MEANS[-1]))
                if q == MEANS[-1]:
                    last.then_inc(ln_mean, 1)

            def keep_warm(n, x):
                for _ in range(n):
                    mm(ps[:, 7, 0:x.shape[-1]], avg[:], x, start=True, stop=True)

            def squares(idx):
                for q, (what, n) in enumerate(SQUARES):
                    if what == "pair":
                        pe.wait_ge(pair_sq, idx + 1)
                        x = pair[:, 3, :]
                    else:
                        pe.wait_ge(ln_sq, idx * CT + n + 1)
                        x = sq[:, n, :]
                    for b in range(NBLK):
                        last = mm(ps[0:NBLK, 5, 0:BLK], avg_row[:, b, :], x[:, b * BLK:(b + 1) * BLK],
                                  start=(q == 0 and b == 0), stop=(q == len(SQUARES) - 1 and b == NBLK - 1))
                last.then_inc(ln_sqmm, 1)
                keep_warm(WARM[0], cn[:, CN["cos"][0]:CN["sin"][1]])
                pe.wait_ge(ln_rstd, idx + 1)
                for b in range(NBLK):
                    last = mm(ps[:, 6, b * BLK:(b + 1) * BLK], ident[0:NBLK, b:b + 1].broadcast_to((NBLK, P)),
                              rstd[:], start=True, stop=True)
                last.then_inc(ln_spread, 1)
                keep_warm(WARM[1], cn[:, CN["cos"][0]:CN["sin"][1]])

            pe.wait_ge(avg_set, 1)
            keep_warm(9, avg[:])
            for q in MEANS:
                mean(0, q, None)
            pe.wait_ge(cn_loaded, 16)
            pe.wait_ge(avg_set, 2 + NBLK)
            squares(0)
            with pe.Fori(0, DEPTH) as L:
                for what, i in SCHED:
                    if what == "G" and i == 0:
                        pe.wait_ge(unit_split, L * UNITS + 2)
                        first_units(L * 2)
                    elif what == "G" and i == 1:
                        pass
                    elif what == "G" and i < U_OUT:
                        if i == 2:
                            pe.wait_ge(dt_copied, L + 1)
                        elif U_CONV <= i - 2 < U_Z:
                            pe.wait_ge(conv_taps, L * 4 * N_CONV + 4 * (i - 2 - U_CONV) + 4)
                        elif U_K <= i - 2 < U_CONV:
                            pe.wait_ge(proj_copied, L * 6 + i - 2 - U_K + 1)
                        elif i - 2 >= U_Z:
                            pe.wait_ge(zs_done, L * CT + i - 2 - U_Z + 1)
                        pe.wait_ge(unit_split, L * UNITS + i + 1)
                        by_columns(i % RING, i % 2)
                    elif what == "G":
                        k = i - U_OUT
                        pe.wait_ge(unit_split, L * UNITS + i + 1)
                        before = None
                        if k == 0:
                            pe.wait_ge(gated, L * 8 + 8)
                            pe.wait_ge(st_done, L * 8 + 8)
                            before = {aux_bank(("RS", 0)): (rms_std, L + 1)}
                        if k >= QPK:
                            pe.wait_ge(sl_done, L * CT + k - QPK + 1)
                        by_rows(i % RING, ahi[:, k, :], alo[:, k, :], k == 0, L * 2 * CT if k == N_OUT - 1 else None, before,
                                range(4, CT) if k < 2 else range(CT), norm=L * 2 + 1)
                    elif what == "GA":
                        u, banks = i
                        pe.wait_ge(unit_split, L * UNITS + u + 1)
                        pe.wait_ge(zs_done, L * CT + CT)
                        if 2 in banks:
                            pe.wait_ge(exp_done, L * 16 + 16)
                        pe.wait_ge(al_done, L * 8 + 8)
                        by_rows(u % RING, ahi[:, u - U_OUT, :], alo[:, u - U_OUT, :], u == U_OUT, banks=banks, ends=False)
                    elif what == "DTT":
                        pe.wait_ge(dt_copied, L + 1)
                        for t in range(NBLK):
                            last = mm(ps[:, aux_bank((what, i)), t * 32:(t + 1) * 32],
                                      zt[0:32, t * BLK:(t + 1) * BLK], ident[0:32, 0:32], start=True, stop=True)
                        last.then_inc(aux_full, 1)
                    elif what == "SM":
                        pe.wait_ge(la_done, L + 1)
                        wait_aux_free(pe, L, (what, i))
                        for t in range(NBLK):
                            for d, w in enumerate(("after", "lower") if t % 2 == 0 else ("upper", "before")):
                                at0 = (2 * t + d) * SSD_HEADS
                                last = mm(ps[:, aux_bank((what, i)), at0:at0 + SSD_HEADS], cst(w),
                                          la[:, t, d * SSD_HEADS:(d + 1) * SSD_HEADS], start=True, stop=True)
                        last.then_inc(aux_full, 1)
                    elif what == "T":
                        pe.wait_ge(silu_done, L * N_CONV + i + 1)
                        wait_aux_free(pe, L, (what, i))
                        src = bc[:, i, :] if i < 4 else xsc[:, i % 2, :]
                        for t in range(NBLK):
                            last = nc.tensor.transpose(ps[:, aux_bank((what, i)), t * BLK:(t + 1) * BLK],
                                                       src[:, t * BLK:(t + 1) * BLK], ident)
                        last.then_inc(aux_full, 1)
                    elif what == "CB":
                        pe.wait_ge(silu_done, L * N_CONV + 4)
                        wait_aux_free(pe, L, (what, i))
                        for n in range(4):
                            t, g = 2 * i + n // 2, n % 2
                            last = mm(ps[:, aux_bank((what, i)), n * P:(n + 1) * P], bc[:, g, t * BLK:(t + 1) * BLK],
                                      bc[:, 2 + g, t * BLK:(t + 1) * BLK], start=True, stop=True)
                        last.then_inc(aux_full, 1)
                    elif what == "VT":
                        pe.wait_ge(proj_copied, L * 6 + 2)
                        wait_aux_free(pe, L, (what, i))
                        for t in range(NBLK):
                            last = nc.tensor.transpose(ps[:, aux_bank((what, i)), t * BLK:(t + 1) * BLK],
                                                       zt[:, t * BLK:(t + 1) * BLK], ident)
                        last.then_inc(aux_full, 1)
                    elif what == "ROT":
                        pe.wait_ge(proj_copied, L * 6 + (1 if i == 4 else 3 + i))
                        wait_aux_free(pe, L, (what, i))
                        mm(ps[:, aux_bank((what, i)), :], cst("rot"), qk[:, i, :], start=True,
                           stop=True).then_inc(aux_full, 1)
                    elif what == "ST":
                        g, t = divmod(i, NBLK)
                        pe.wait_ge(xw_done, L * 8 + (i ^ 1) + 1)
                        wait_aux_free(pe, L, (what, i))
                        mm(ps[:, aux_bank((what, i)), :], b_tm[:, t, g * STATE:(g + 1) * STATE],
                           xw[:, t, :], start=True, stop=True).then_inc(aux_full, 1)
                    elif what == "YO":
                        g, t = divmod(i, NBLK)
                        pe.wait_ge(st_done, L * 8 + i + 1)
                        wait_y_free(pe, L, (what, i))
                        mm(ps[:, y_bank((what, i)), :], bc[:, 2 + g, t * BLK:(t + 1) * BLK],
                           st[:, t ^ 1, :], start=True, stop=True).then_inc(y_full, 1)
                    elif what == "SB":
                        t, g, d = SEGS[i]
                        pe.wait_ge(r_done, L * 16 + i + 1)
                        pe.wait_ge(r_low, L * 16 + i + 1)
                        if i >= 1:
                            pe.wait_ge(exp_done, L * 16 + i)
                        else:
                            pe.wait_ge(as_exp, L * 8 + 8)
                        for n in range(2):
                            for part in (seg_hi, seg_lo):
                                last = mm(ps[:, 2 + n, :], cut[:, 1 - d, :],
                                          part[i % 2][:, 4 * n:4 * n + 4, :].rearrange("p h q -> p (h q)"),
                                          start=(part is seg_hi), stop=(part is seg_lo))
                        last.then_inc(seg_full, 1)
                    elif what == "SD":
                        t, g, d = SEGS[i]
                        m = i // 2
                        pe.wait_ge(xd_done, L * 16 + 2 * m + 2)
                        pe.wait_ge(w_done, L * 16 + i + 1)
                        if d == 0:
                            wait_y_free(pe, L, ("SD", m))
                        bank = y_bank(("SD", m))
                        for n in range(HPG):
                            last = mm(ps[:, bank, n * HEAD:(n + 1) * HEAD], seg_e[i % 3][:, n, :],
                                      xd[:, m % 2, d, n * HEAD:(n + 1) * HEAD], start=(d == 0 and n == 0), stop=(d == 1),
                                      skip_group_check=True)
                        last.then_inc(seg_used, 1)
                    elif what == "YT":
                        g, t = divmod(i, NBLK)
                        pe.wait_ge(ya_done, L * 8 + i + 1)
                        wait_aux_free(pe, L, (what, i))
                        bank = aux_bank((what, i))
                        for n in range(4):
                            c = 4 * g + n
                            last = nc.tensor.transpose(ps[:, bank, n * BLK:(n + 1) * BLK],
                                                       xs_tm[:, t, c * P:(c + 1) * P], ident)
                        last.then_inc(aux_full, 1)
                    elif what == "AS":
                        t, g = ATTN[i]
                        rows = slice(g * HEAD, (g + 1) * HEAD)
                        if i == 0:
                            pe.wait_ge(rope_done, L * 5 + 5)
                            pe.wait_ge(as_const, 3)
                        else:
                            pe.wait_ge(as_exp, L * 8 + i)
                        o = 1 - t % 2
                        for m in range(2):
                            mm(ps[:, 2 + m, :].rearrange("p (j k) -> p j k", k=SEQ)[:, :, o * P:(o + 1) * P], big_i[:],
                               cut[:, t % 2, :].unsqueeze(1).broadcast_to((P, 2, P)), start=True, stop=False,
                               skip_group_check=True)
                            for n in range(2):
                                last = mm(ps[:, 2 + m, n * SEQ:(n + 1) * SEQ],
                                          qk[rows, 2 * m + n, t * BLK:(t + 1) * BLK],
                                          qk[rows, 4, (t // 2) * SEQ:(t // 2 + 1) * SEQ], start=False, stop=True,
                                          skip_group_check=True)
                        last.then_inc(as_full, 1)
                    elif what == "AP":
                        pe.wait_ge(as_norm, L * 8 + i + 1)
                        for kt in range(2):
                            wait_y_free(pe, L, (what, i, kt))
                            for j in range(QPK):
                                last = nc.tensor.transpose(ps[:, y_bank((what, i, kt)), j * BLK:(j + 1) * BLK],
                                                           sc[i % 2][:, j, kt * P:(kt + 1) * P], ident)
                            last.then_inc(y_full, 1)
                    elif what == "AV":
                        t, g = ATTN[i]
                        pe.wait_ge(v_done, L + 1)
                        pe.wait_ge(pt_done, L * 8 + i + 1)
                        wait_aux_free(pe, L, (what, i))
                        for kt in range(2):
                            last = mm(ps[g * HEAD:(g + 1) * HEAD, aux_bank((what, i)), :],
                                      v_tm[:, (t // 2) * 2 + kt, g * HEAD:(g + 1) * HEAD], p_t[i % 2][:, kt, :],
                                      start=(kt == 0), stop=(kt == 1))
                        last.then_inc(aux_full, 1)
                    elif what == "RS":
                        if i < 2:
                            pe.wait_ge(rms_pair, L * 4 + (3 if i == 0 else 4))
                        else:
                            pe.wait_ge(rms_sq, L * CT + CT - 3 + i)
                        if i == 0:
                            wait_aux_free(pe, L, (what, i))
                        x = rms_sum[i % 2][:] if i < 2 else sqr[i][:]
                        last = mm(ps[:, aux_bank(("RS", 0)), :], avg[:], x, start=(i == 0), stop=(i == 1))
                        if i == 1:
                            last.then_inc(rms_mm, 1)

                squares(L * 2 + 1)

                pe.wait_ge(unit_split, L * UNITS + U_UP + 2)
                first_units(L * 2 + 1)

                def glu(I, p):
                    k = I * RING + p
                    pe.wait_ge(glu_done, L * FT + k + 1)
                    for half in range(2):
                        n = U_UP + 2 * p + half
                        pe.wait_ge(unit_split, L * UNITS + I * 2 * RING + (n + 1))
                        by_columns(n % RING, 2 * (p % RING) + half)

                with pe.Fori(0, FT // RING) as I:
                    for p in range(RING):
                        glu(I, p + 1)

                def down(k, n, start=False, residuals=None):
                    pe.wait_ge(unit_split, L * UNITS + k + (U_DOWN + 1))
                    pe.wait_ge(glu_ready, L * FT + k + 1)
                    banks, before = range(CT), None
                    if start:
                        pe.wait_ge(glu_done, L * FT + FT + RING - 1)
                        banks, before = (2, 3, 4, 5, 6, 7, 0, 1), {0: (glu_done, L * FT + FT + RING)}
                    if isinstance(k, int):
                        xhi, xlo = uhi[:, k, :], ulo[:, k, :]
                    else:
                        xhi = uhi[:, bass.ds(k, 1), :].rearrange("p a n -> p (a n)")
                        xlo = ulo[:, bass.ds(k, 1), :].rearrange("p a n -> p (a n)")
                    by_rows((U_DOWN + n) % RING, xhi, xlo, start, residuals, before, banks, norm=L * 2 + 2)

                down(0, 0, start=True)
                with pe.Fori(0, (FT - 4) // RING) as I:
                    for j in range(RING):
                        down(I * RING + (1 + j), 1 + j)
                for k in range(FT - 3, FT):
                    down(k, k, residuals=L * 2 * CT + CT if k == FT - 1 else None)
                squares(L * 2 + 2)

        @block.vector
        def _(dve):
            V = nc.vector

            def split_lo(slot, count):
                dve.wait_ge(unit_hi, count)
                V.tensor_tensor(wlo[:, slot, :], raw[:, slot, :], f(whi[:, slot, :]), ALU.subtract).then_inc(unit_split, 1)

            def split_next(L, n, more=0):
                split_lo(n % RING, L * UNITS + (n + RING + 1) + more * RING)

            def residual(L, first, acc, rebuilt):
                for n, c in enumerate(ACC_ORDER):
                    if n < CT - 1:
                        dve.wait_ge(acc_done, acc + n + 1)
                    else:
                        dve.wait_ge(unit_used, first)
                    dve.wait_ge(rebuilt, L * CT + c + 1)
                    V.scalar_tensor_tensor(out=h[:, c, :], in0=h[:, c, :], scalar=ALPHA, in1=ps[:, c, :],
                                           op0=ALU.mult, op1=ALU.add).then_inc(res_done, 1)

            def low(idx, c, bet):
                dve.wait_ge(ln_hi, idx * CT + c + 1)
                V.scalar_tensor_tensor(out=hlo[:, c, :], in0=h[:, c, :], scalar=bet[:, c:c + 1],
                                       in1=f(hhi[:, c, :]), op0=ALU.add, op1=ALU.subtract).then_inc(h_ready[0], 1)

            def layer_norm(idx, gam, bet, between=None):
                dve.wait_ge(ln_mean, idx + 1)
                for c in range(CT):
                    V.tensor_tensor(h[:, c, :], h[:, c, :], ps[:, 4, :], ALU.subtract).then_inc(ln_cent, 1)
                if between:
                    between()
                dve.wait_ge(ln_std, idx + 1)
                V.reciprocal(rstd[:], rstd[:]).then_inc(ln_rstd, 1)
                dve.wait_ge(ln_spread, idx + 1)
                for c in range(CT):
                    V.scalar_tensor_tensor(out=h[:, c, :], in0=h[:, c, :], scalar=gam[:, c:c + 1], in1=ps[:, 6, :],
                                           op0=ALU.mult, op1=ALU.mult).then_inc(ln_scaled, 1)
                    if c % 2:
                        low(idx, c - 1, bet)

            dve.sem_inc(glu_done, RING)
            for k in range(CT // 2):
                dve.wait_ge(x_loaded[k], 16)
            layer_norm(0, cst("ln_g"), cst("ln_b"), lambda: dve.wait_ge(cn_loaded, 16))
            dve.wait_ge(unit_split, 2)
            split_lo(2, RING)

            with dve.Fori(0, DEPTH) as L:
                count = [0]

                def chain(ins):
                    count[0] += 1
                    ins.then_inc(link, 1)
                    dve.wait_ge(link, L * LINKS + count[0])

                dve.wait_ge(pm_loaded, L * 16 + 16)
                for what, i in SCHED:
                    if what == "S":
                        split_next(L, i - RING)
                    elif what in ("F", "F2") and U_CONV <= i < U_Z:
                        j = i - U_CONV
                        dve.wait_ge(conv_center, L * N_CONV + j + 1)
                        dst = cv[:, j % 2, :].rearrange("p (b s) -> p b s", b=NSEQ)
                        src = ps[:, i % 2, :].rearrange("p (b s) -> p b s", b=NSEQ)
                        for n, tap in ((0, 0), (1, 1)) if what == "F" else ((2, 3), (3, 4)):
                            s = tap - 2
                            lo, hi = max(0, -s), SEQ - max(0, s)
                            if n:
                                dve.wait_ge(conv_taps, L * 4 * N_CONV + 4 * j + n)
                            V.scalar_tensor_tensor(out=dst[:, :, lo:hi], in0=src[:, :, lo + s:hi + s],
                                                   scalar=pmc("conv_w", 5 * j + tap, 5 * j + tap + 1),
                                                   in1=dst[:, :, lo:hi], op0=ALU.mult, op1=ALU.add).then_inc(conv_taps, 1)
                    elif what == "SILU":
                        dve.wait_ge(conv_tanh, L * N_CONV + i + 1)
                        x = bc[:, i, :] if i < 4 else xsc[:, i % 2, :]
                        V.scalar_tensor_tensor(out=x, in0=x, scalar=1.0, in1=cv[:, i % 2, :],
                                               op0=ALU.add, op1=ALU.mult).then_inc(silu_done, 1)
                    elif what == "F" and i >= U_Z:
                        c = i - U_Z
                        if c == 0:
                            wait_aux_full(dve, L, ("AV", 7))
                        if c == 4:
                            wait_aux_full(dve, L, ("T", N_CONV - 1))
                        dve.wait_ge(tanh_done, L * CT + c + 1)
                        V.scalar_tensor_tensor(out=zs[:, c, :], in0=zt[:], scalar=1.0, in1=ps[:, i % 2, :],
                                               op0=ALU.add, op1=ALU.mult).then_inc(zs_done, 1)
                    elif what == "SP":
                        X, AB, E_, DEN, U1, U2, PL, MX = (sp[:, n, :] for n in range(8))
                        wait_aux_full(dve, L, ("DTT", 0))
                        bias = pmc("dt_bias").unsqueeze(1).broadcast_to((P, NBLK, 32))
                        V.tensor_tensor(X.rearrange("p (t c) -> p t c", c=32),
                                        ps[:, aux_bank(("DTT", 0)), 0:128].rearrange("p (t c) -> p t c", c=32),
                                        bias, ALU.add).then_inc(dtx_done, 1)
                        dve.wait_ge(dtx_done, L + 1)
                        V.scalar_tensor_tensor(out=AB, in0=X, scalar=-1.0, in1=X, op0=ALU.mult, op1=ALU.max).then_inc(dt_abs, 1)
                        dve.wait_ge(dt_exp, L * 2 + 2)
                        chain(V.tensor_scalar(DEN, E_, 2.0, None, ALU.add))
                        chain(V.reciprocal(DEN, DEN))
                        chain(V.tensor_tensor(U1, E_, DEN, ALU.mult))
                        chain(V.tensor_tensor(U2, U1, U1, ALU.mult))
                        chain(V.tensor_scalar(PL, U2, 1.0 / 15, None, ALU.mult))
                        for n in range(6, 0, -1):
                            chain(V.scalar_tensor_tensor(out=PL, in0=PL, scalar=1.0 / (2 * n + 1), in1=U2,
                                                         op0=ALU.add, op1=ALU.mult))
                        chain(V.scalar_tensor_tensor(out=PL, in0=PL, scalar=1.0, in1=U1, op0=ALU.add, op1=ALU.mult))
                        chain(V.tensor_scalar(MX, X, 0.0, None, ALU.max))
                        chain(V.scalar_tensor_tensor(out=dt[:].rearrange("p t c -> p (t c)"), in0=PL, scalar=2.0,
                                                     in1=MX, op0=ALU.mult, op1=ALU.add))
                        V.scalar_tensor_tensor(out=la[:], in0=dt[:], scalar=-1.0,
                                               in1=neg_a[:].unsqueeze(1).broadcast_to((P, NBLK, 32)),
                                               op0=ALU.mult, op1=ALU.mult).then_inc(la_done, 1)
                    elif what == "SM":
                        dve.wait_ge(la_high, L + 1)
                        V.tensor_tensor(la_lo[:], la[:], f(la_hi[:]), ALU.subtract).then_inc(la_split, 1)
                        dve.wait_ge(dec_done, L + 1)
                        V.tensor_tensor(dd[:].rearrange("p t d h -> p (t d h)"), dt[:].rearrange("p t c -> p (t c)"),
                                        dec[:].rearrange("p t d h -> p (t d h)"), ALU.mult).then_inc(dd_done, 1)
                    elif what == "CB":
                        wait_aux_full(dve, L, (what, i))
                        src = ps[:, aux_bank((what, i)), :].rearrange("p (n q) -> p n q", q=P)
                        for d, m in enumerate(("upper", "lower")):
                            V.scalar_tensor_tensor(out=cb[:, d, 4 * i:4 * i + 4, :], in0=src, scalar=0.25,
                                                   in1=cst(m).unsqueeze(1).broadcast_to((P, 4, P)),
                                                   op0=ALU.mult, op1=ALU.mult).then_inc(cb_done, 1)
                    elif what == "ROT":
                        wait_aux_full(dve, L, (what, i))
                        n = (i + 1) % 5
                        tt = ropet[:].rearrange("p (b s) -> p b s", b=NSEQ)
                        x = qk[:, i, :].rearrange("p (b s) -> p b s", b=NSEQ)
                        r = ps[:, aux_bank((what, i)), :].rearrange("p (b s) -> p b s", b=NSEQ)
                        if n:
                            dve.wait_ge(rope_done, L * 5 + n)
                        V.tensor_tensor(tt, r, cst("sin").unsqueeze(1).broadcast_to((P, NSEQ, SEQ)), ALU.mult).then_inc(rope_sin, 1)
                        chain(V.tensor_tensor(x, x, cst("cos").unsqueeze(1).broadcast_to((P, NSEQ, SEQ)), ALU.mult))
                        dve.wait_ge(rope_sin, L * 5 + n + 1)
                        V.tensor_tensor(qk[:, i, :], qk[:, i, :], ropet[:], ALU.add).then_inc(rope_done, 1)
                    elif what == "SA":
                        t, g, d = SEGS[i]
                        if i == 1:
                            wait_aux_full(dve, L, ("AV", 7))
                        if i >= 2:
                            dve.wait_ge(seg_full, L * 16 + i - 1)
                        a0 = d * SSD_HEADS + g * HPG
                        V.tensor_tensor(seg_hi[i % 2][:], cst("upper" if d == 0 else "lower").unsqueeze(1).broadcast_to((P, HPG, P)),
                                        f(la_hi[:, t, a0:a0 + HPG]).unsqueeze(2).broadcast_to((P, HPG, P)),
                                        ALU.mult).then_inc(r_done, 1)
                    elif what == "SC":
                        t, g, d = SEGS[i]
                        dve.wait_ge(exp_done, L * 16 + i + 1)
                        if i == 0:
                            dve.wait_ge(cb_done, L * 4 + 4)
                        V.tensor_tensor(seg_e[i % 3][:], seg_e[i % 3][:],
                                        cb[:, d, 2 * t + g, :].unsqueeze(1).broadcast_to((P, HPG, P)),
                                        ALU.mult).then_inc(w_done, 1)
                    elif what == "YO":
                        g, t = divmod(i, NBLK)
                        wait_y_full(dve, L, (what, i))
                        V.scalar_tensor_tensor(out=yo[:].rearrange("p (h c) -> p h c", c=HEAD),
                                               in0=ps[:, y_bank((what, i)), :].rearrange("p (h c) -> p h c", c=HEAD), scalar=0.5,
                                               in1=dec[:, t, 1 - t % 2, g * HPG:(g + 1) * HPG].unsqueeze(2).broadcast_to((P, HPG, HEAD)),
                                               op0=ALU.mult, op1=ALU.mult).then_inc(yo_done, 1)
                        dve.wait_ge(yo_done, L * 8 + i + 1)
                        dve.wait_ge(yd_done, L * 8 + i + 1)
                        y = xs_tm[:, t, g * 512:(g + 1) * 512]
                        chain(V.tensor_tensor(y, y, yo[:], ALU.add))
                    elif what == "YA":
                        g, t = divmod(i, NBLK)
                        dve.wait_ge(seg_used, L * 16 + 2 * i + 2)
                        y = xs_tm[:, t, g * 512:(g + 1) * 512]
                        V.tensor_tensor(y, y, ps[:, y_bank(("SD", i)), :], ALU.add).then_inc(ya_done, 1)
                    elif what == "YT":
                        g, t = divmod(i, NBLK)
                        wait_aux_full(dve, L, (what, i))
                        dve.wait_ge(zs_done, L * CT + 4 * g + 4)
                        bank = aux_bank((what, i))
                        z = zs[:, 4 * g:4 * g + 4, t * BLK:(t + 1) * BLK]
                        V.scalar_tensor_tensor(out=z, in0=ps[:, bank, :].rearrange("p (n q) -> p n q", q=BLK),
                                               scalar=0.5, in1=z, op0=ALU.mult, op1=ALU.mult).then_inc(gated, 1)
                    elif what == "AM":
                        t, g = ATTN[i]
                        dve.wait_ge(as_full, L * 8 + i + 1)
                        sink = pmc("sink", g * QPK, (g + 1) * QPK)
                        top, minus, sink_in = (ast[:, i % 2, n, :] for n in range(3))
                        chain(V.tensor_reduce(top, ps[:, 2:4, :].rearrange("p b (j k) -> p (b j) k", k=SEQ), AX_X, ALU.max))
                        chain(V.scalar_tensor_tensor(out=top, in0=top, scalar=SCALE, in1=sink, op0=ALU.mult, op1=ALU.max))
                        chain(V.tensor_scalar(minus, top, -1.0, None, ALU.mult))
                        V.tensor_tensor(sink_in, sink, top, ALU.subtract).then_inc(as_max, 1)
                    elif what == "AD":
                        dve.wait_ge(as_exp, L * 8 + i + 1)
                        if i >= 2:
                            dve.wait_ge(as_norm, L * 8 + i - 1)
                        den = ast[:, i % 2, 5, :]
                        chain(V.tensor_tensor(den, ast[:, i % 2, 3, :], ast[:, i % 2, 4, :], ALU.add))
                        V.reciprocal(den, den).then_inc(as_den, 1)
                    elif what == "AV":
                        t, g = ATTN[i]
                        rows = slice(g * HEAD, (g + 1) * HEAD)
                        dve.wait_ge(ah_done, L * 8 + i + 1)
                        V.tensor_tensor(alo[rows, 0:QPK, t * BLK:(t + 1) * BLK],
                                        ps[rows, aux_bank((what, i)), :].rearrange("p (j q) -> p j q", q=BLK),
                                        f(ahi[rows, 0:QPK, t * BLK:(t + 1) * BLK]), ALU.subtract).then_inc(al_done, 1)
                    elif what == "RMS":
                        dve.wait_ge(rms_std, L + 1)
                        chain(V.reciprocal(std[:], std[:]))
                        V.scalar_tensor_tensor(out=zs[:, 0, :], in0=zs[:, 0, :], scalar=pmc("norm_g", 0, 1), in1=std[:],
                                               op0=ALU.mult, op1=ALU.mult).then_inc(ssd_normed, 1)
                    elif what == "RN":
                        if i + 1 < CT:
                            V.scalar_tensor_tensor(out=zs[:, i + 1, :], in0=zs[:, i + 1, :],
                                                   scalar=pmc("norm_g", i + 1, i + 2), in1=std[:],
                                                   op0=ALU.mult, op1=ALU.mult).then_inc(ssd_normed, 1)
                        dve.wait_ge(sh_done, L * CT + i + 1)
                        V.tensor_tensor(alo[:, QPK + i, :], zs[:, i, :], f(ahi[:, QPK + i, :]), ALU.subtract).then_inc(sl_done, 1)

                assert count[0] == LINKS, count[0]
                residual(L, L * UNITS + U_UP, L * 14, h_rebuilt)
                split_next(L, U_UP - 2)
                dve.wait_ge(pf_loaded, L * 16 + 16)
                (g0, g1), (b0, b1) = PF["ln1_g"], PF["ln1_b"]
                layer_norm(L * 2 + 1, pf[:, g0:g1], pf[:, b0:b1], lambda: split_next(L, U_UP - 1))

                def glu(I, p):
                    n, bank = U_UP + 2 * p, 2 * (p % RING)
                    k = I * RING + p
                    w0, _ = PF["conv_w"]
                    dst = gcv[:].rearrange("p (b s) -> p b s", b=NSEQ)
                    src = ps[:, bank, :].rearrange("p (b s) -> p b s", b=NSEQ)
                    dve.wait_ge(glu_center, L * FT + k + 1)
                    V.scalar_tensor_tensor(out=dst[:, :, 1:SEQ], in0=src[:, :, 0:SEQ - 1], scalar=pf[:, bass.ds(k * 3 + w0, 1)],
                                           in1=dst[:, :, 1:SEQ], op0=ALU.mult, op1=ALU.add).then_inc(glu_taps, 1)
                    dve.wait_ge(glu_taps, (L * FT + k) * 2 + 1)
                    V.scalar_tensor_tensor(out=dst[:, :, 0:SEQ - 1], in0=src[:, :, 1:SEQ], scalar=pf[:, bass.ds(k * 3 + (w0 + 2), 1)],
                                           in1=dst[:, :, 0:SEQ - 1], op0=ALU.mult, op1=ALU.add).then_inc(glu_taps, 1)
                    split_next(L, n, I * 2)
                    dve.wait_ge(unit_used, L * UNITS + I * 2 * RING + (n + 2))
                    dve.wait_ge(glu_silu, L * FT + k + 1)
                    V.tensor_tensor(guf[:], gsg[:], ps[:, bank + 1, :], ALU.mult).then_inc(glu_done, 1)
                    split_next(L, n + 1, I * 2)
                    dve.wait_ge(glu_hi, L * FT + k + 1)
                    V.tensor_tensor(ulo[:, bass.ds(k, 1), :].rearrange("p a n -> p (a n)"), guf[:],
                                    f(uhi[:, bass.ds(k, 1), :]).rearrange("p a n -> p (a n)"),
                                    ALU.subtract).then_inc(glu_ready, 1)

                glu(0, 0)
                with dve.Fori(0, FT // RING) as I:
                    for p in range(RING):
                        glu(I, p + 1)
                with dve.Fori(0, FT // RING - 1) as I:
                    for j in range(RING):
                        split_next(L, U_DOWN + j, I)
                for n in (UNITS - 4, UNITS - 3):
                    split_next(L, n)
                residual(L, L * UNITS + UNITS, L * 14 + 7, h_back)
                split_next(L, UNITS - 2)
                (g0, g1), (b0, b1) = PF["ln2_g"], PF["ln2_b"]
                layer_norm(L * 2 + 2, pf[:, g0:g1], pf[:, b0:b1], lambda: split_next(L, UNITS - 1))
            for c in range(0, CT, 2):
                wait_tile(dve, 2 * DEPTH, c)
                V.tensor_tensor(h[:, c, :], f(hhi[:, c, :]), f(hlo[:, c, :]), ALU.add).then_inc(y_ready, 1)


def constants():
    k = np.arange(P)[:, None]
    q = np.arange(P)[None, :]
    rot = np.zeros((P, P), np.float32)
    for m in range(P):
        if m % HEAD < HEAD // 2:
            rot[m + HEAD // 2, m] = -1.0
        else:
            rot[m - HEAD // 2, m] = 1.0
    freq = np.float32(10000.0) ** (-np.arange(0, HEAD, 2, dtype=np.float32) / np.float32(HEAD))
    ang = np.arange(SEQ, dtype=np.float32)[None, :] * freq[np.arange(P) % (HEAD // 2)][:, None]
    return {
        "ident": np.eye(P), "upper": q >= k, "lower": q <= k,
        "after": k > q, "before": k < q, "rot": rot, "cos": np.cos(ang), "sin": np.sin(ang),
        "eps": np.full((P, 1), EPS),
    }


def lay_out(x_prompt, x_sample, ln_in_g, ln_in_b, w_in, attn_sink, ssd_conv_w, ssd_conv_b, ssd_a_log,
            ssd_dt_bias, ssd_d, ssd_norm_g, w_out, ln1_g, ln1_b, w_up, ffn_conv_w, ffn_conv_b, w_down,
            ln2_g, ln2_b):
    def by_columns(w):
        n = w.shape[1] // P
        return w.reshape(CT, P, n, P).transpose(2, 1, 0, 3).reshape(n, P, D_MODEL)

    def channels(v):
        return v.reshape(-1, P).T

    def everywhere(v):
        return np.broadcast_to(v.reshape(1, -1), (P, v.size))

    x = np.concatenate([x_prompt.reshape(SEQ, D_MODEL), x_sample.reshape(SEQ, D_MODEL)])
    x_t = x.T.reshape(CT, P, TOK).transpose(1, 0, 2)
    aw, kw = 512, 128
    z0 = aw + 2 * kw
    xbc0 = z0 + SSD_WIDTH
    dt0 = xbc0 + SSD_WIDTH + 4 * STATE
    units, pms, pfs = [], [], []
    for i in range(DEPTH):
        w = w_in[i]
        dtw = np.zeros((D_MODEL, P), w.dtype)
        dtw[:, :32] = w[:, dt0:dt0 + 32]
        xbc = w[:, xbc0:dt0]
        q = w[:, :aw].reshape(D_MODEL, 2, QPK, HEAD).transpose(0, 2, 1, 3).reshape(D_MODEL, aw)
        units.append(by_columns(np.concatenate(
            [dtw, w[:, aw:z0], q, xbc[:, SSD_WIDTH:], xbc[:, :SSD_WIDTH], w[:, z0:xbc0]], axis=1)))
        wo = w_out[i]
        wa = wo[:aw].reshape(2, QPK, HEAD, D_MODEL).transpose(1, 0, 2, 3).reshape(QPK, P, D_MODEL)
        units += [wa, wo[aw:].reshape(CT, P, D_MODEL)]
        up = by_columns(w_up[i])
        units.append(np.stack([up[:FT], up[FT:]], axis=1).reshape(2 * FT, P, D_MODEL))
        units.append(w_down[i].reshape(FT, P, D_MODEL))
        cw = np.concatenate([ssd_conv_w[i][:, SSD_WIDTH:], ssd_conv_w[i][:, :SSD_WIDTH]], axis=1)
        cbias = np.concatenate([ssd_conv_b[i][SSD_WIDTH:], ssd_conv_b[i][:SSD_WIDTH]])
        pms.append(np.concatenate([
            cw.reshape(5, N_CONV, P).transpose(2, 1, 0).reshape(P, 5 * N_CONV), channels(cbias),
            channels(ssd_norm_g[i]), everywhere(attn_sink[i]), everywhere(ssd_a_log[i]),
            everywhere(ssd_dt_bias[i]), everywhere(ssd_d[i])], axis=1))
        pfs.append(np.concatenate([
            ffn_conv_w[i].reshape(3, FT, P).transpose(2, 1, 0).reshape(P, 3 * FT), channels(ffn_conv_b[i]),
            channels(ln1_g[i]), channels(ln1_b[i]), channels(ln2_g[i]), channels(ln2_b[i])], axis=1))
    cn = np.zeros((P, CN_W), x.dtype)
    for name, v in constants().items():
        cn[:, CN[name][0]:CN[name][1]] = v
    cn[:, CN["ln_g"][0]:CN["ln_g"][1]] = channels(ln_in_g)
    cn[:, CN["ln_b"][0]:CN["ln_b"][1]] = channels(ln_in_b)
    return {"x_t": x_t, "units": np.concatenate(units), "pm": np.stack(pms), "pf": np.stack(pfs), "cn": cn}


def kernel(**inputs):
    import concourse.bacc as _bacc
    from concourse.bass_utils import run_bass_kernel_spmd as _run

    nc = _bacc.Bacc("TRN2", target_bir_lowering=False, num_devices=1)
    arrays, args = {}, []
    for name, a in lay_out(**{k: np.asarray(v) for k, v in inputs.items()}).items():
        a = np.ascontiguousarray(a)
        arrays[f"in_{name}"] = a
        args.append(nc.dram_tensor(f"in_{name}", a.shape, mybir.dt.from_np(a.dtype), kind="ExternalInput").ap())
    y_t = nc.dram_tensor("out_y", (P, CT, TOK), F32, kind="ExternalOutput").ap()
    trunk(nc, *args, y_t)
    r = _run(nc, [arrays], core_ids=[0])
    y = np.asarray(r.results[0]["out_y"]).transpose(2, 1, 0).reshape(NSEQ, 1, SEQ, D_MODEL)
    return y[0], y[1]
```
